# Optimizing a Trainium2 kernel written in Bass

```python
import jax, jax.numpy as jnp
from jax import lax
import numpy as np

D_MODEL = 1024
BATCH = 1
SEQ = 512
DEPTH = 2

HEAD_DIM = 64
D_MIX = D_MODEL
N_HEADS_FOX = D_MIX // (2 * HEAD_DIM)
N_HEADS_DIL = D_MIX // (2 * HEAD_DIM)
D_FOX = N_HEADS_FOX * HEAD_DIM
D_DIL = N_HEADS_DIL * HEAD_DIM
N_IN = 4 * D_FOX + N_HEADS_FOX + 4 * D_DIL
PLE_DIM = 256
ROPE_THETA = 500000.0
ROPE_DIM = HEAD_DIM // 4
DILATED_PATTERNS = ((128, 1), (512, 4), (2048, 16))
BLOCK = 128
EPS = 1e-6
NEG = -1e30
FORGET_BIAS_INIT = 3.0


def rms_norm(x, g):
    xf = x.astype(jnp.float32)
    y = xf * lax.rsqrt(jnp.mean(xf * xf, axis=-1, keepdims=True) + EPS)
    return (y * g.astype(jnp.float32)).astype(x.dtype)

def partial_rope(x, positions):
    half = ROPE_DIM // 2
    inv_freq = ROPE_THETA ** (-jnp.arange(half, dtype=jnp.float32) / half)
    ang = positions.astype(jnp.float32)[..., None] * inv_freq
    cos = jnp.cos(ang)[:, :, None, :]
    sin = jnp.sin(ang)[:, :, None, :]
    xr = x[..., :ROPE_DIM].astype(jnp.float32)
    x1, x2 = xr[..., :half], xr[..., half:]
    rot = jnp.concatenate([x1 * cos - x2 * sin, x2 * cos + x1 * sin], axis=-1)
    return jnp.concatenate([rot.astype(x.dtype), x[..., ROPE_DIM:]], axis=-1)

def forgetting_attention(q, k, v, log_f):
    B, S, H, Dh = q.shape
    nb = S // BLOCK
    scale = Dh ** -0.5
    c = jnp.cumsum(log_f.astype(jnp.float32), axis=1).transpose(0, 2, 1)
    qb = q.reshape(B, nb, BLOCK, H, Dh).transpose(1, 0, 2, 3, 4)
    cb = c.reshape(B, H, nb, BLOCK).transpose(2, 0, 1, 3)
    key_pos = jnp.arange(S)

    def one_block(args):
        i, q_i, c_i = args
        s = jnp.einsum('bqhd,bkhd->bhqk', q_i, k, preferred_element_type=jnp.float32) * scale
        s = s + c_i[..., :, None] - c[:, :, None, :]
        q_pos = i * BLOCK + jnp.arange(BLOCK)
        causal = key_pos[None, :] <= q_pos[:, None]
        s = jnp.where(causal, s, NEG)
        prob = jax.nn.softmax(s, axis=-1)
        return jnp.einsum('bhqk,bkhd->bqhd', prob.astype(v.dtype), v)

    out = lax.map(one_block, (jnp.arange(nb), qb, cb))
    return out.transpose(1, 0, 2, 3, 4).reshape(B, S, H, Dh)

def dilated_branch(q, k, v, window, dilation):
    B, S, H, Dh = q.shape
    L = S // dilation
    n_back = window // dilation
    n_prev = -(-n_back // BLOCK)
    nb = -(-L // BLOCK)
    Lp = nb * BLOCK
    N = B * dilation
    KW = (n_prev + 1) * BLOCK

    def to_streams(x):
        x = x.reshape(B, L, dilation, H, Dh).transpose(0, 2, 1, 3, 4).reshape(N, L, H, Dh)
        return jnp.pad(x, ((0, 0), (0, Lp - L), (0, 0), (0, 0)))

    def key_band(x):
        xs = jnp.pad(to_streams(x), ((0, 0), (n_prev * BLOCK, 0), (0, 0), (0, 0)))
        xs = xs.reshape(N, nb + n_prev, BLOCK, H, Dh)
        return jnp.concatenate([xs[:, j:j + nb] for j in range(n_prev + 1)], axis=2)

    qs = to_streams(q).reshape(N, nb, BLOCK, H, Dh)
    kb, vb = key_band(k), key_band(v)
    s = jnp.einsum('nbqhd,nbkhd->nbhqk', qs, kb, preferred_element_type=jnp.float32) * (Dh ** -0.5)
    qq = jnp.arange(BLOCK)[:, None]
    kk = jnp.arange(KW)[None, :]
    dist = qq + n_prev * BLOCK - kk
    key_idx = jnp.arange(nb)[:, None, None] * BLOCK - n_prev * BLOCK + kk[None]
    valid = (dist >= 0) & (dist <= n_back) & (key_idx >= 0)
    s = jnp.where(valid[None, :, None], s, NEG)
    lse = jax.nn.logsumexp(s, axis=-1)
    prob = jnp.exp(s - lse[..., None])
    o = jnp.einsum('nbhqk,nbkhd->nbqhd', prob.astype(v.dtype), vb)

    def from_streams(x):
        tail = x.shape[3:]
        x = x.reshape((N, Lp) + tail)[:, :L]
        x = x.reshape((B, dilation, L) + tail).swapaxes(1, 2)
        return x.reshape((B, S) + tail)

    return from_streams(o), from_streams(lse.transpose(0, 1, 3, 2))

def dilated_attention(q, k, v):
    outs, lses = [], []
    for window, dilation in DILATED_PATTERNS:
        o, l = dilated_branch(q, k, v, window, dilation)
        outs.append(o)
        lses.append(l)
    w = jax.nn.softmax(jnp.stack(lses, axis=0), axis=0)
    o = jnp.stack(outs, axis=0).astype(jnp.float32)
    return jnp.sum(w[..., None] * o, axis=0).astype(q.dtype)

def hybrid_layer(h, p_i, positions, norm_g, w_in, b_f, qk_g, w_out, w_ple, ple_norm_g, w_ple_gate):
    B, S, _ = h.shape
    u = rms_norm(h, norm_g)
    z = u @ w_in
    cuts = np.cumsum([D_FOX, D_FOX, D_FOX, D_FOX, N_HEADS_FOX, D_DIL, D_DIL, D_DIL])
    qa, ka, va, ga, fa, qb, kb, vb, gb = jnp.split(z, cuts.tolist(), axis=-1)
    heads = lambda t, n: t.reshape(B, S, n, HEAD_DIM)

    qa = rms_norm(heads(qa, N_HEADS_FOX), qk_g[0])
    ka = rms_norm(heads(ka, N_HEADS_FOX), qk_g[1])
    log_f = jax.nn.log_sigmoid(fa.astype(jnp.float32) + b_f.astype(jnp.float32))
    oa = forgetting_attention(qa, ka, heads(va, N_HEADS_FOX), log_f).reshape(B, S, D_FOX)
    oa = oa * jax.nn.silu(ga)

    qb = partial_rope(rms_norm(heads(qb, N_HEADS_DIL), qk_g[2]), positions)
    kb = partial_rope(rms_norm(heads(kb, N_HEADS_DIL), qk_g[3]), positions)
    ob = dilated_attention(qb, kb, heads(vb, N_HEADS_DIL)).reshape(B, S, D_DIL)
    ob = ob * jax.nn.silu(gb)

    h = h + jnp.concatenate([oa, ob], axis=-1) @ w_out

    gate = jax.nn.sigmoid(rms_norm(h, ple_norm_g) @ w_ple_gate)
    return h + (p_i @ w_ple) * gate

def first_inputs(seed: int = 0) -> dict:
    key = jax.random.key(seed)
    ks = jax.random.split(key, 12)
    f32 = jnp.float32
    x = jax.random.normal(ks[0], (BATCH, SEQ, D_MODEL), f32)
    p = jax.random.normal(ks[1], (DEPTH, BATCH, SEQ, PLE_DIM), f32)
    positions = jnp.broadcast_to(jnp.arange(SEQ, dtype=jnp.int32), (BATCH, SEQ))
    norm_g = 1.0 + 0.05 * jax.random.normal(ks[2], (DEPTH, D_MODEL), f32)
    w_in = jax.random.normal(ks[3], (DEPTH, D_MODEL, N_IN), f32) * D_MODEL ** -0.5
    b_f = FORGET_BIAS_INIT + 0.1 * jax.random.normal(ks[4], (DEPTH, N_HEADS_FOX), f32)
    qk_norm_g = 1.0 + 0.05 * jax.random.normal(ks[5], (DEPTH, 4, HEAD_DIM), f32)
    w_out = jax.random.normal(ks[6], (DEPTH, D_MIX, D_MODEL), f32) * D_MIX ** -0.5
    w_ple = jax.random.normal(ks[7], (DEPTH, PLE_DIM, D_MODEL), f32) * PLE_DIM ** -0.5
    ple_norm_g = 1.0 + 0.05 * jax.random.normal(ks[8], (DEPTH, D_MODEL), f32)
    w_ple_gate = jax.random.normal(ks[9], (DEPTH, D_MODEL, D_MODEL), f32) * D_MODEL ** -0.5
    return {"x": x, "p": p, "positions": positions, "norm_g": norm_g, "w_in": w_in,
            "b_f": b_f, "qk_norm_g": qk_norm_g, "w_out": w_out, "w_ple": w_ple,
            "ple_norm_g": ple_norm_g, "w_ple_gate": w_ple_gate}

def first_block(x, p, positions, norm_g, w_in, b_f, qk_norm_g, w_out, w_ple, ple_norm_g, w_ple_gate):
    h = x
    for i in range(DEPTH):
        h = hybrid_layer(h, p[i], positions, norm_g[i], w_in[i], b_f[i], qk_norm_g[i],
                         w_out[i], w_ple[i], ple_norm_g[i], w_ple_gate[i])
    return h


CHUNK = 64
N_MEM = 256
D_MIX_2 = D_MODEL
D_A = D_MIX_2 // 2
D_B = D_MIX_2 - D_A
HGRN_KDIM = 128
HGRN_HEADS = D_A // HGRN_KDIM
HGRN_VDIM = D_A // HGRN_HEADS
POOL_WINDOWS = (2, 4, 8, 16)
POOL_GROUPS = len(POOL_WINDOWS)
POOL_CH = D_B // POOL_GROUPS
D_IN = 4 * D_A + D_B
D_FF = ((8 * D_MODEL // 3) + 127) // 128 * 128
XA_HEADS = 4
XA_HEAD_DIM = D_MODEL // XA_HEADS


def rmsnorm(x, g):
    xf = x.astype(jnp.float32)
    y = xf * lax.rsqrt(jnp.mean(xf * xf, axis=-1, keepdims=True) + EPS)
    return (y * g.astype(jnp.float32)).astype(x.dtype)

def swiglu(h, w1, w3, w2):
    return (jax.nn.silu(h @ w1) * (h @ w3)) @ w2

def hgrn2_chunkwise(q, k, v, log_f):
    B, T, H, K = q.shape
    V = v.shape[-1]
    nc = T // CHUNK

    def to_chunks(a):
        return a.reshape(B, nc, CHUNK, H, a.shape[-1]).transpose(1, 0, 3, 2, 4)

    causal = jnp.tril(jnp.ones((CHUNK, CHUNK), dtype=bool))[:, :, None]

    def step(S, inp):
        qc, kc, vc, gc = inp
        b = jnp.cumsum(gc, axis=2)
        o_inter = jnp.einsum('bhtk,bhkv->bhtv', qc * jnp.exp(b), S)
        rel = b[:, :, :, None, :] - b[:, :, None, :, :]
        decay = jnp.exp(jnp.where(causal, rel, -jnp.inf))
        A = jnp.einsum('bhtk,bhsk,bhtsk->bhts', qc, kc, decay)
        o = o_inter + jnp.einsum('bhts,bhsv->bhtv', A, vc)
        b_last = b[:, :, -1:, :]
        S = jnp.exp(b_last[:, :, 0, :, None]) * S + jnp.einsum(
            'bhsk,bhsv->bhkv', kc * jnp.exp(b_last - b), vc)
        return S, o

    S0 = jnp.zeros((B, H, K, V), jnp.float32)
    _, o = lax.scan(step, S0, (to_chunks(q), to_chunks(k), to_chunks(v), to_chunks(log_f)))
    return o.transpose(1, 0, 3, 2, 4).reshape(B, T, H, V)

def hgrn2_mixer(q_in, f_in, i_in, g_in, lb, norm_g):
    B, T, _ = q_in.shape
    shp = (B, T, HGRN_HEADS, HGRN_KDIM)
    q = q_in.astype(jnp.float32).reshape(shp)
    z = f_in.astype(jnp.float32).reshape(shp)
    lbh = lb.reshape(HGRN_HEADS, HGRN_KDIM)
    log_f = jnp.logaddexp(jnp.log(lbh), jnp.log1p(-lbh) + jax.nn.log_sigmoid(z))
    k = (1.0 - lbh) * jax.nn.sigmoid(-z)
    v = i_in.astype(jnp.float32).reshape(B, T, HGRN_HEADS, HGRN_VDIM)
    o = hgrn2_chunkwise(q, k, v, log_f)
    o = o * lax.rsqrt(jnp.mean(o * o, axis=-1, keepdims=True) + EPS)
    o = o * norm_g.astype(jnp.float32).reshape(HGRN_HEADS, HGRN_VDIM)
    o = o.reshape(B, T, D_A) * jax.nn.silu(g_in.astype(jnp.float32))
    return o.astype(q_in.dtype)

def multiscale_pool(u, pool_w, pool_scale):
    B, T, _ = u.shape
    uf = u.astype(jnp.float32).reshape(B, T, POOL_GROUPS, POOL_CH)
    cs = jnp.cumsum(uf, axis=1)
    t_count = jnp.arange(1, T + 1, dtype=jnp.float32)
    outs = []
    for j, w in enumerate(POOL_WINDOWS):
        csj = cs[:, :, j]
        prev = jnp.pad(csj, ((0, 0), (w, 0), (0, 0)))[:, :T]
        mean = (csj - prev) / jnp.minimum(t_count, w)[None, :, None]
        outs.append(mean - uf[:, :, j])
    p = jnp.stack(outs, axis=2)
    y = jnp.einsum('btgc,gcd->btgd', p, pool_w.astype(jnp.float32)).reshape(B, T, D_B)
    return (y * pool_scale.astype(jnp.float32)).astype(u.dtype)

def mem_cross_attention(h, mem_n, wq, wkv, wo):
    B, T, _ = h.shape
    M = mem_n.shape[1]
    q = (h @ wq).reshape(B, T, XA_HEADS, XA_HEAD_DIM)
    kv = (mem_n @ wkv).reshape(B, M, 2, XA_HEADS, XA_HEAD_DIM)
    k, v = kv[:, :, 0], kv[:, :, 1]
    s = jnp.einsum('bthd,bmhd->bhtm', q, k).astype(jnp.float32) * (XA_HEAD_DIM ** -0.5)
    p = jax.nn.softmax(s, axis=-1).astype(h.dtype)
    o = jnp.einsum('bhtm,bmhd->bthd', p, v).reshape(B, T, D_MODEL)
    return o @ wo

def second_inputs(seed: int = 0) -> dict:
    key = jax.random.key(seed)
    ks = jax.random.split(key, 24)
    f32 = jnp.float32

    def nrm(k, shape, scale):
        return jax.random.normal(k, shape, f32) * scale

    def gain(k, shape):
        return 1.0 + 0.1 * jax.random.normal(k, shape, f32)

    L, D, F = DEPTH, D_MODEL, D_FF
    return {
        'x': nrm(ks[0], (BATCH, SEQ, D), 1.0),
        'mem': nrm(ks[1], (BATCH, N_MEM, D), 1.0),
        'ffn1_norm': gain(ks[2], (L, D)),
        'ffn1_w1': nrm(ks[3], (L, D, F), D ** -0.5),
        'ffn1_w3': nrm(ks[4], (L, D, F), D ** -0.5),
        'ffn1_w2': nrm(ks[5], (L, F, D), F ** -0.5),
        'mix_norm': gain(ks[6], (L, D)),
        'w_in': nrm(ks[7], (L, D, D_IN), D ** -0.5),
        'lb_logits': nrm(ks[8], (L, D_A), 1.0),
        'hgrn_norm': gain(ks[9], (L, D_A)),
        'pool_w': nrm(ks[10], (L, POOL_GROUPS, POOL_CH, POOL_CH), POOL_CH ** -0.5),
        'pool_scale': gain(ks[11], (L, D_B)),
        'w_out': nrm(ks[12], (L, D_MIX_2, D), D_MIX_2 ** -0.5),
        'xa_norm': gain(ks[13], (L, D)),
        'mem_norm': gain(ks[14], (L, D)),
        'xa_wq': nrm(ks[15], (L, D, D), D ** -0.5),
        'xa_wkv': nrm(ks[16], (L, D, 2 * D), D ** -0.5),
        'xa_wo': nrm(ks[17], (L, D, D), D ** -0.5),
        'ffn2_norm': gain(ks[18], (L, D)),
        'ffn2_w1': nrm(ks[19], (L, D, F), D ** -0.5),
        'ffn2_w3': nrm(ks[20], (L, D, F), D ** -0.5),
        'ffn2_w2': nrm(ks[21], (L, F, D), F ** -0.5),
        'final_norm': gain(ks[22], (D,)),
    }

def second_block(x, mem, ffn1_norm, ffn1_w1, ffn1_w3, ffn1_w2, mix_norm, w_in, lb_logits,
              hgrn_norm, pool_w, pool_scale, w_out, xa_norm, mem_norm, xa_wq, xa_wkv,
              xa_wo, ffn2_norm, ffn2_w1, ffn2_w3, ffn2_w2, final_norm):
    lb_all = jnp.cumsum(jax.nn.softmax(lb_logits.astype(jnp.float32), axis=0), axis=0)
    lb_all = lb_all - lb_all[0:1]
    splits = [D_A, 2 * D_A, 3 * D_A, 4 * D_A]
    for l in range(DEPTH):
        x = x + 0.5 * swiglu(rmsnorm(x, ffn1_norm[l]), ffn1_w1[l], ffn1_w3[l], ffn1_w2[l])
        h = rmsnorm(x, mix_norm[l])
        proj = h @ w_in[l]
        q_a, f_a, i_a, g_a, u_b = jnp.split(proj, splits, axis=-1)
        o_a = hgrn2_mixer(q_a, f_a, i_a, g_a, lb_all[l], hgrn_norm[l])
        o_b = multiscale_pool(u_b, pool_w[l], pool_scale[l])
        x = x + jnp.concatenate([o_a, o_b], axis=-1) @ w_out[l]
        x = x + mem_cross_attention(rmsnorm(x, xa_norm[l]), rmsnorm(mem, mem_norm[l]),
                                    xa_wq[l], xa_wkv[l], xa_wo[l])
        x = x + 0.5 * swiglu(rmsnorm(x, ffn2_norm[l]), ffn2_w1[l], ffn2_w3[l], ffn2_w2[l])
    return rmsnorm(x, final_norm)


def setup_inputs(seed=0):
    out = dict(first_inputs(seed))
    for name, value in second_inputs(seed + 1).items():
        if name != "x":
            out[name + "_2"] = value
    return out


def reference(
    x, p, positions, norm_g, w_in, b_f, qk_norm_g, w_out, w_ple, ple_norm_g, w_ple_gate, mem_2,
    ffn1_norm_2, ffn1_w1_2, ffn1_w3_2, ffn1_w2_2, mix_norm_2, w_in_2, lb_logits_2, hgrn_norm_2,
    pool_w_2, pool_scale_2, w_out_2, xa_norm_2, mem_norm_2, xa_wq_2, xa_wkv_2, xa_wo_2,
    ffn2_norm_2, ffn2_w1_2, ffn2_w3_2, ffn2_w2_2, final_norm_2,
):
    x = first_block(
        x, p, positions, norm_g, w_in, b_f, qk_norm_g, w_out, w_ple, ple_norm_g, w_ple_gate,
    )
    return second_block(
        x, mem_2, ffn1_norm_2, ffn1_w1_2, ffn1_w3_2, ffn1_w2_2, mix_norm_2, w_in_2, lb_logits_2,
        hgrn_norm_2, pool_w_2, pool_scale_2, w_out_2, xa_norm_2, mem_norm_2, xa_wq_2, xa_wkv_2,
        xa_wo_2, ffn2_norm_2, ffn2_w1_2, ffn2_w3_2, ffn2_w2_2, final_norm_2,
    )


_drawn_inputs = setup_inputs


def setup_inputs(seed=0):
    import zlib

    import numpy as np

    out = dict(_drawn_inputs(seed))
    spreads = {}
    factors = {'b_f': 40.952,
     'qk_norm_g': 3.672,
     'ple_norm_g': 3.472,
     'xa_norm_2': 5.451,
     'mem_norm_2': 3.752}
    for name, (base, spread) in spreads.items():
        noise = np.random.default_rng([zlib.crc32(name.encode()), seed]).standard_normal(out[name].shape)
        drawn = base * np.exp(spread * noise) if base else spread * noise
        out[name] = __import__('jax').numpy.asarray(drawn.astype(out[name].dtype))
    for name, factor in factors.items():
        out[name] = (out[name] * factor).astype(out[name].dtype)
    return out
```

```python
from contextlib import ExitStack

import numpy as np

import concourse.bass as bass
from concourse import mybir

F32 = mybir.dt.float32
F32R = mybir.dt.float32r
I32 = mybir.dt.int32
U8 = mybir.dt.uint8
ALU = mybir.AluOpType
ACT = mybir.ActivationFunctionType
AX = mybir.AxisListType

P = 128
DEPTH = 2
SEQ = 512
NT = SEQ // P
D = 1024
KD = D // P
EPS = 1e-6
NEG = -1e30
LOWEST = -3.0e38

HEAD = 64
NH = 8
ROPE = 16
HALF = ROPE // 2
PLE = 256

NMEM = 256
MT = NMEM // P
DFF = 2816
DA = 512
HH = 4
LEVELS = 7
XH = 4
XD = 256

BLK = 2048
NB1 = 25
NB2 = 96
NCHUNK = DFF // 256

S0, S1, S2, S3 = 0, 128, 384, 768
SOFF = (S0, S1, S2, S3)
PTOFF = (0, 512, 1024, 896)
MB_CAUSAL, MB_DIL = 0, 1


def constants():
    q = np.arange(P)[:, None]
    k = np.arange(P)[None, :]
    fox = np.zeros((P, NT, P), np.float32)
    fox[:, NT - 1] = np.where(k <= q, 0.0, NEG)
    dil = np.zeros((P, NT, P), np.float32)
    for j in range(NT):
        dist = (NT - 1 - j) * P + q - k
        count = ((dist >= 0) & (dist <= 128)).astype(int) + ((dist >= 0) & (dist % 4 == 0)) + ((dist >= 0) & (dist % 16 == 0))
        dil[:, j] = np.where(count > 0, np.log(np.maximum(count, 1).astype(np.float32)), NEG)
    upto = np.ones((P, NT, P), np.float32)
    upto[:, 0] = (q <= k)
    ident = np.eye(P, dtype=np.float32)
    inv = (np.float32(500000.0) ** (-np.arange(HALF, dtype=np.float32) / np.float32(HALF))).astype(np.float32)
    inv = np.broadcast_to(inv, (P, HALF))
    first = np.concatenate([ident, fox.reshape(P, -1), dil.reshape(P, -1), upto.reshape(P, -1), inv], 1)

    s, t = q, k
    level = np.zeros((P, LEVELS + 1, P), np.float32)
    masks = []
    for n in range(LEVELS):
        m = P >> (n + 1)
        ref = (t // (2 * m)) * 2 * m + m - 1
        right = (t // m) % 2 == 1
        level[:, n] = np.where(right, (s > ref) & (s <= t), (s > t) & (s <= ref))
        keep = ((s // (2 * m)) == (t // (2 * m))) & ((s // m) % 2 == 0)
        masks.append(keep[:, right[0]])
    level[:, LEVELS] = s <= t
    after = (s > t).astype(np.float32)
    second = np.concatenate([ident, level.reshape(P, -1), after], 1)
    masks = np.concatenate([np.tile(a, (1, NT)) for a in masks + [s == t]], 1).astype(np.float32)
    bands = np.zeros((P, 4, 3, P), np.float32)
    for g, w in enumerate((2, 4, 8, 16)):
        bands[:, g, 0] = ((s <= t) & (s > t - w)) / np.minimum(t + 1, w) - (s == t)
        bands[:, g, 1] = ((s <= t) & (s > t - w)) / w - (s == t)
        bands[:, g, 2] = (s - P > t - w) / w
    flag = np.zeros((DEPTH, P, 2), np.float32)
    flag[1:, :, 0] = 1.0
    flag[:1, :, 1] = NEG
    return [np.ascontiguousarray(a, np.float32) for a in (first, second, masks, bands.reshape(P, -1), flag)]


class Semaphores:

    def __init__(self, nc, ctx):
        self.nc, self.ctx, self.numbers = nc, ctx, []

    def __call__(self, name):
        s = self.ctx.enter_context(self.nc.semaphore(name))
        self.numbers.append(s.num)
        return s

    def span(self):
        return range(min(self.numbers), max(self.numbers) + 1)


class Memory:

    def __init__(self, nc):
        self.nc, self.top = nc, (nc.sbuf_base + 63) // 64 * 64

    def put(self, name, shape, dtype=F32):
        size = 4
        for n in shape[1:]:
            size *= n
        if dtype == U8:
            size //= 4
        h = self.nc.alloc_sbuf_tensor_at(name, shape, dtype, offset=self.top)
        self.top += (size + 63) // 64 * 64
        return h


def plus(i, step, base):
    return base if i is None else i * step + base


def refine(dve, mean, root, scratch):
    dve.scalar_tensor_tensor(scratch, root, -0.5, root, ALU.mult, ALU.mult)
    dve.drain()
    dve.tensor_tensor(scratch, scratch, mean, ALU.mult)
    dve.drain()
    dve.scalar_tensor_tensor(root, scratch, 1.5, root, ALU.add, ALU.mult)
    dve.drain()


class WeightStream:

    def __init__(self, sem, raw, hi, lo, dram, per_layer, layer):
        self.raw, self.hi, self.lo = raw, hi, lo
        self.dram = dram.rearrange("l b p n -> (l b) p n")
        self.per_layer, self.layer = per_layer, layer
        self.loaded = [sem("w_loaded0"), sem("w_loaded1")]
        self.hi_done, self.lo_done, self.used = sem("w_hi_done"), sem("w_lo_done"), sem("w_used")

    def load(self, sp, g, i=None, step=0):
        if i is None and g >= self.per_layer:
            return
        if i is not None or g >= 2:
            sp.wait_ge(self.lo_done, plus(i, step, g - 1))
        sp.dma_start(self.raw[g % 2][:], self.dram[bass.ds(self.layer * self.per_layer + plus(i, step, g), 1)]
                     .rearrange("o p n -> p (o n)")).then_inc(self.loaded[g % 2], 16)

    def split_hi(self, act, g, i=None, step=0):
        if i is None and g >= self.per_layer:
            return
        act.wait_ge(self.loaded[g % 2], plus(i, step * 8, 16 * (g // 2 + 1)))
        if i is not None or g >= 2:
            act.wait_ge(self.used, plus(i, step, g - 1))
        act.activation(self.hi[g % 2][:], self.raw[g % 2][:], ACT.Copy).then_inc(self.hi_done, 1)

    def split_lo(self, dve, g, i=None, step=0):
        if i is None and g >= self.per_layer:
            return
        dve.wait_ge(self.hi_done, plus(i, step, g + 1))
        dve.tensor_tensor(self.lo[g % 2][:], self.raw[g % 2][:], self.hi[g % 2][:], ALU.subtract).then_inc(self.lo_done, 1)

    def ready(self, pe, g, i=None, step=0):
        pe.wait_ge(self.lo_done, plus(i, step, g + 1))

    def wait_used(self, eng, g, i=None, step=0):
        eng.wait_ge(self.used, plus(i, step, g + 1))


def split_products(pe, out, still, moving, first, last):
    (sh, sl), (mh, ml) = still, moving
    pe.matmul(out, sh, mh, start=first, stop=False)
    pe.matmul(out, sh, ml, start=False, stop=False)
    return pe.matmul(out, sl, mh, start=False, stop=last)


def block_to_tokens(pe, w, g, u, outs, nt=NT, kd=KD, halves=1):
    n = BLK // kd // halves
    for t in range(nt):
        for h in range(halves):
            for k in range(kd):
                a = k * n * halves + h * n
                last = split_products(
                    pe, outs(t, h), [x[:, k, t * P:(t + 1) * P] for x in u],
                    (w.hi[g % 2][:, a:a + n], w.lo[g % 2][:, a:a + n]), k == 0, k == kd - 1)
    last.then_inc(w.used, 1)


def block_to_features(pe, w, g, u, outs):
    for f in range(2):
        for k in range(KD):
            a = k * 256 + f * P
            last = split_products(
                pe, outs(f), (w.hi[g % 2][:, a:a + P], w.lo[g % 2][:, a:a + P]),
                [x[:, k, :] for x in u], k == 0, k == KD - 1)
    last.then_inc(w.used, 1)


def to_features_phase(nc, sem, name, PS, ident, src, nt, uh, ul, gain=None, norm=None, extra=None):
    squared, mean_ready, rstd_ready, src_ready = (sem(f"{name}_{n}") for n in ("squared", "mean", "rstd", "src"))
    turned, hi_ready = sem(f"{name}_turned"), sem(f"{name}_hi")
    n = nt * P

    with nc.Block() as block:
        @block.sync
        def _(sp):
            if extra:
                extra("sync", sp)

        @block.scalar
        def _(act):
            if norm:
                x, sums, rstd, scratch = norm
                for t in range(nt):
                    act.activation(src[:, t, :], x[:, t, :], ACT.Square, accum_out=sums[:, t:t + 1]).then_inc(squared, 1)
                act.wait_ge(mean_ready, 1)
                act.activation(rstd[:, 0:nt], rstd[:, 0:nt], ACT.Sqrt).then_inc(rstd_ready, 1)
            if extra:
                extra("scalar", act)
            for k in range(KD):
                act.wait_ge(turned, k + 1)
                act.activation(uh[:, k, 0:n], PS[:, k, 0:n], ACT.Copy, scale=gain(k) if gain else 1.0).then_inc(hi_ready, 1)

        @block.vector
        def _(dve):
            if norm:
                x, sums, rstd, scratch = norm
                dve.wait_ge(squared, nt)
                dve.tensor_scalar(sums[:, 0:nt], sums[:, 0:nt], 1.0 / D, EPS, ALU.mult, ALU.add)
                dve.drain()
                dve.reciprocal(rstd[:, 0:nt], sums[:, 0:nt]).then_inc(mean_ready, 1)
                dve.wait_ge(rstd_ready, 1)
                refine(dve, sums[:, 0:nt], rstd[:, 0:nt], scratch[:, 0:nt])
                for t in range(nt):
                    dve.tensor_scalar(src[:, t, :], x[:, t, :], rstd[:, t:t + 1], None, ALU.mult).then_inc(src_ready, 1)
            if extra:
                extra("vector", dve)
            for k in range(KD):
                dve.wait_ge(hi_ready, k + 1)
                if gain:
                    dve.scalar_tensor_tensor(ul[:, k, 0:n], PS[:, k, 0:n], gain(k), uh[:, k, 0:n], ALU.mult, ALU.subtract)
                else:
                    dve.tensor_tensor(ul[:, k, 0:n], PS[:, k, 0:n], uh[:, k, 0:n], ALU.subtract)

        @block.tensor
        def _(pe):
            for t in range(nt):
                if norm:
                    pe.wait_ge(src_ready, t + 1)
                for k in range(KD):
                    i = pe.transpose(PS[:, k, t * P:(t + 1) * P], src[:, t, k * P:(k + 1) * P], ident)
                    if t == nt - 1:
                        i.then_inc(turned, 1)


def residual_phase(nc, sem, name, PS, w, g0, u, X, extra_blocks=0, extra=None):
    free = sem(f"{name}_free")

    with nc.Block() as block:
        @block.sync
        def _(sp):
            if g0 + 6 <= w.per_layer:
                with sp.Fori(0, 2) as i:
                    for j in range(2):
                        w.load(sp, g0 + 2 + j, i, 2)
            else:
                w.load(sp, g0 + 2)
                w.load(sp, g0 + 3)
            for j in range(extra_blocks):
                w.load(sp, g0 + 6 + j)

        @block.scalar
        def _(act):
            with act.Fori(0, 2) as i:
                for j in range(2):
                    w.split_hi(act, g0 + 1 + j, i, 2)
            if extra:
                extra("scalar", act)

        @block.vector
        def _(dve):
            dve.sem_inc(free, 2)
            with dve.Fori(0, 2) as i:
                for j in range(2):
                    w.split_lo(dve, g0 + 1 + j, i, 2)
                    w.wait_used(dve, g0 + j, i, 2)
                    part = X[:, :, bass.ds(i * 512 + j * 256, 256)]
                    dve.tensor_tensor(part, PS[:, 4 * j:4 * j + 4, 0:256], part, ALU.add).then_inc(free, 1)
            if extra:
                extra("vector", dve)

        @block.tensor
        def _(pe):
            with pe.Fori(0, 2) as i:
                for j in range(2):
                    w.ready(pe, g0 + j, i, 2)
                    pe.wait_ge(free, plus(i, 2, 1 + j))
                    block_to_tokens(pe, w, g0 + j, u, lambda t, h: PS[:, 4 * j + t, 0:256])
            if extra:
                pe.wait_ge(free, 6)
                extra("tensor", pe)


def projection_phase_1(nc, sem, name, PS, w, g0, u, m, dilated):
    sq_done, mean_ready, rstd_ready = sem(f"{name}_sq"), sem(f"{name}_mean"), sem(f"{name}_rstd")
    normed, turned, copied = sem(f"{name}_normed"), sem(f"{name}_turned"), sem(f"{name}_copied")
    v_done = sem(f"{name}_v")
    if not dilated:
        fa_split, fa_done, fa_z, fa_exp, fa_ln = (sem(f"{name}_{n}") for n in ("fasplit", "fa", "faz", "faexp", "faln"))
        lf_ready, cum_done, cum_copied, cum_moved = (sem(f"{name}_{n}") for n in ("lf", "cum", "cumcopied", "cummoved"))
    zn = m.zn
    gains = (2, 3) if dilated else (0, 1)

    with nc.Block() as block:
        @block.sync
        def _(sp):
            for j in range(8):
                w.load(sp, g0 + 2 + j)
            if not dilated:
                sp.wait_ge(cum_copied, 2)
                sp.dma_start(m.QT[HEAD + 1:HEAD + 2, :, :], m.cum[:]).then_inc(cum_moved, 16)
                sp.dma_start(m.KT[HEAD:HEAD + 1, :, :], m.ncum[:]).then_inc(cum_moved, 16)
                sp.wait_ge(cum_moved, 32)

        @block.gpsimd
        def _(pool):
            if not dilated:
                pool.memset(m.QT[HEAD:HEAD + 2, :, :], 1.0).then_inc(cum_copied, 1)
                pool.memset(m.KT[HEAD:HEAD + 2, :, :], 1.0).then_inc(cum_copied, 1)

        def heads_copy(act, j, scale):
            dst = (m.QT, m.KT)[j]
            for r in range(2):
                act.wait_ge(turned, 2 * j + r + 1)
                act.activation(dst[0:HEAD, 4 * r:4 * r + 4, :], PS[0:HEAD, 4 * j:4 * j + 4, :], ACT.Copy, scale=scale)\
                   .then_inc(copied, 1)

        def norm_act(act, j):
            w.wait_used(act, g0 + 2 * j + 1)
            act.activation(zn[j][:], PS[:, 4 * j:4 * j + 4, :].rearrange("p a n -> p (a n)"), ACT.Square).then_inc(sq_done, 1)
            act.wait_ge(mean_ready, j + 1)
            act.activation(m.rstd[:], m.rstd[:], ACT.Sqrt).then_inc(rstd_ready, 1)

        @block.scalar
        def _(act):
            if not dilated:
                act.activation(m.fa_hi[:], m.fa_raw[:], ACT.Copy).then_inc(fa_split, 1)
            w.split_hi(act, g0 + 1)
            if not dilated:
                act.wait_ge(fa_z, 1)
                act.activation(m.fa_e[:], m.fa_y[:], ACT.Abs).then_inc(fa_exp, 1)
                act.wait_ge(fa_exp, 1)
                act.activation(m.fa_e[:], m.fa_e[:], ACT.Exp, scale=-1.0).then_inc(fa_exp, 1)
                act.wait_ge(fa_exp, 2)
                act.activation(m.fa_e[:], m.fa_e[:], ACT.Ln, bias=1.0).then_inc(fa_ln, 1)
                act.wait_ge(cum_done, 1)
                act.activation(m.cum[:], PS[0:NH, 5, :], ACT.Copy).then_inc(cum_copied, 1)
                act.activation(m.ncum[:], PS[0:NH, 5, :], ACT.Copy, scale=-1.0).then_inc(cum_copied, 1)
            w.split_hi(act, g0 + 2)
            norm_act(act, 0)
            w.split_hi(act, g0 + 3)
            w.split_hi(act, g0 + 4)
            heads_copy(act, 0, HEAD ** -0.5)
            w.split_hi(act, g0 + 5)
            norm_act(act, 1)
            w.split_hi(act, g0 + 6)
            heads_copy(act, 1, 1.0)
            w.split_hi(act, g0 + 7)
            w.wait_used(act, g0 + 5)
            act.activation(m.V[:], PS[:, 0:4, :], ACT.Copy).then_inc(v_done, 1)
            w.split_hi(act, g0 + 8)
            w.wait_used(act, g0 + 7)
            act.activation(m.G[:], PS[:, 4:8, :], ACT.Silu)

        def norm_dve(dve, j):
            z = PS[:, 4 * j:4 * j + 4, :].rearrange("p a (h d) -> p (a h) d", d=HEAD)
            n3 = zn[j][:].rearrange("p (a d) -> p a d", d=HEAD)
            dve.wait_ge(sq_done, j + 1)
            dve.tensor_reduce(m.sums[:], n3, AX.X, ALU.add)
            dve.drain()
            dve.tensor_scalar(m.sums[:], m.sums[:], 1.0 / HEAD, EPS, ALU.mult, ALU.add)
            dve.drain()
            dve.reciprocal(m.rstd[:], m.sums[:]).then_inc(mean_ready, 1)
            dve.wait_ge(rstd_ready, j + 1)
            refine(dve, m.sums[:], m.rstd[:], m.scratch[:])
            shape = [P, NT * NH, HEAD]
            dve.tensor_tensor(n3, z, m.rstd[:].unsqueeze(2).to_broadcast(shape), ALU.mult)
            dve.drain()
            gi = gains[j]
            i = dve.tensor_tensor(n3, n3, m.qk_gain[:, gi * HEAD:(gi + 1) * HEAD].unsqueeze(1).to_broadcast(shape), ALU.mult)
            if dilated:
                dve.drain()
                z4 = zn[j][:].rearrange("p (t h d) -> p t h d", t=NT, h=NH)
                x1, x2 = z4[:, :, :, 0:HALF], z4[:, :, :, HALF:ROPE]
                full = [P, NT, NH, HALF]
                cos, sin = (a[:].unsqueeze(2).to_broadcast(full) for a in (m.cos, m.sin))
                dve.tensor_tensor(m.rot[0][:], x1, cos, ALU.mult)
                dve.tensor_tensor(m.rot[1][:], x2, sin, ALU.mult)
                dve.tensor_tensor(m.rot[2][:], x2, cos, ALU.mult)
                dve.tensor_tensor(m.rot[3][:], x1, sin, ALU.mult)
                dve.drain()
                dve.tensor_tensor(x1, m.rot[0][:], m.rot[1][:], ALU.subtract)
                i = dve.tensor_tensor(x2, m.rot[2][:], m.rot[3][:], ALU.add)
            dve.drain()
            dve.sem_inc(normed, 1)

        @block.vector
        def _(dve):
            if not dilated:
                dve.wait_ge(fa_split, 1)
                dve.tensor_tensor(m.fa_lo[:], m.fa_raw[:], m.fa_hi[:], ALU.subtract).then_inc(fa_split, 1)
            w.split_lo(dve, g0 + 1)
            if not dilated:
                dve.wait_ge(fa_done, 1)
                dve.tensor_tensor(m.fa_y[:], PS[:, 4, 0:NT * NH], m.fa_bias[:].unsqueeze(1).to_broadcast([P, NT, NH])
                                  , ALU.add).then_inc(fa_z, 1)
                dve.wait_ge(fa_z, 1)
                dve.wait_ge(fa_ln, 1)
                dve.scalar_tensor_tensor(m.lf[:], m.fa_y[:], 0.0, m.fa_e[:], ALU.min, ALU.subtract).then_inc(lf_ready, 1)
            w.split_lo(dve, g0 + 2)
            norm_dve(dve, 0)
            w.split_lo(dve, g0 + 3)
            w.split_lo(dve, g0 + 4)
            w.split_lo(dve, g0 + 5)
            norm_dve(dve, 1)
            for j in (6, 7, 8):
                w.split_lo(dve, g0 + j)

        @block.tensor
        def _(pe):
            def turn(j):
                for r in range(2):
                    if r == 0:
                        pe.wait_ge(normed, j + 1)
                    else:
                        pe.wait_ge(copied, 2 * j + 1)
                    for h in range(4):
                        for t in range(NT):
                            a = t * NH * HEAD + (4 * r + h) * HEAD
                            i = pe.transpose(PS[0:HEAD, 4 * j + h, t * P:(t + 1) * P], zn[j][:, a:a + HEAD], m.ident)
                    i.then_inc(turned, 1)

            def project(part):
                for half in range(2):
                    g = g0 + 2 * part + half
                    w.ready(pe, g)
                    block_to_tokens(pe, w, g, u, lambda t, h: PS[:, 4 * (part % 2) + t, half * 256:half * 256 + 256])

            if not dilated:
                pe.wait_ge(fa_split, 2)
                for t in range(NT):
                    for k in range(KD):
                        i = split_products(pe, PS[:, 4, t * NH:(t + 1) * NH], [x[:, k, t * P:(t + 1) * P] for x in u],
                                           [x[:, k * NH:(k + 1) * NH] for x in (m.fa_hi, m.fa_lo)], k == 0, k == KD - 1)
                i.then_inc(fa_done, 1)
            project(0)
            if not dilated:
                pe.wait_ge(lf_ready, 1)
                for j in range(NT):
                    i = pe.matmul(PS[0:NH, 5, j * P:SEQ], m.lf[:, j * NH:(j + 1) * NH], m.upto[:, 0:SEQ - j * P],
                                  start=j == 0, stop=j == NT - 1)
                i.then_inc(cum_done, 1)
                pe.wait_ge(cum_copied, 4)
            project(1)
            turn(0)
            pe.wait_ge(copied, 2)
            project(2)
            turn(1)
            pe.wait_ge(copied, 4)
            project(3)


def attention_phase_1(nc, sem, name, PS, m, rows, mask, column):
    scored, shifted, exped = (sem(f"{name}_{n}") for n in ("scored", "shifted", "exped"))
    turned, pt_act, pt_dve, out_done, mixed = (sem(f"{name}_{n}") for n in ("turned", "ptact", "ptdve", "out", "mixed"))
    score_at = [PS[:, 1, 384:512], PS[:, 2, 0:256], PS[:, 1, 0:384], PS[:, 0, 0:512]]

    with nc.Block() as block:
        @block.scalar
        def _(act):
            def exps(h):
                act.wait_ge(shifted, h + 1)
                for t in range(NT):
                    part = m.S[h % 2][:, SOFF[t]:SOFF[t] + (t + 1) * P]
                    act.activation(part, part, ACT.Exp, bias=m.nmax[h % 2][:, t:t + 1],
                                   accum_out=m.psum[h % 4][:, t:t + 1]).then_inc(exped, 1)

            exps(0)
            for h in range(NH):
                act.wait_ge(turned, h + 1)
                if h >= 2:
                    act.wait_ge(out_done, h - 1)
                act.activation(m.PT[h % 2][:, 0:512], PS[:, 3, :], ACT.Copy).then_inc(pt_act, 1)
                if h + 1 < NH:
                    exps(h + 1)

        @block.vector
        def _(dve):
            def add_mask(h):
                dve.wait_ge(scored, h + 1)
                if h >= 2:
                    dve.wait_ge(turned, h - 1)
                for t in range(NT):
                    n = (t + 1) * P
                    dve.tensor_tensor_reduce(out=m.S[h % 2][:, SOFF[t]:SOFF[t] + n], in0=score_at[t],
                                             in1=mask[:, SEQ - n:SEQ], scale=1.0, scalar=LOWEST, op0=ALU.add,
                                             op1=ALU.max, accum_out=m.nmax[h % 2][:, t:t + 1])
                dve.drain()
                dve.tensor_scalar(m.nmax[h % 2][:], m.nmax[h % 2][:], -1.0, None, ALU.mult).then_inc(shifted, 1)

            def finish(h):
                dve.wait_ge(out_done, h + 1)
                dve.reciprocal(m.rinv[:], m.psum[h % 4][:])
                dve.drain()
                full = [P, NT, HEAD]
                dve.tensor_tensor(m.o[:].rearrange("p (t d) -> p t d", d=HEAD),
                                  PS[:, 6 + h % 2, 0:NT * HEAD].rearrange("p (t d) -> p t d", d=HEAD),
                                  m.rinv[:].unsqueeze(2).to_broadcast(full), ALU.mult)
                dve.drain()
                dve.tensor_tensor(m.mix[:, :, column + h * HEAD:column + (h + 1) * HEAD],
                                  m.o[:].rearrange("p (t d) -> p t d", d=HEAD),
                                  m.G[:, :, h * HEAD:(h + 1) * HEAD], ALU.mult).then_inc(mixed, 1)

            add_mask(0)
            for h in range(NH):
                if h + 1 < NH:
                    add_mask(h + 1)
                dve.wait_ge(turned, h + 1)
                if h >= 2:
                    dve.wait_ge(out_done, h - 1)
                dve.tensor_copy(m.PT[h % 2][:, 512:1280], PS[:, 4:6, :].rearrange("p a n -> p (a n)")[:, 0:768]).then_inc(pt_dve, 1)
                if h >= 1:
                    finish(h - 1)
            finish(NH - 1)

        @block.tensor
        def _(pe):
            def scores(h):
                if h >= 1:
                    pe.wait_ge(shifted, h)
                for t in range(NT):
                    i = pe.matmul(score_at[t], m.QT[0:rows, h, t * P:(t + 1) * P], m.KT[0:rows, h, 0:(t + 1) * P],
                                  start=True, stop=True)
                i.then_inc(scored, 1)

            def turn(h):
                pe.wait_ge(exped, NT * (h + 1))
                if h >= 1:
                    pe.wait_ge(pt_act, h)
                    pe.wait_ge(pt_dve, h)
                flat = PS[:, 3:6, :].rearrange("p a n -> p (a n)")
                for j in range(NT):
                    for t in range(j, NT):
                        a = PTOFF[j] + (t - j) * P
                        i = pe.transpose(flat[:, a:a + P], m.S[h % 2][:, SOFF[t] + j * P:SOFF[t] + (j + 1) * P], m.ident)
                i.then_inc(turned, 1)

            def outputs(h):
                pe.wait_ge(pt_act, h + 1)
                pe.wait_ge(pt_dve, h + 1)
                if h >= 2:
                    pe.wait_ge(mixed, h - 1)
                for t in range(NT):
                    for j in range(t + 1):
                        a = PTOFF[j] + (t - j) * P
                        i = pe.matmul(PS[:, 6 + h % 2, t * HEAD:(t + 1) * HEAD], m.PT[h % 2][:, a:a + P],
                                      m.V[:, j, h * HEAD:(h + 1) * HEAD], start=j == 0, stop=j == t)
                i.then_inc(out_done, 1)

            scores(0)
            for h in range(NH):
                if h + 1 < NH:
                    scores(h + 1)
                turn(h)
                if h >= 1:
                    outputs(h - 1)
            outputs(NH - 1)


def gate_phase(nc, sem, PS, w, g0, u, X, m):
    sig_done, banks_free, sig_free = sem("gate_sig"), sem("gate_banks"), sem("gate_sig_free")

    with nc.Block() as block:
        @block.sync
        def _(sp):
            w.load(sp, g0 + 2)
            w.load(sp, g0 + 3)

        @block.scalar
        def _(act):
            for b in range(4):
                w.split_hi(act, g0 + b + 1)
                w.wait_used(act, g0 + b)
                if b >= 2:
                    act.wait_ge(sig_free, b - 1)
                act.activation(m.sig[b % 2][:], PS[:, 4 * (b % 2):4 * (b % 2) + 4, 0:256], ACT.Sigmoid).then_inc(sig_done, 1)
                act.wait_ge(sig_done, b + 1)
                act.sem_inc(banks_free, 1)

        @block.vector
        def _(dve):
            for b in range(4):
                w.split_lo(dve, g0 + b + 1)
                dve.wait_ge(sig_done, b + 1)
                cols = slice(b * 256, (b + 1) * 256)
                dve.tensor_tensor(m.sig[b % 2][:], m.sig[b % 2][:], m.ple[:, :, cols], ALU.mult)
                dve.drain()
                dve.tensor_tensor(X[:, :, cols], X[:, :, cols], m.sig[b % 2][:], ALU.add).then_inc(sig_free, 1)

        @block.tensor
        def _(pe):
            pe.sem_inc(banks_free, 2)
            with pe.Fori(0, 2) as i:
                for j in range(2):
                    w.ready(pe, g0 + j, i, 2)
                    pe.wait_ge(banks_free, plus(i, 2, 1 + j))
                    block_to_tokens(pe, w, g0 + j, u, lambda t, h: PS[:, 4 * j + t, 0:256])


class Box:
    pass


def first_model(nc, PS, X, stream_mem, uh, ul, free, ins, layer_count=DEPTH):
    (w1, consts, positions, norm_gains, qk_gains, fa_w, fa_b, pT) = ins
    mem = Memory(nc)
    mem.top = free
    m = Box()
    xn = mem.put("xn1", [P, NT, D])
    m.mix = xn
    table = mem.put("table1", [P, P + 3 * SEQ + HALF])
    m.ident = table[:, 0:P]
    mask_fox, mask_dil = table[:, P:P + SEQ], table[:, P + SEQ:P + 2 * SEQ]
    m.upto = table[:, P + 2 * SEQ:P + 3 * SEQ]
    inv_freq = table[:, P + 3 * SEQ:]
    gains = mem.put("norm_gains1", [P, 2 * KD])
    m.qk_gain = mem.put("qk_gain", [P, 4 * HEAD])
    m.cos, m.sin = mem.put("cos", [P, NT, HALF]), mem.put("sin", [P, NT, HALF])
    m.fa_raw, m.fa_hi, m.fa_lo = mem.put("fa_raw", [P, KD * NH]), mem.put("fa_hi", [P, KD * NH], F32R), mem.put("fa_lo", [P, KD * NH], F32R)
    m.fa_bias = mem.put("fa_bias", [P, NH])
    m.fa_y, m.fa_e, m.lf = (mem.put(n, [P, NT * NH]) for n in ("fa_y", "fa_e", "lf"))
    m.sums, m.rstd, m.scratch = (mem.put(n, [P, NT * NH]) for n in ("sums", "rstd", "scratch"))
    m.nmax = [mem.put(f"nmax{i}", [P, NT]) for i in range(2)]
    m.psum = [mem.put(f"psum{i}", [P, NT]) for i in range(4)]
    m.rinv = mem.put("rinv", [P, NT])
    m.o = mem.put("o1", [P, NT * HEAD])
    p_hi, p_lo = mem.put("p_hi", [P, 2, SEQ], F32R), mem.put("p_lo", [P, 2, SEQ], F32R)
    at = mem.top
    m.QT = mem.put("QT", [HEAD + 2, NH, SEQ])
    m.KT = mem.put("KT", [HEAD + 2, NH, SEQ])
    m.V, m.G = mem.put("V1", [P, NT, NH * HEAD]), mem.put("G1", [P, NT, NH * HEAD])
    at2 = mem.top
    m.S = [mem.put(f"S{i}", [P, 1280]) for i in range(2)]
    m.PT = [mem.put(f"PT{i}", [P, 1280]) for i in range(2)]
    end = mem.top
    mem.top = at2
    m.zn = [mem.put(f"zn{i}", [P, NT * NH * HEAD]) for i in range(2)]
    m.cum, m.ncum = mem.put("cum", [NH, SEQ]), mem.put("ncum", [NH, SEQ])
    end = max(end, mem.top)
    m.rot = []
    for i in range(4):
        m.rot.append(mem.put(f"rot{i}", [P, NT, NH, HALF]))
    end = max(end, mem.top)
    assert end <= nc.sbuf_usable_end, end
    mem.top = at
    m.ple = mem.put("ple", [P, NT, D])
    m.sig = [mem.put(f"sig{i}", [P, NT, 256]) for i in range(2)]
    p_raw = mem.put("p_raw", [P, 2, SEQ])
    mem.top = at
    pos, posf, ang, turns, red, over = (mem.put(n, [P, NT], I32) if n == "pos" else mem.put(n, [P, NT] if n == "posf" else [P, NT, HALF])
                                        for n in ("pos", "posf", "ang", "turns", "red", "over"))

    with ExitStack() as ctx:
        sem = Semaphores(nc, ctx)
        arrived, angles, rounded = sem("tables_arrived"), sem("angles_ready"), sem("rotary_done")
        with nc.Block() as block:
            @block.sync
            def _(sp):
                sp.dma_start(table[:], consts).then_inc(arrived, 16)
                sp.dma_start(pos[:], positions.rearrange("b (t p) -> p (b t)", p=P), allow_slow_non_contiguous=True).then_inc(arrived, 16)

            @block.vector
            def _(dve):
                C1, C2 = 6.28125, 0.0019350051879882812
                C3 = 2 * np.pi - C1 - C2
                dve.wait_ge(arrived, 32)
                dve.tensor_copy(posf[:], pos[:])
                dve.drain()
                dve.tensor_tensor(ang[:], posf[:].unsqueeze(2).to_broadcast([P, NT, HALF]),
                                  inv_freq.unsqueeze(1).to_broadcast([P, NT, HALF]), ALU.mult)
                dve.drain()
                dve.tensor_scalar(turns[:], ang[:], float(1 / (2 * np.pi)), 12582912.0, ALU.mult, ALU.add)
                dve.drain()
                dve.tensor_scalar(turns[:], turns[:], 12582912.0, None, ALU.subtract)
                dve.drain()
                for c in (C1, C2, C3):
                    dve.scalar_tensor_tensor(ang[:], turns[:], -float(c), ang[:], ALU.mult, ALU.add)
                    dve.drain()
                dve.tensor_scalar(red[:], ang[:], float(np.pi / 2), None, ALU.add)
                dve.drain()
                dve.tensor_scalar(over[:], red[:], float(np.pi), -2 * float(np.pi), ALU.is_gt, ALU.mult)
                dve.drain()
                dve.tensor_tensor(red[:], red[:], over[:], ALU.add)
                dve.drain()
                for a in (red, ang):
                    dve.tensor_scalar(a[:], a[:], 3.1415925, -3.1415925, ALU.min, ALU.max).then_inc(angles, 1)

            @block.scalar
            def _(act):
                act.wait_ge(angles, 2)
                act.activation(m.cos[:], red[:], ACT.Sin)
                act.activation(m.sin[:], ang[:], ACT.Sin)
        nc.all_engine_barrier(sems_to_clear=sem.span())

    with ExitStack() as ctx:
        sem = Semaphores(nc, ctx)
        stream_sems = sem
        with nc.Fori(0, layer_count) as layer:
            w = WeightStream(stream_sems, *stream_mem, w1, NB1, layer)
            small = sem("small_arrived")
            p_split = sem("p_split")

            def start(kind, eng):
                one = bass.ds(layer, 1)
                if kind == "sync":
                    eng.dma_start(gains[:], norm_gains[one].rearrange("o p n -> p (o n)")).then_inc(small, 16)
                    w.load(eng, 0)
                    w.load(eng, 1)
                    eng.dma_start(m.qk_gain[:], qk_gains[one].rearrange("o p n -> p (o n)")).then_inc(small, 16)
                    eng.dma_start(m.fa_raw[:], fa_w[one].rearrange("o p n -> p (o n)")).then_inc(small, 16)
                    eng.dma_start(m.fa_bias[:], fa_b[one].rearrange("o p n -> p (o n)")).then_inc(small, 16)
                    eng.dma_start(p_raw[:].rearrange("p k n -> p (k n)"), pT[one].rearrange("o p n -> p (o n)")).then_inc(small, 16)
                if kind == "scalar":
                    eng.wait_ge(small, 80)
                    eng.activation(p_hi[:], p_raw[:], ACT.Copy).then_inc(p_split, 1)
                    w.split_hi(eng, 0)
                if kind == "vector":
                    eng.wait_ge(p_split, 1)
                    eng.tensor_tensor(p_lo[:], p_raw[:], p_hi[:], ALU.subtract)
                    w.split_lo(eng, 0)

            to_features_phase(nc, sem, "norm1", PS, m.ident, xn, NT, uh, ul, gain=lambda k: gains[:, k:k + 1],
                              norm=(X, m.sums, m.rstd, m.scratch), extra=start)
            u = (uh, ul)
            projection_phase_1(nc, sem, "fox", PS, w, 0, u, m, False)
            attention_phase_1(nc, sem, "foxatt", PS, m, HEAD + 2, mask_fox, 0)
            projection_phase_1(nc, sem, "dil", PS, w, 8, u, m, True)
            attention_phase_1(nc, sem, "dilatt", PS, m, HEAD, mask_dil, NH * HEAD)
            to_features_phase(nc, sem, "mix1", PS, m.ident, m.mix, NT, uh, ul)

            def ple(kind, eng):
                g = 20
                if kind == "scalar":
                    w.split_hi(eng, g + 1)
                    w.wait_used(eng, g)
                    for t in range(NT):
                        eng.activation(m.ple[:, t, :].rearrange("p (a n) -> p a n", n=512), PS[:, 2 * t:2 * t + 2, :], ACT.Copy)
                if kind == "vector":
                    w.split_lo(eng, g + 1)
                if kind == "tensor":
                    w.ready(eng, g)
                    block_to_tokens(eng, w, g, (p_hi, p_lo), lambda t, h: PS[:, 2 * t + h, :], kd=2, halves=2)

            residual_phase(nc, sem, "out1", PS, w, 16, u, X, 1, ple)
            to_features_phase(nc, sem, "norm1g", PS, m.ident, xn, NT, uh, ul, gain=lambda k: gains[:, KD + k:KD + k + 1],
                              norm=(X, m.sums, m.rstd, m.scratch))
            gate_phase(nc, sem, PS, w, 21, u, X, m)
            nc.all_engine_barrier(sems_to_clear=sem.span())


def ffn_phase(nc, sem, name, PS, w, g0, u, X, f):
    silu_done, gated, h_hi, h_lo = (sem(f"{name}_{n}") for n in ("silu", "gated", "hhi", "hlo"))
    summed, free = sem(f"{name}_summed"), sem(f"{name}_free")
    LOOPS = (NCHUNK - 1) // 2
    END = g0 + 3 * NCHUNK

    def at(i, c, per=1, base=0):
        return plus(i, 2 * per, per * (1 + c) + base)

    with nc.Block() as block:
        @block.sync
        def _(sp):
            w.load(sp, g0 + 2)
            w.load(sp, g0 + 3)
            with sp.Fori(0, LOOPS - 1) as i:
                for j in range(6):
                    w.load(sp, g0 + 4 + j, i, 6)
            for g in range(g0 + 4 + 6 * (LOOPS - 1), END + 2):
                w.load(sp, g)

        @block.scalar
        def _(act):
            w.split_hi(act, g0 + 1)
            w.wait_used(act, g0)
            act.activation(f.silu[:], PS[:, 0:2, :], ACT.Silu).then_inc(silu_done, 1)
            w.split_hi(act, g0 + 2)
            act.wait_ge(gated, 1)
            act.activation(f.h_hi[:], f.h[:], ACT.Copy).then_inc(h_hi, 1)
            with act.Fori(0, LOOPS) as i:
                for c in range(2):
                    g = g0 + 2 + 3 * c
                    w.split_hi(act, g + 1, i, 6)
                    w.wait_used(act, g, i, 6)
                    act.activation(f.silu[:], PS[:, 0:2, :], ACT.Silu).then_inc(silu_done, 1)
                    w.split_hi(act, g + 2, i, 6)
                    w.split_hi(act, g + 3, i, 6)
                    act.wait_ge(gated, at(i, c, 1, 1))
                    act.activation(f.h_hi[:], f.h[:], ACT.Copy).then_inc(h_hi, 1)
            w.split_hi(act, END)

        @block.vector
        def _(dve):
            def gate(g, i, step, n):
                dve.wait_ge(silu_done, n)
                w.wait_used(dve, g, i, step)
                dve.tensor_tensor(f.h[:], PS[:, 2:4, :], f.silu[:], ALU.mult).then_inc(gated, 1)
                dve.wait_ge(h_hi, n)
                dve.tensor_tensor(f.h_lo[:], f.h[:], f.h_hi[:], ALU.subtract).then_inc(h_lo, 1)

            def add(g, i, c, step):
                for t in range(NT):
                    if t < NT - 1:
                        dve.wait_ge(summed, at(i, c, NT - 1, t + 2 - NT))
                    else:
                        w.wait_used(dve, g, i, step)
                    b = 4 + 2 * (t % 2)
                    x = X[:, t, :].rearrange("p (a n) -> p a n", n=512)
                    dve.scalar_tensor_tensor(x, PS[:, b:b + 2, :], 0.5, x, ALU.mult, ALU.add).then_inc(free, 1)

            dve.sem_inc(free, 2)
            w.split_lo(dve, g0 + 1)
            w.split_lo(dve, g0 + 2)
            gate(g0 + 1, None, 0, 1)
            with dve.Fori(0, LOOPS) as i:
                for c in range(2):
                    g = g0 + 2 + 3 * c
                    w.split_lo(dve, g + 1, i, 6)
                    w.split_lo(dve, g + 2, i, 6)
                    add(g + 1, i, c, 6)
                    w.split_lo(dve, g + 3, i, 6)
                    gate(g + 2, i, 6, at(i, c, 1, 1))
            w.split_lo(dve, END)
            add(END - 1, None, NCHUNK - 1, 0)

        @block.tensor
        def _(pe):
            def up(g, bank, i, step):
                w.ready(pe, g, i, step)
                block_to_features(pe, w, g, u, lambda t: PS[:, bank + t, :])

            def down(g, i, c, step):
                w.ready(pe, g, i, step)
                pe.wait_ge(h_lo, at(i, c))
                for t in range(NT):
                    pe.wait_ge(free, at(i, c, NT, t + 1 - NT))
                    for half in range(2):
                        for k in range(2):
                            a = k * D + half * 512
                            last = split_products(
                                pe, PS[:, 4 + 2 * (t % 2) + half, :], [x[:, k, t * P:(t + 1) * P] for x in (f.h_hi, f.h_lo)],
                                (w.hi[g % 2][:, a:a + 512], w.lo[g % 2][:, a:a + 512]), k == 0, k == 1)
                    last.then_inc(summed if t < NT - 1 else w.used, 1)

            up(g0, 0, None, 0)
            up(g0 + 1, 2, None, 0)
            with pe.Fori(0, LOOPS) as i:
                for c in range(2):
                    g = g0 + 2 + 3 * c
                    pe.wait_ge(silu_done, at(i, c))
                    up(g, 0, i, 6)
                    down(g + 1, i, c, 6)
                    pe.wait_ge(gated, at(i, c))
                    up(g + 2, 2, i, 6)
            down(END - 1, None, NCHUNK - 1, 0)


def projection_phase_2(nc, sem, PS, w, g0, u, m, one, pool_in, row_in, flag):
    s = Box()
    s.small, s.rmax, s.rexp, s.rsum, s.rln = (sem(f"mix2_{n}") for n in ("small", "rmax", "rexp", "rsum", "rln"))
    s.zread, s.zmin, s.ln1, s.ln2, s.diff = (sem(f"mix2_{n}") for n in ("zread", "zmin", "ln1", "ln2", "diff"))
    s.vread, s.uread, s.silu = (sem(f"mix2_{n}") for n in ("vread", "uread", "silu"))

    with nc.Block() as block:
        @block.sync
        def _(sp):
            sp.dma_start(m.lb[:], row_in[2]).then_inc(s.small, 16)
            sp.dma_start(m.flag[:], flag[one].rearrange("o p n -> p (o n)")).then_inc(s.small, 16)
            sp.dma_start(m.hnorm[:], row_in[0][one].rearrange("o p n -> p (o n)")).then_inc(s.small, 16)
            sp.dma_start(m.pscale[:], row_in[1][one].rearrange("o p n -> p (o n)")).then_inc(s.small, 16)
            sp.dma_start(m.bands[:], pool_in[0]).then_inc(s.small, 16)
            sp.dma_start(m.pool_w[:], pool_in[1][one].rearrange("o p n -> p (o n)")).then_inc(s.small, 16)
            for j in range(10):
                w.load(sp, g0 + 2 + j)

        zf = PS[:, 0:4, :]

        @block.scalar
        def _(act):
            act.wait_ge(s.rmax, 1)
            act.activation(m.e[:], m.lb[:], ACT.Exp).then_inc(s.rexp, 1)
            w.split_hi(act, g0 + 1)
            act.wait_ge(s.rsum, 1)
            act.activation(m.lnsum[:], m.esum[:], ACT.Ln).then_inc(s.rln, 1)
            w.split_hi(act, g0 + 2)
            w.wait_used(act, g0 + 1)
            act.activation(m.t1[:], zf, ACT.Abs).then_inc(s.zread, 1)
            act.activation(m.K[:], zf, ACT.Sigmoid, scale=-1.0).then_inc(s.zread, 1)
            w.split_hi(act, g0 + 3)
            act.wait_ge(s.zread, 2)
            act.activation(m.t1[:], m.t1[:], ACT.Exp, scale=-1.0)
            act.drain()
            act.activation(m.t1[:], m.t1[:], ACT.Ln, bias=1.0).then_inc(s.ln1, 1)
            w.split_hi(act, g0 + 4)
            w.wait_used(act, g0 + 3)
            act.activation(m.V[:], PS[:, 4:8, :], ACT.Copy).then_inc(s.vread, 1)
            act.wait_ge(s.diff, 1)
            act.activation(m.t2[:], m.t2[:], ACT.Abs)
            act.drain()
            act.activation(m.t2[:], m.t2[:], ACT.Exp, scale=-1.0)
            act.drain()
            act.activation(m.t2[:], m.t2[:], ACT.Ln, bias=1.0).then_inc(s.ln2, 1)
            w.split_hi(act, g0 + 5)
            w.split_hi(act, g0 + 6)
            w.wait_used(act, g0 + 5)
            act.activation(m.U[:], PS[:, 0:4, :], ACT.Copy).then_inc(s.uread, 1)
            w.split_hi(act, g0 + 7)
            w.split_hi(act, g0 + 8)
            w.wait_used(act, g0 + 7)
            act.activation(m.Q[:], PS[:, 4:8, :], ACT.Copy)
            w.split_hi(act, g0 + 9)
            w.split_hi(act, g0 + 10)
            w.wait_used(act, g0 + 9)
            act.activation(m.G[:], PS[:, 0:4, :], ACT.Silu).then_inc(s.silu, 1)

        @block.vector
        def _(dve):
            l0, l1 = m.lb[:, 0:DA], m.lb[:, DA:2 * DA]
            e0, e1 = m.e[:, 0:DA], m.e[:, DA:2 * DA]
            full = [P, NT, DA]
            dve.wait_ge(s.small, 96)
            dve.tensor_tensor(m.esum[:], l0, l1, ALU.max)
            dve.drain()
            for part in (l0, l1):
                dve.tensor_tensor(part, part, m.esum[:], ALU.subtract)
            dve.drain()
            dve.sem_inc(s.rmax, 1)
            dve.wait_ge(s.rexp, 1)
            dve.tensor_tensor(m.esum[:], e0, e1, ALU.add).then_inc(s.rsum, 1)
            dve.wait_ge(s.rsum, 1)
            w.split_lo(dve, g0 + 1)
            dve.wait_ge(s.rln, 1)
            for part in (l0, l1):
                dve.tensor_tensor(part, part, m.lnsum[:], ALU.subtract)
            dve.reciprocal(m.esum[:], m.esum[:])
            dve.drain()
            for part in (e0, e1):
                dve.tensor_tensor(part, part, m.esum[:], ALU.mult)
            dve.drain()
            dve.tensor_tensor(m.esum[:], e0, e1, ALU.add)
            dve.drain()
            dve.tensor_tensor(m.esum[:], m.esum[:], e0, ALU.subtract)
            on, floor = m.flag[:, 0:1], m.flag[:, 1:2]
            dve.tensor_scalar(m.ln1m[:], l0, on, None, ALU.mult)
            dve.tensor_scalar(m.lnlb[:], l1, on, floor, ALU.mult, ALU.add)
            dve.drain()
            dve.tensor_scalar(m.one_less[:], m.esum[:], on, -1.0, ALU.mult, ALU.mult)
            dve.drain()
            dve.tensor_scalar(m.one_less[:], m.one_less[:], 1.0, None, ALU.add)
            w.split_lo(dve, g0 + 2)
            dve.wait_ge(s.zread, 2)
            dve.tensor_scalar(m.t2[:], zf, 0.0, None, ALU.min).then_inc(s.zmin, 1)
            w.split_lo(dve, g0 + 3)
            dve.drain()
            dve.wait_ge(s.ln1, 1)
            dve.tensor_tensor(m.t2[:], m.t2[:], m.t1[:], ALU.subtract)
            dve.drain()
            rows = [a[:].unsqueeze(1).to_broadcast(full) for a in (m.ln1m, m.lnlb, m.one_less)]
            dve.tensor_tensor(m.t2[:], m.t2[:], rows[0], ALU.add)
            dve.drain()
            dve.tensor_tensor(m.LF[:], m.t2[:], rows[1], ALU.max)
            dve.drain()
            dve.tensor_tensor(m.t2[:], m.t2[:], rows[1], ALU.subtract).then_inc(s.diff, 1)
            w.split_lo(dve, g0 + 4)
            dve.tensor_tensor(m.K[:], m.K[:], rows[2], ALU.mult)
            w.split_lo(dve, g0 + 5)
            dve.wait_ge(s.ln2, 1)
            dve.drain()
            dve.tensor_tensor(m.LF[:], m.LF[:], m.t2[:], ALU.add)
            for j in (6, 7, 8, 9, 10):
                w.split_lo(dve, g0 + j)
            dve.wait_ge(s.silu, 1)
            dve.drain()
            dve.tensor_tensor(m.G[:], m.G[:], m.hnorm[:].unsqueeze(1).to_broadcast(full), ALU.mult)

        @block.tensor
        def _(pe):
            def project(part):
                for half in range(2):
                    g = g0 + 2 * part + half
                    w.ready(pe, g)
                    block_to_tokens(pe, w, g, u, lambda t, h: PS[:, 4 * (part % 2) + t, half * 256:half * 256 + 256])

            project(0)
            project(1)
            pe.wait_ge(s.zread, 2)
            pe.wait_ge(s.zmin, 1)
            project(2)
            pe.wait_ge(s.vread, 1)
            for half in range(2):
                g = g0 + 6 + half
                w.ready(pe, g)
                block_to_features(pe, w, g, u, lambda t: PS[:, 4 + 2 * half + t, :])
            pe.wait_ge(s.uread, 1)
            project(4)


def pool_and_states_phase(nc, sem, PS, m):
    pooled, pool_copied, mapped, mapped_read = (sem(f"pool_{n}") for n in ("pooled", "copied", "mapped", "read"))
    suffix, suffix_exp, kp, dec, dec_exp, outer = (sem(f"state_{n}") for n in ("suffix", "sexp", "kp", "dec", "dexp", "outer"))

    with nc.Block() as block:
        @block.scalar
        def _(act):
            for g in range(4):
                act.wait_ge(pooled, g + 1)
                act.activation(m.pT[:, g, :], PS[:, g, :], ACT.Copy).then_inc(pool_copied, 1)
            for c in range(NT):
                act.wait_ge(suffix, c + 1)
                act.activation(m.Kp[:, c, :], PS[:, 4 + c, :], ACT.Exp).then_inc(suffix_exp, 1)
            act.wait_ge(dec, 1)
            act.activation(m.dec[:], PS[:, 7, 0:HH * 2], ACT.Exp).then_inc(dec_exp, 1)

        @block.vector
        def _(dve):
            for c in range(NT - 1):
                dve.wait_ge(suffix_exp, c + 1)
                dve.tensor_tensor(m.Kp[:, c, :], m.Kp[:, c, :], m.K[:, c, :], ALU.mult).then_inc(kp, 1)
            for g in range(4):
                dve.wait_ge(mapped, g + 1)
                dve.tensor_tensor(m.mix[:, :, DA + g * P:DA + (g + 1) * P], PS[:, g, :].rearrange("p (t n) -> p t n", n=P),
                                  m.pscale[:, g * P:(g + 1) * P].unsqueeze(1).to_broadcast([P, NT, P]), ALU.mult)
            dve.wait_ge(outer, 1)
            dve.wait_ge(dec_exp, 1)
            dve.tensor_copy(m.St[:, 0, :], PS[:, 4, :])
            for c in (1, 2):
                dve.drain()
                for h in range(HH):
                    cols = slice(h * P, (h + 1) * P)
                    d = (c - 1) * HH + h
                    dve.scalar_tensor_tensor(m.St[:, c, cols], m.St[:, c - 1, cols], m.dec[:, d:d + 1],
                                             PS[:, 4 + c, cols], ALU.mult, ALU.add)

        @block.tensor
        def _(pe):
            for g in range(4):
                for t in range(NT):
                    out = PS[:, g, t * P:(t + 1) * P]
                    i = pe.matmul(out, m.U[:, t, g * P:(g + 1) * P], m.band(g, 1 if t else 0), start=True, stop=t == 0)
                    if t:
                        i = pe.matmul(out, m.U[:, t - 1, g * P:(g + 1) * P], m.band(g, 2), start=False, stop=True)
                i.then_inc(pooled, 1)
            for c in range(NT):
                pe.matmul(PS[:, 4 + c, :], m.after, m.LF[:, c, :], start=True, stop=True).then_inc(suffix, 1)
            for g in range(4):
                pe.wait_ge(pool_copied, g + 1)
                for t in range(NT):
                    i = pe.matmul(PS[:, g, t * P:(t + 1) * P], m.pT[:, g, t * P:(t + 1) * P], m.pool_w[:, g * P:(g + 1) * P],
                                  start=True, stop=True)
                i.then_inc(mapped, 1)
            pe.wait_ge(suffix_exp, 4)
            for c in (1, 2):
                for h in range(HH):
                    d = (c - 1) * HH + h
                    i = pe.matmul(PS[:, 7, d:d + 1], m.LF[:, c, h * P:(h + 1) * P], m.level[:, LEVELS * P + P - 1:LEVELS * P + P],
                                  start=True, stop=True)
            i.then_inc(dec, 1)
            pe.wait_ge(kp, 3)
            for c in range(NT - 1):
                for h in range(HH):
                    cols = slice(h * P, (h + 1) * P)
                    i = pe.matmul(PS[:, 4 + c, cols], m.Kp[:, c, cols], m.V[:, c, cols], start=True, stop=True)
            i.then_inc(outer, 1)


def recurrence_phase(nc, sem, PS, m):
    k_turned, k_copied, summed, exped, weighed, scored, kept, out_done, out_sq, out_read = (
        sem(f"rec_{n}") for n in ("kturned", "kcopied", "summed", "exped", "weighed", "scored", "kept", "out", "outsq", "outread"))
    zeroed, mean_ready, rstd_ready = sem("rec_zeroed"), sem("rec_mean"), sem("rec_rstd")
    UNITS = 5

    def right(ap, n, side=1):
        mm = P >> (n + 1)
        return ap.rearrange("p (b two m) -> p b two m", two=2, m=mm)[:, :, side, :]

    with nc.Block() as block:
        @block.gpsimd
        def _(pool):
            for i in range(2):
                pool.memset(m.AT[i][:], 0.0).then_inc(zeroed, 1)

        @block.scalar
        def _(act):
            def exps(h):
                act.wait_ge(k_turned, h + 1)
                if h >= 2:
                    act.wait_ge(out_done, h - 1)
                act.activation(m.Kf[h % 2][:], PS[:, 4, :], ACT.Copy).then_inc(k_copied, 1)
                for c in range(NT):
                    act.wait_ge(summed, NT * h + c + 1)
                    b = 2 * (c % 2)
                    act.activation(m.E[h % 2][:, :, c * P:(c + 1) * P],
                                   PS[:, b:b + 2, :].rearrange("p a (l t) -> p (a l) t", t=P), ACT.Exp).then_inc(exped, 1)

            exps(0)
            exps(1)
            for h in range(HH):
                act.wait_ge(out_done, h + 1)
                act.activation(m.mix[:, :, h * P:(h + 1) * P], PS[:, 7, :].rearrange("p (c v) -> p c v", v=P), ACT.Square)\
                   .then_inc(out_sq, 1)
                if h + 2 < HH:
                    exps(h + 2)
            act.wait_ge(mean_ready, 1)
            act.activation(m.orstd[:], m.orstd[:], ACT.Sqrt).then_inc(rstd_ready, 1)

        @block.vector
        def _(dve):
            def weigh(h):
                dve.wait_ge(k_copied, h + 1)
                dve.wait_ge(exped, NT * (h + 1))
                E = m.E[h % 2]
                for n in range(LEVELS):
                    for side, src in ((1, m.Q[:, h, :]), (0, m.Kf[h % 2][:])):
                        e = right(E[:, n, :], n, side)
                        dve.tensor_tensor(e, e, right(src, n, side), ALU.mult)
                dve.tensor_tensor(E[:, LEVELS, :], E[:, LEVELS, :], m.Q[:, h, :], ALU.mult)
                dve.drain()
                dve.sem_inc(weighed, 1)

            def keep(h):
                if h >= 2:
                    dve.wait_ge(out_done, h - 1)
                AT = m.AT[h % 2]
                for unit in range(UNITS):
                    dve.wait_ge(scored, UNITS * h + unit + 1)
                    b = 5 + unit % 2
                    for n in (2 * unit, 2 * unit + 1):
                        if n < LEVELS:
                            mm = P >> (n + 1)
                            a = (n % 2) * 256
                            dve.copy_predicated(right(AT[:].rearrange("p c t -> p (c t)"), n),
                                                m.masks[:, n * 256:(n + 1) * 256].rearrange("p (b m) -> p b m", m=mm),
                                                PS[:, b, a:a + 256].rearrange("p (b m) -> p b m", m=mm))
                            dve.drain()
                    if unit == UNITS - 1:
                        dve.copy_predicated(AT[:].rearrange("p c t -> p (c t)"), m.masks[:, LEVELS * 256:], PS[:, b, :])
                    dve.drain()
                    dve.sem_inc(kept, 1)

            def finish(h):
                dve.wait_ge(out_sq, h + 1)
                dve.tensor_reduce(m.osum[:, h * NT:(h + 1) * NT], m.mix[:, :, h * P:(h + 1) * P], AX.X, ALU.add)
                dve.drain()
                dve.tensor_copy(m.mix[:, :, h * P:(h + 1) * P], PS[:, 7, :].rearrange("p (c v) -> p c v", v=P))
                dve.drain()
                dve.sem_inc(out_read, 1)

            dve.wait_ge(zeroed, 2)
            weigh(0)
            for h in range(HH):
                keep(h)
                if h + 1 < HH:
                    weigh(h + 1)
                finish(h)
            dve.tensor_scalar(m.osum[:], m.osum[:], 1.0 / P, EPS, ALU.mult, ALU.add)
            dve.drain()
            dve.reciprocal(m.orstd[:], m.osum[:]).then_inc(mean_ready, 1)
            dve.tensor_tensor(m.mix[:, :, 0:DA], m.mix[:, :, 0:DA], m.G[:], ALU.mult)
            dve.wait_ge(rstd_ready, 1)
            refine(dve, m.osum[:], m.orstd[:], m.scratch[:])
            for c in range(NT):
                part = m.mix[:, c, 0:DA].rearrange("p (h v) -> p h v", v=P)
                rs = m.orstd[:].rearrange("p (h c) -> p h c", c=NT)[:, :, c:c + 1]
                dve.tensor_tensor(part, part, rs.to_broadcast([P, HH, P]), ALU.mult)

        @block.tensor
        def _(pe):
            def sums(h):
                if h:
                    pe.wait_ge(k_copied, h)
                for c in range(NT):
                    i = pe.transpose(PS[:, 4, c * P:(c + 1) * P], m.K[:, c, h * P:(h + 1) * P], m.ident)
                i.then_inc(k_turned, 1)
                for c in range(NT):
                    if NT * h + c >= 2:
                        pe.wait_ge(exped, NT * h + c - 1)
                    for half in range(2):
                        i = pe.matmul(PS[:, 2 * (c % 2) + half, :], m.LF[:, c, h * P:(h + 1) * P],
                                      m.level[:, half * 512:half * 512 + 512], start=True, stop=True)
                    i.then_inc(summed, 1)

            def scores(h):
                pe.wait_ge(weighed, h + 1)
                W = m.E[h % 2]
                for unit in range(UNITS):
                    if UNITS * h + unit >= 2:
                        pe.wait_ge(kept, UNITS * h + unit - 1)
                    b = 5 + unit % 2
                    if unit < UNITS - 1:
                        for n in (2 * unit, 2 * unit + 1):
                            if n < LEVELS:
                                for c in range(NT):
                                    tile = W[:, n, c * P:(c + 1) * P]
                                    a = (n % 2) * 256 + c * 64
                                    i = pe.matmul(PS[:, b, a:a + 64], tile, right(tile, n), start=True, stop=True)
                    else:
                        for c in range(NT):
                            i = pe.matmul(PS[:, b, c * P:(c + 1) * P], m.Kf[h % 2][:, c * P:(c + 1) * P],
                                          m.Q[:, h, c * P:(c + 1) * P], start=True, stop=True)
                    i.then_inc(scored, 1)

            def outputs(h):
                pe.wait_ge(kept, UNITS * (h + 1))
                if h:
                    pe.wait_ge(out_read, h)
                cols = slice(h * P, (h + 1) * P)
                for c in range(NT):
                    out = PS[:, 7, c * P:(c + 1) * P]
                    i = pe.matmul(out, m.AT[h % 2][:, c, :], m.V[:, c, cols], start=True, stop=c == 0)
                    if c:
                        i = pe.matmul(out, m.E[h % 2][:, LEVELS, c * P:(c + 1) * P], m.St[:, c - 1, cols], start=False, stop=True)
                i.then_inc(out_done, 1)

            sums(0)
            sums(1)
            for h in range(HH):
                scores(h)
                outputs(h)
                if h + 2 < HH:
                    sums(h + 2)


def cross_projection_phase(nc, sem, PS, w, g0, u, um, m):
    free = sem("cross_free")
    scale = XD ** -0.5

    with nc.Block() as block:
        @block.sync
        def _(sp):
            with sp.Fori(0, 6) as i:
                for j in range(2):
                    w.load(sp, g0 + 2 + j, i, 2)

        @block.scalar
        def _(act):
            act.sem_inc(free, 2)
            for part in range(3):
                with act.Fori(0, 2) as i:
                    for j in range(2):
                        g = g0 + 4 * part + j
                        w.split_hi(act, g + 1, i, 2)
                        w.wait_used(act, g, i, 2)
                        if part == 0:
                            out, src = m.qT[:, bass.ds(i * 4 + 2 * j, 2), :], PS[:, 2 * j:2 * j + 2, :]
                        elif part == 1:
                            out, src = m.kT[:, bass.ds(i * 4 + 2 * j, 2), :], PS[:, 2 * j:2 * j + 2, 0:NMEM]
                        else:
                            out, src = m.Vm[:, :, bass.ds(i * 512 + j * 256, 256)], PS[:, 2 * j:2 * j + 2, 0:256]
                        act.activation(out, src, ACT.Copy, scale=scale if part == 0 else 1.0).then_inc(free, 1)

        @block.vector
        def _(dve):
            with dve.Fori(0, 6) as i:
                for j in range(2):
                    w.split_lo(dve, g0 + 1 + j, i, 2)

        @block.tensor
        def _(pe):
            for part in range(3):
                with pe.Fori(0, 2) as i:
                    for j in range(2):
                        g = g0 + 4 * part + j
                        w.ready(pe, g, i, 2)
                        pe.wait_ge(free, plus(i, 2, 4 * part + j + 1))
                        if part < 2:
                            n = (SEQ, NMEM)[part]
                            block_to_features(pe, w, g, (u, um)[part], lambda t: PS[:, 2 * j + t, 0:n])
                        else:
                            block_to_tokens(pe, w, g, um, lambda t, h: PS[:, 2 * j + t, 0:256], nt=MT)


def cross_attention_phase(nc, sem, PS, m, uh, ul):
    scored, max_ready, exped, p_ready, turned, pt_act, pt_dve, out_done, hi_done, lo_done = (
        sem(f"cross_{n}") for n in ("scored", "max", "exped", "p", "turned", "ptact", "ptdve", "out", "hi", "lo"))

    with nc.Block() as block:
        @block.scalar
        def _(act):
            def exps(h):
                act.wait_ge(max_ready, h + 1)
                for t in range(NT):
                    act.activation(m.Pm[h % 2][:, t, :], PS[:, 2 * (h % 2) + t // 2, (t % 2) * 256:(t % 2) * 256 + 256], ACT.Exp,
                                   bias=m.xmax[h % 2][:, t:t + 1], accum_out=m.xsum[h % 2][:, t:t + 1]).then_inc(exped, 1)

            exps(0)
            for h in range(XH):
                if h + 1 < XH:
                    exps(h + 1)
                act.wait_ge(turned, h + 1)
                act.activation(m.PTm[h % 2][:, 0, :], PS[:, 4, :], ACT.Copy).then_inc(pt_act, 1)
                for f in range(2):
                    act.wait_ge(out_done, 2 * h + f + 1)
                    act.activation(uh[:, 2 * h + f, :], PS[:, 6 + f, :], ACT.Copy).then_inc(hi_done, 1)

        @block.vector
        def _(dve):
            def maxes(h):
                dve.wait_ge(scored, h + 1)
                dve.tensor_reduce(m.xmax[h % 2][:], PS[:, 2 * (h % 2):2 * (h % 2) + 2, :].rearrange("p a (t n) -> p (a t) n", n=NMEM),
                                  AX.X, ALU.max)
                dve.drain()
                dve.tensor_scalar(m.xmax[h % 2][:], m.xmax[h % 2][:], -1.0, None, ALU.mult).then_inc(max_ready, 1)

            maxes(0)
            for h in range(XH):
                if h + 1 < XH:
                    maxes(h + 1)
                dve.wait_ge(exped, NT * (h + 1))
                dve.reciprocal(m.xsum[h % 2][:], m.xsum[h % 2][:])
                dve.drain()
                dve.tensor_tensor(m.Pm[h % 2][:], m.Pm[h % 2][:], m.xsum[h % 2][:].unsqueeze(2).to_broadcast([P, NT, NMEM]),
                                  ALU.mult).then_inc(p_ready, 1)
                dve.wait_ge(turned, h + 1)
                dve.tensor_copy(m.PTm[h % 2][:, 1, :], PS[:, 5, :]).then_inc(pt_dve, 1)
                for f in range(2):
                    dve.wait_ge(hi_done, 2 * h + f + 1)
                    dve.tensor_tensor(ul[:, 2 * h + f, :], PS[:, 6 + f, :], uh[:, 2 * h + f, :], ALU.subtract).then_inc(lo_done, 1)

        @block.tensor
        def _(pe):
            def scores(h):
                if h >= 2:
                    pe.wait_ge(exped, NT * (h - 1))
                for t in range(NT):
                    out = PS[:, 2 * (h % 2) + t // 2, (t % 2) * 256:(t % 2) * 256 + 256]
                    for f in range(2):
                        i = pe.matmul(out, m.qT[:, 2 * h + f, t * P:(t + 1) * P], m.kT[:, 2 * h + f, :], start=f == 0, stop=f == 1)
                i.then_inc(scored, 1)

            scores(0)
            for h in range(XH):
                if h + 1 < XH:
                    scores(h + 1)
                pe.wait_ge(p_ready, h + 1)
                if h:
                    pe.wait_ge(pt_act, h)
                    pe.wait_ge(pt_dve, h)
                for t in range(NT):
                    for k in range(MT):
                        i = pe.transpose(PS[:, 4 + k, t * P:(t + 1) * P], m.Pm[h % 2][:, t, k * P:(k + 1) * P], m.ident)
                i.then_inc(turned, 1)
                pe.wait_ge(pt_act, h + 1)
                pe.wait_ge(pt_dve, h + 1)
                for f in range(2):
                    if h:
                        pe.wait_ge(lo_done, 2 * h - 1 + f)
                    for k in range(MT):
                        a = h * XD + f * P
                        i = pe.matmul(PS[:, 6 + f, :], m.Vm[:, k, a:a + P], m.PTm[h % 2][:, k, :], start=k == 0, stop=k == 1)
                    i.then_inc(out_done, 1)


def second_model(nc, PS, X, stream_mem, uh, ul, free, ins, out):
    (w2, consts, mask_in, bands_in, flag_in, mem_in, norm_gains, row_in, pool_w, final_gain) = ins
    mem = Memory(nc)
    mem.top = free
    m, f = Box(), Box()
    start_xn = mem.top
    xn = mem.put("xn2", [P, NT, D])
    m.mix = xn
    after_xn = mem.top
    mem.top = start_xn
    m.lb, m.e = mem.put("lb", [P, 2 * DA]), mem.put("lb_exp", [P, 2 * DA])
    m.esum, m.lnsum = mem.put("lb_sum", [P, DA]), mem.put("lb_lnsum", [P, DA])
    m.ln1m, m.lnlb = mem.put("ln_one_less", [P, DA]), mem.put("ln_lb", [P, DA])
    assert mem.top <= after_xn
    mem.top = after_xn
    table = mem.put("table2", [P, P + (LEVELS + 1) * P + P])
    m.ident = table[:, 0:P]
    m.level = table[:, P:P + (LEVELS + 1) * P]
    m.after = table[:, P + (LEVELS + 1) * P:]
    masks = mem.put("masks", [P, (LEVELS + 2) * 256], U8)
    m.masks = masks[:, :]
    gains = mem.put("norm_gains2", [P, 5 * KD])
    m.flag = mem.put("flag", [P, 2])
    m.sums, m.rstd, m.scratch = mem.put("sums2", [P, NT]), mem.put("rstd2", [P, NT]), mem.put("scratch2", [P, HH * NT])
    m.osum, m.orstd, m.dec = mem.put("osum", [P, HH * NT]), mem.put("orstd", [P, HH * NT]), mem.put("dec", [P, HH * 2])
    m.xmax = [mem.put(f"xmax{i}", [P, NT]) for i in range(2)]
    m.xsum = [mem.put(f"xsum{i}", [P, NT]) for i in range(2)]
    shared = mem.top
    m.LF, m.K, m.V, m.G = (mem.put(n, [P, NT, DA]) for n in ("LF", "K2", "V2", "G2"))
    m.Q = mem.put("Q2", [P, HH, SEQ])
    e_at = mem.top
    m.E = [mem.put(f"E{i}", [P, LEVELS + 1, SEQ]) for i in range(2)]
    after_e = mem.top
    m.Kf = [mem.put(f"Kf{i}", [P, SEQ]) for i in range(2)]
    m.AT = [mem.put(f"AT{i}", [P, NT, P]) for i in range(2)]
    m.St = mem.put("St", [P, NT - 1, DA])
    end = mem.top
    mem.top = after_e
    bands = mem.put("bands", [P, 12 * P])
    m.bands = bands
    m.band = lambda g, kind: bands[:, (g * 3 + kind) * P:(g * 3 + kind + 1) * P]
    m.pool_w = mem.put("pool_w", [P, 4 * P])
    end = max(end, mem.top)
    assert mem.top <= after_e + 10 * 1024
    mem.top = e_at
    m.t1, m.t2, m.U = (mem.put(n, [P, NT, DA]) for n in ("t1", "t2", "U2"))
    m.one_less, m.pscale, m.hnorm = (mem.put(n, [P, DA]) for n in ("one_less", "pscale", "hnorm"))
    assert mem.top <= after_e
    mem.top = e_at
    m.pT, m.Kp = mem.put("pT", [P, 4, SEQ]), mem.put("Kp", [P, NT, DA])
    mem.top = shared
    f.silu, f.h = mem.put("silu", [P, 2, SEQ]), mem.put("h", [P, 2, SEQ])
    f.h_hi, f.h_lo = mem.put("h_hi", [P, 2, SEQ], F32R), mem.put("h_lo", [P, 2, SEQ], F32R)
    mem.top = shared
    mh, ml = mem.put("mem_hi", [P, KD, NMEM], F32R), mem.put("mem_lo", [P, KD, NMEM], F32R)
    m.qT, m.kT = mem.put("qT", [P, KD, SEQ]), mem.put("kT", [P, KD, NMEM])
    m.Vm = mem.put("Vm", [P, MT, D])
    m.Pm = [mem.put(f"Pm{i}", [P, NT, NMEM]) for i in range(2)]
    m.PTm = [mem.put(f"PTm{i}", [P, MT, SEQ]) for i in range(2)]
    m.memory = mem.put("memory", [P, MT, D])
    end = max(end, mem.top)
    assert end <= nc.sbuf_usable_end, (end, nc.sbuf_usable_end)
    mem.top = shared
    final_row = mem.put("final_row", [P, D])
    mask_numbers = mem.put("mask_numbers", [P, (LEVELS + 2) * 256])

    u = (uh, ul)
    with ExitStack() as ctx:
        sem = Semaphores(nc, ctx)
        arrived = sem("tables2_arrived")
        with nc.Block() as block:
            @block.sync
            def _(sp):
                sp.dma_start(table[:], consts).then_inc(arrived, 16)
                sp.dma_start(mask_numbers[:], mask_in).then_inc(arrived, 16)

            @block.vector
            def _(dve):
                dve.wait_ge(arrived, 32)
                dve.tensor_copy(masks[:], mask_numbers[:])
        nc.all_engine_barrier(sems_to_clear=sem.span())

    with ExitStack() as ctx:
        sem = Semaphores(nc, ctx)
        with nc.Fori(0, DEPTH) as layer:
            w = WeightStream(sem, *stream_mem, w2, NB2, layer)
            small = sem("small2")
            one = bass.ds(layer, 1)

            def start(kind, eng):
                if kind == "sync":
                    eng.dma_start(gains[:], norm_gains[one].rearrange("o p n -> p (o n)")).then_inc(small, 16)
                    w.load(eng, 0)
                    w.load(eng, 1)
                    eng.wait_ge(small, 16)
                if kind == "scalar":
                    eng.wait_ge(small, 16)
                    w.split_hi(eng, 0)
                if kind == "vector":
                    w.split_lo(eng, 0)

            def load_memory(kind, eng):
                if kind == "sync":
                    eng.dma_start(m.memory[:], mem_in.rearrange("b (t p) n -> p (b t) n", p=P)).then_inc(m.memory_arrived, 16)
                    eng.wait_ge(m.memory_arrived, 16)

            def norm(name, n, extra=None):
                to_features_phase(nc, sem, name, PS, m.ident, xn, NT, uh, ul, extra=extra, norm=(X, m.sums, m.rstd, m.scratch),
                                  gain=lambda k: gains[:, n * KD + k:n * KD + k + 1])

            norm("normf1", 0, start)
            ffn_phase(nc, sem, "ffn1", PS, w, 0, u, X, f)
            norm("normmix", 1)
            projection_phase_2(nc, sem, PS, w, 33, u, m, one, (bands_in, pool_w), row_in, flag_in)
            pool_and_states_phase(nc, sem, PS, m)
            recurrence_phase(nc, sem, PS, m)
            to_features_phase(nc, sem, "mix2", PS, m.ident, m.mix, NT, uh, ul)
            residual_phase(nc, sem, "out2", PS, w, 43, u, X)
            m.memory_arrived = sem("memory_arrived")
            norm("normxa", 2, load_memory)
            to_features_phase(nc, sem, "normmem", PS, m.ident, xn, MT, mh, ml, norm=(m.memory, m.sums, m.rstd, m.scratch),
                              gain=lambda k: gains[:, 3 * KD + k:3 * KD + k + 1])
            cross_projection_phase(nc, sem, PS, w, 47, u, (mh, ml), m)
            cross_attention_phase(nc, sem, PS, m, uh, ul)
            residual_phase(nc, sem, "xout", PS, w, 59, u, X)
            norm("normf2", 4)
            ffn_phase(nc, sem, "ffn2", PS, w, 63, u, X, f)
            nc.all_engine_barrier(sems_to_clear=sem.span())

    with ExitStack() as ctx:
        sem = Semaphores(nc, ctx)
        arrived, squared, mean_ready, rstd_ready, done, stored = (
            sem(f"final_{n}") for n in ("arrived", "squared", "mean", "rstd", "done", "stored"))
        with nc.Block() as block:
            @block.sync
            def _(sp):
                sp.dma_start(final_row[:], final_gain).then_inc(arrived, 16)
                for t in range(NT):
                    sp.wait_ge(done, t + 1)
                    sp.dma_start(out[0, t * P:(t + 1) * P, :], X[:, t, :]).then_inc(stored, 16)
                sp.wait_ge(stored, 16 * NT)

            @block.scalar
            def _(act):
                for t in range(NT):
                    act.activation(xn[:, t, :], X[:, t, :], ACT.Square, accum_out=m.sums[:, t:t + 1]).then_inc(squared, 1)
                act.wait_ge(mean_ready, 1)
                act.activation(m.rstd[:], m.rstd[:], ACT.Sqrt).then_inc(rstd_ready, 1)

            @block.vector
            def _(dve):
                dve.wait_ge(squared, NT)
                dve.tensor_scalar(m.sums[:], m.sums[:], 1.0 / D, EPS, ALU.mult, ALU.add)
                dve.drain()
                dve.reciprocal(m.rstd[:], m.sums[:]).then_inc(mean_ready, 1)
                dve.wait_ge(rstd_ready, 1)
                refine(dve, m.sums[:], m.rstd[:], m.scratch[:, 0:NT])
                dve.wait_ge(arrived, 16)
                for t in range(NT):
                    dve.scalar_tensor_tensor(X[:, t, :], X[:, t, :], m.rstd[:, t:t + 1], final_row[:], ALU.mult, ALU.mult)\
                       .then_inc(done, 1)


def two_models(nc, x, first_ins, second_ins, out):
    mem = Memory(nc)
    PS = nc.alloc_psum_tensor("PS", [P, 8, 512], F32)
    X = mem.put("X", [P, NT, D])
    uh, ul = mem.put("uh", [P, KD, SEQ], F32R), mem.put("ul", [P, KD, SEQ], F32R)
    stream_mem = ([mem.put(f"w_raw{i}", [P, BLK]) for i in range(2)], [mem.put(f"w_hi{i}", [P, BLK], F32R) for i in range(2)],
                  [mem.put(f"w_lo{i}", [P, BLK], F32R) for i in range(2)])
    with nc.semaphore("x_arrived") as x_arrived:
        with nc.Block() as block:
            @block.sync
            def _(sp):
                sp.dma_start(X[:], x.rearrange("b (t p) n -> p (b t) n", p=P)).then_inc(x_arrived, 16)
                sp.wait_ge(x_arrived, 16)
        nc.all_engine_barrier(sems_to_clear=range(x_arrived.num, x_arrived.num + 1))
    first_model(nc, PS, X, stream_mem, uh, ul, mem.top, first_ins)
    second_model(nc, PS, X, stream_mem, uh, ul, mem.top, second_ins, out)


def wide_blocks(a):
    n = a.shape[2] // 256
    return a.reshape(DEPTH, KD, P, n, 256).transpose(0, 3, 2, 1, 4).reshape(DEPTH, n, P, BLK)


def deep_blocks(a):
    n = a.shape[1] // 256
    return a.reshape(DEPTH, n, 2, P, D).transpose(0, 1, 3, 2, 4).reshape(DEPTH, n, P, BLK)


def columns(a):
    return a.reshape(DEPTH, KD, P).transpose(0, 2, 1)


def replicated(a):
    return np.repeat(a[:, None, :], P, axis=1)


def kernel(**inputs):
    import concourse.bacc as _bacc
    from concourse.bass_utils import run_bass_kernel_spmd as _run

    a = {n: np.asarray(v) for n, v in inputs.items()}
    w_in = a["w_in"]
    q4 = 4 * 512
    fox, dil = w_in[:, :, 0:q4], w_in[:, :, q4 + NH:]
    w1 = np.concatenate([wide_blocks(fox), wide_blocks(dil), wide_blocks(a["w_out"]), deep_blocks(a["w_ple"]),
                         wide_blocks(a["w_ple_gate"])], 1)
    fa_w = w_in[:, :, q4:q4 + NH].reshape(DEPTH, KD, P, NH).transpose(0, 2, 1, 3).reshape(DEPTH, P, KD * NH)

    def ffn(n):
        up, gate, down = wide_blocks(a[n + "_w1_2"]), wide_blocks(a[n + "_w3_2"]), deep_blocks(a[n + "_w2_2"])
        order = [up[:, 0], gate[:, 0]]
        for c in range(1, NCHUNK):
            order += [up[:, c], down[:, c - 1], gate[:, c]]
        return np.stack(order + [down[:, NCHUNK - 1]], 1)

    qfigu = wide_blocks(a["w_in_2"])
    mixer = np.concatenate([qfigu[:, 2:4], qfigu[:, 4:6], qfigu[:, 8:10], qfigu[:, 0:2], qfigu[:, 6:8]], 1)
    w2 = np.concatenate([ffn("ffn1"), mixer, wide_blocks(a["w_out_2"]), wide_blocks(a["xa_wq_2"]),
                         wide_blocks(a["xa_wkv_2"]), wide_blocks(a["xa_wo_2"]), ffn("ffn2")], 1)
    first_table, second_table, masks, bands, flag = constants()
    arrays = {
        "x": a["x"], "w1": w1, "first_table": first_table, "positions": a["positions"],
        "gains1": np.concatenate([columns(a["norm_g"]), columns(a["ple_norm_g"])], 2),
        "qk_gains": replicated(a["qk_norm_g"].reshape(DEPTH, 4 * HEAD)), "fa_w": fa_w, "fa_b": replicated(a["b_f"]),
        "pT": a["p"][:, 0].transpose(0, 2, 1).reshape(DEPTH, 2, P, SEQ).transpose(0, 2, 1, 3).reshape(DEPTH, P, 2 * SEQ),
        "w2": w2, "second_table": second_table, "masks": masks, "bands": bands, "flag": flag, "mem": a["mem_2"],
        "gains2": np.concatenate([columns(a[n]) for n in ("ffn1_norm_2", "mix_norm_2", "xa_norm_2", "mem_norm_2", "ffn2_norm_2")], 2),
        "hgrn_norm": replicated(a["hgrn_norm_2"]), "pool_scale": replicated(a["pool_scale_2"]),
        "lb_logits": np.concatenate(list(replicated(a["lb_logits_2"])), 1),
        "pool_w": a["pool_w_2"].transpose(0, 2, 1, 3).reshape(DEPTH, P, 4 * P),
        "final": np.repeat(a["final_norm_2"][None, :], P, axis=0),
    }
    nc = _bacc.Bacc("TRN2", target_bir_lowering=False, num_devices=1)
    fed, ap = {}, {}
    for name, v in arrays.items():
        v = np.ascontiguousarray(v)
        fed[f"in_{name}"] = v
        ap[name] = nc.dram_tensor(f"in_{name}", v.shape, mybir.dt.from_np(v.dtype), kind="ExternalInput").ap()
    out = nc.dram_tensor("out_0", (1, SEQ, D), F32, kind="ExternalOutput").ap()
    two_models(nc, ap["x"],
               [ap[n] for n in ("w1", "first_table", "positions", "gains1", "qk_gains", "fa_w", "fa_b", "pT")],
               [ap["w2"], ap["second_table"], ap["masks"], ap["bands"], ap["flag"], ap["mem"], ap["gains2"],
                (ap["hgrn_norm"], ap["pool_scale"], ap["lb_logits"]), ap["pool_w"], ap["final"]], out)
    return _run(nc, [fed], core_ids=[0]).results[0]["out_0"]
```

```python
from contextlib import ExitStack

import numpy as np

import concourse.bass as bass
from concourse import mybir

F32 = mybir.dt.float32
F32R = mybir.dt.float32r
I32 = mybir.dt.int32
U8 = mybir.dt.uint8
ALU = mybir.AluOpType
ACT = mybir.ActivationFunctionType
AX = mybir.AxisListType

P = 128
DEPTH = 2
SEQ = 512
NT = SEQ // P
D = 1024
KD = D // P
EPS = 1e-6
NEG = -1e30
LOWEST = -3.0e38

HEAD = 64
NH = 8
ROPE = 16
HALF = ROPE // 2
PLE = 256

NMEM = 256
MT = NMEM // P
DFF = 2816
DA = 512
HH = 4
LEVELS = 7
XH = 4
XD = 256

BLK = 2048
NB1 = 25
NB2 = 96
NCHUNK = DFF // 256

S0, S1, S2, S3 = 0, 128, 384, 768
SOFF = (S0, S1, S2, S3)
PTOFF = (0, 512, 1024, 896)
MB_CAUSAL, MB_DIL = 0, 1


def constants():
    q = np.arange(P)[:, None]
    k = np.arange(P)[None, :]
    fox = np.zeros((P, NT, P), np.float32)
    fox[:, NT - 1] = np.where(k <= q, 0.0, NEG)
    dil = np.zeros((P, NT, P), np.float32)
    for j in range(NT):
        dist = (NT - 1 - j) * P + q - k
        count = ((dist >= 0) & (dist <= 128)).astype(int) + ((dist >= 0) & (dist % 4 == 0)) + ((dist >= 0) & (dist % 16 == 0))
        dil[:, j] = np.where(count > 0, np.log(np.maximum(count, 1).astype(np.float32)), NEG)
    upto = np.ones((P, NT, P), np.float32)
    upto[:, 0] = (q <= k)
    ident = np.eye(P, dtype=np.float32)
    inv = (np.float32(500000.0) ** (-np.arange(HALF, dtype=np.float32) / np.float32(HALF))).astype(np.float32)
    inv = np.broadcast_to(inv, (P, HALF))
    first = np.concatenate([ident, fox.reshape(P, -1), dil.reshape(P, -1), upto.reshape(P, -1), inv], 1)

    s, t = q, k
    level = np.zeros((P, LEVELS + 1, P), np.float32)
    masks = []
    for n in range(LEVELS):
        m = P >> (n + 1)
        ref = (t // (2 * m)) * 2 * m + m - 1
        right = (t // m) % 2 == 1
        level[:, n] = np.where(right, (s > ref) & (s <= t), (s > t) & (s <= ref))
        keep = ((s // (2 * m)) == (t // (2 * m))) & ((s // m) % 2 == 0)
        masks.append(keep[:, right[0]])
    level[:, LEVELS] = s <= t
    after = (s > t).astype(np.float32)
    second = np.concatenate([ident, level.reshape(P, -1), after], 1)
    masks = np.concatenate([np.tile(a, (1, NT)) for a in masks + [s == t]], 1).astype(np.float32)
    bands = np.zeros((P, 4, 3, P), np.float32)
    for g, w in enumerate((2, 4, 8, 16)):
        bands[:, g, 0] = ((s <= t) & (s > t - w)) / np.minimum(t + 1, w) - (s == t)
        bands[:, g, 1] = ((s <= t) & (s > t - w)) / w - (s == t)
        bands[:, g, 2] = (s - P > t - w) / w
    flag = np.zeros((DEPTH, P, 2), np.float32)
    flag[1:, :, 0] = 1.0
    flag[:1, :, 1] = NEG
    return [np.ascontiguousarray(a, np.float32) for a in (first, second, masks, bands.reshape(P, -1), flag)]


class Semaphores:

    def __init__(self, nc, ctx):
        self.nc, self.ctx, self.numbers = nc, ctx, []

    def __call__(self, name):
        s = self.ctx.enter_context(self.nc.semaphore(name))
        self.numbers.append(s.num)
        return s

    def span(self):
        return range(min(self.numbers), max(self.numbers) + 1)


class Memory:

    def __init__(self, nc):
        self.nc, self.top = nc, (nc.sbuf_base + 63) // 64 * 64

    def put(self, name, shape, dtype=F32):
        size = 4
        for n in shape[1:]:
            size *= n
        if dtype == U8:
            size //= 4
        h = self.nc.alloc_sbuf_tensor_at(name, shape, dtype, offset=self.top)
        self.top += (size + 63) // 64 * 64
        return h


def plus(i, step, base):
    return base if i is None else i * step + base


def refine(dve, mean, root, scratch):
    dve.scalar_tensor_tensor(scratch, root, -0.5, root, ALU.mult, ALU.mult)
    dve.drain()
    dve.tensor_tensor(scratch, scratch, mean, ALU.mult)
    dve.drain()
    dve.scalar_tensor_tensor(root, scratch, 1.5, root, ALU.add, ALU.mult)
    dve.drain()


class WeightStream:

    def __init__(self, sem, raw, hi, lo, dram, per_layer, layer):
        self.raw, self.hi, self.lo = raw, hi, lo
        self.dram = dram.rearrange("l b p n -> (l b) p n")
        self.per_layer, self.layer = per_layer, layer
        self.loaded = [sem("w_loaded0"), sem("w_loaded1")]
        self.hi_done, self.lo_done, self.used = sem("w_hi_done"), sem("w_lo_done"), sem("w_used")

    def load(self, sp, g, i=None, step=0):
        if i is None and g >= self.per_layer:
            return
        if i is not None or g >= 2:
            sp.wait_ge(self.lo_done, plus(i, step, g - 1))
        sp.dma_start(self.raw[g % 2][:], self.dram[bass.ds(self.layer * self.per_layer + plus(i, step, g), 1)]
                     .rearrange("o p n -> p (o n)")).then_inc(self.loaded[g % 2], 16)

    def split_hi(self, act, g, i=None, step=0):
        if i is None and g >= self.per_layer:
            return
        act.wait_ge(self.loaded[g % 2], plus(i, step * 8, 16 * (g // 2 + 1)))
        if i is not None or g >= 2:
            act.wait_ge(self.used, plus(i, step, g - 1))
        act.activation(self.hi[g % 2][:], self.raw[g % 2][:], ACT.Copy).then_inc(self.hi_done, 1)

    def split_lo(self, dve, g, i=None, step=0):
        if i is None and g >= self.per_layer:
            return
        dve.wait_ge(self.hi_done, plus(i, step, g + 1))
        dve.tensor_tensor(self.lo[g % 2][:], self.raw[g % 2][:], self.hi[g % 2][:], ALU.subtract).then_inc(self.lo_done, 1)

    def ready(self, pe, g, i=None, step=0):
        pe.wait_ge(self.lo_done, plus(i, step, g + 1))

    def wait_used(self, eng, g, i=None, step=0):
        eng.wait_ge(self.used, plus(i, step, g + 1))


def split_products(pe, out, still, moving, first, last):
    (sh, sl), (mh, ml) = still, moving
    pe.matmul(out, sh, mh, start=first, stop=False)
    pe.matmul(out, sh, ml, start=False, stop=False)
    return pe.matmul(out, sl, mh, start=False, stop=last)


def block_to_tokens(pe, w, g, u, outs, nt=NT, kd=KD, halves=1, before=None, made=None):
    if made:
        n = BLK // KD
        for k in range(KD):
            for t in range(nt):
                if t == 0 or k == 0:
                    made(pe, k, t + 1)
                last = split_products(
                    pe, outs(t, 0), [x[:, k, t * P:(t + 1) * P] for x in u],
                    (w.hi[g % 2][:, k * n:(k + 1) * n], w.lo[g % 2][:, k * n:(k + 1) * n]), k == 0, k == KD - 1)
        last.then_inc(w.used, 1)
        return
    n = BLK // kd // halves
    for t in range(nt):
        if before:
            before(t)
        for h in range(halves):
            for k in range(kd):
                a = k * n * halves + h * n
                last = split_products(
                    pe, outs(t, h), [x[:, k, t * P:(t + 1) * P] for x in u],
                    (w.hi[g % 2][:, a:a + n], w.lo[g % 2][:, a:a + n]), k == 0, k == kd - 1)
    last.then_inc(w.used, 1)


def block_to_features(pe, w, g, u, outs, made=None):
    for f, k in [(f, k) for k in range(KD) for f in range(2)] if made else [(f, k) for f in range(2) for k in range(KD)]:
        if made and (f == 0 or k == 0):
            made(pe, k, f + 1)
        a = k * 256 + f * P
        last = split_products(
            pe, outs(f), (w.hi[g % 2][:, a:a + P], w.lo[g % 2][:, a:a + P]),
            [x[:, k, :] for x in u], k == 0, k == KD - 1)
    last.then_inc(w.used, 1)


def to_features_phase(block, sem, name, PS, ident, src, nt, uh, ul, gain=None, norm=None, extra=None,
                      squares=None, late=None, src_done=None):
    squared, mean_ready, rstd_ready, src_ready = (sem(f"{name}_{n}") for n in ("squared", "mean", "rstd", "src"))
    turned, hi_ready, lo_ready = sem(f"{name}_turned"), sem(f"{name}_hi"), sem(f"{name}_lo")
    n = nt * P

    @block.sync
    def _(sp):
        if extra:
            extra("sync", sp)

    @block.scalar
    def _(act):
        if norm:
            x, sums, rstd, scratch = norm
            if not squares:
                for t in range(nt):
                    act.activation(src[:, t, :], x[:, t, :], ACT.Square, accum_out=sums[:, t:t + 1]).then_inc(squared, 1)
            act.wait_ge(mean_ready, 1)
            act.activation(rstd[:, 0:nt], rstd[:, 0:nt], ACT.Sqrt).then_inc(rstd_ready, 1)
        if extra:
            extra("scalar", act)
        for k in range(KD):
            act.wait_ge(turned, k + 1)
            act.activation(uh[:, k, 0:n], PS[:, k, 0:n], ACT.Copy, scale=gain(k) if gain else 1.0).then_inc(hi_ready, 1)
        if late:
            late("scalar", act)

    @block.vector
    def _(dve):
        if norm:
            x, sums, rstd, scratch = norm
            if squares != "made":
                dve.wait_ge(*(squares or (squared, nt)))
            dve.tensor_scalar(sums[:, 0:nt], sums[:, 0:nt], 1.0 / D, EPS, ALU.mult, ALU.add)
            dve.drain()
            dve.reciprocal(rstd[:, 0:nt], sums[:, 0:nt]).then_inc(mean_ready, 1)
            dve.wait_ge(rstd_ready, 1)
            refine(dve, sums[:, 0:nt], rstd[:, 0:nt], scratch[:, 0:nt])
            for t in range(nt):
                dve.tensor_scalar(src[:, t, :], x[:, t, :], rstd[:, t:t + 1], None, ALU.mult).then_inc(src_ready, 1)
        if extra:
            extra("vector", dve)
        for k in range(KD):
            dve.wait_ge(hi_ready, k + 1)
            if gain:
                i = dve.scalar_tensor_tensor(ul[:, k, 0:n], PS[:, k, 0:n], gain(k), uh[:, k, 0:n], ALU.mult, ALU.subtract)
            else:
                i = dve.tensor_tensor(ul[:, k, 0:n], PS[:, k, 0:n], uh[:, k, 0:n], ALU.subtract)
            i.then_inc(lo_ready, 1)
        if late:
            late("vector", dve)

    @block.tensor
    def _(pe):
        if extra:
            extra("tensor", pe)
        if src_done:
            pe.wait_ge(*src_done)
        for t in range(nt):
            if norm:
                pe.wait_ge(src_ready, t + 1)
            for k in range(KD):
                i = pe.transpose(PS[:, k, t * P:(t + 1) * P], src[:, t, k * P:(k + 1) * P], ident)
                if t == nt - 1:
                    i.then_inc(turned, 1)

    return lambda pe, k, banks: pe.wait_ge(lo_ready, max(k + 1, banks))


def residual_phase(block, sem, name, PS, w, g0, u, X, m, extra_blocks=0, made=None):
    squared, sums_ready = sem(f"{name}_squared"), sem(f"{name}_sums")
    free = sem(f"{name}_free")

    @block.sync
    def _(sp):
        if g0 + 6 <= w.per_layer:
            with sp.Fori(0, 2) as i:
                for j in range(2):
                    w.load(sp, g0 + 2 + j, i, 2)
        else:
            w.load(sp, g0 + 2)
            w.load(sp, g0 + 3)
        for j in range(extra_blocks):
            w.load(sp, g0 + 6 + j)

    @block.scalar
    def _(act):
        with act.Fori(0, 2) as i:
            for j in range(2):
                w.split_hi(act, g0 + 1 + j, i, 2)
        for part, (cols, n) in enumerate(((slice(0, 768), 3), (slice(768, D), 4))):
            act.wait_ge(free, 2 + n)
            for t in range(NT):
                act.activation(m.mix[:, t, cols], X[:, t, cols], ACT.Square,
                               accum_out=m.part_sums[:, part * NT + t:part * NT + t + 1]).then_inc(squared, 1)

    @block.vector
    def _(dve):
        dve.sem_inc(free, 2)
        with dve.Fori(0, 2) as i:
            for j in range(2):
                w.split_lo(dve, g0 + 1 + j, i, 2)
                w.wait_used(dve, g0 + j, i, 2)
                part = X[:, :, bass.ds(i * 512 + j * 256, 256)]
                dve.tensor_tensor(part, PS[:, 4 * j:4 * j + 4, 0:256], part, ALU.add).then_inc(free, 1)
        dve.wait_ge(squared, 2 * NT)
        dve.tensor_tensor(m.sums[:, 0:NT], m.part_sums[:, 0:NT], m.part_sums[:, NT:2 * NT], ALU.add).then_inc(sums_ready, 1)

    @block.tensor
    def _(pe):
        with pe.Fori(0, 2) as i:
            for j in range(2):
                w.ready(pe, g0 + j, i, 2)
                pe.wait_ge(free, plus(i, 2, 1 + j))
                block_to_tokens(pe, w, g0 + j, u, lambda t, h: PS[:, 4 * j + t, 0:256], made=made if j == 0 else None)
        pe.wait_ge(free, 6)

    return sums_ready, 1


def projection_phase_1(block, sem, name, PS, w, g0, u, m, dilated, made=None, at_free=None, mixed=None):
    g_out = sem(f"{name}_gout")
    z_out, sq_done, mean_ready, rstd_ready = (sem(f"{name}_{n}") for n in ("zout", "sq", "mean", "rstd"))
    normed, turned, even_copied, odd_copied, v_out = (sem(f"{name}_{n}") for n in ("normed", "turned", "even", "odd", "vout"))
    if not dilated:
        fa_done, fa_z, fa_exp, fa_ln = (sem(f"{name}_{n}") for n in ("fa", "faz", "faexp", "faln"))
        lf_ready, cum_done, ones_set, cum_copied, cum_moved = (
            sem(f"{name}_{n}") for n in ("lf", "cum", "ones", "cumcopied", "cummoved"))
    zn = m.zn
    gains = (2, 3) if dilated else (0, 1)

    @block.sync
    def _(sp):
        for j in range(8):
            w.load(sp, g0 + 2 + j)
        if not dilated:
            sp.wait_ge(ones_set, 2)
            sp.wait_ge(cum_copied, 2)
            sp.dma_start(m.QT[HEAD + 1:HEAD + 2, :, :], m.cum[:]).then_inc(cum_moved, 16)
            sp.dma_start(m.KT[HEAD:HEAD + 1, :, :], m.ncum[:]).then_inc(cum_moved, 16)
            sp.wait_ge(cum_moved, 32)

    @block.gpsimd
    def _(pool):
        if not dilated:
            pool.wait_ge(*at_free)
            pool.memset(m.QT[HEAD:HEAD + 2, :, :], 1.0).then_inc(ones_set, 1)
            pool.memset(m.KT[HEAD:HEAD + 2, :, :], 1.0).then_inc(ones_set, 1)

    def heads(j, odd):
        dst = (m.QT, m.KT)[j][0:HEAD, :, :].rearrange("p (a two) n -> p a two n", two=2)[:, :, odd, :]
        return dst, PS[HEAD * odd:HEAD * odd + HEAD, 0:4, :]

    scales = (HEAD ** -0.5, 1.0)

    @block.scalar
    def _(act):
        def take(j):
            w.wait_used(act, g0 + 2 * j + 1)
            act.activation(zn[j][:], PS[:, 4 * j:4 * j + 4, :].rearrange("p a n -> p (a n)"), ACT.Copy).then_inc(z_out, 1)

        def squares(j):
            act.wait_ge(z_out, j + 1)
            if mixed and j == 0:
                act.wait_ge(*mixed)
            act.activation(m.G[:].rearrange("p a n -> p (a n)"), zn[j][:], ACT.Square).then_inc(sq_done, 1)

        def root(j):
            act.wait_ge(mean_ready, j + 1)
            act.activation(m.rstd[:], m.rstd[:], ACT.Sqrt).then_inc(rstd_ready, 1)

        def even_heads(j):
            act.wait_ge(turned, j + 1)
            dst, src = heads(j, 0)
            act.activation(dst, src, ACT.Copy, scale=scales[j]).then_inc(even_copied, 1)

        w.split_hi(act, g0 + 1)
        if not dilated:
            act.wait_ge(fa_z, 1)
            act.activation(m.fa_e[:], m.fa_y[:], ACT.Abs).then_inc(fa_exp, 1)
            act.wait_ge(fa_exp, 1)
            act.activation(m.fa_e[:], m.fa_e[:], ACT.Exp, scale=-1.0).then_inc(fa_exp, 1)
            act.wait_ge(fa_exp, 2)
            act.activation(m.fa_e[:], m.fa_e[:], ACT.Ln, bias=1.0).then_inc(fa_ln, 1)
        w.split_hi(act, g0 + 2)
        take(0)
        w.split_hi(act, g0 + 3)
        squares(0)
        if not dilated:
            act.wait_ge(cum_done, 1)
            act.activation(m.cum[:], PS[0:NH, 7, :], ACT.Copy).then_inc(cum_copied, 1)
            act.activation(m.ncum[:], PS[0:NH, 7, :], ACT.Copy, scale=-1.0).then_inc(cum_copied, 1)
        root(0)
        w.split_hi(act, g0 + 4)
        take(1)
        w.split_hi(act, g0 + 5)
        squares(1)
        even_heads(0)
        root(1)
        w.split_hi(act, g0 + 6)
        w.wait_used(act, g0 + 5)
        act.activation(m.V[:], PS[:, 4:8, :], ACT.Copy).then_inc(v_out, 1)
        w.split_hi(act, g0 + 7)
        even_heads(1)
        w.split_hi(act, g0 + 8)
        w.wait_used(act, g0 + 7)
        act.activation(m.G[:], PS[:, 4:8, :], ACT.Silu).then_inc(g_out, 1)

    @block.vector
    def _(dve):
        shape = [P, NT * NH, HEAD]

        def means(j):
            dve.wait_ge(sq_done, j + 1)
            dve.tensor_reduce(m.sums[:], m.G[:].rearrange("p a (h d) -> p (a h) d", d=HEAD), AX.X, ALU.add)
            dve.drain()
            dve.tensor_scalar(m.sums[:], m.sums[:], 1.0 / HEAD, EPS, ALU.mult, ALU.add)
            dve.drain()
            dve.reciprocal(m.rstd[:], m.sums[:]).then_inc(mean_ready, 1)

        def norm(j):
            n3 = zn[j][:].rearrange("p (a d) -> p a d", d=HEAD)
            dve.wait_ge(rstd_ready, j + 1)
            refine(dve, m.sums[:], m.rstd[:], m.scratch[:])
            dve.tensor_tensor(n3, n3, m.rstd[:].unsqueeze(2).to_broadcast(shape), ALU.mult)
            dve.drain()
            gi = gains[j]
            dve.tensor_tensor(n3, n3, m.qk_gain[:, gi * HEAD:(gi + 1) * HEAD].unsqueeze(1).to_broadcast(shape), ALU.mult)
            dve.drain()
            if dilated:
                z4 = zn[j][:].rearrange("p (t h d) -> p t h d", t=NT, h=NH)
                x1, x2 = z4[:, :, :, 0:HALF], z4[:, :, :, HALF:ROPE]
                full = [P, NT, NH, HALF]
                cos, sin = (a[:].unsqueeze(2).to_broadcast(full) for a in (m.cos, m.sin))
                dve.tensor_tensor(m.rot[0][:], x1, cos, ALU.mult)
                dve.tensor_tensor(m.rot[1][:], x2, sin, ALU.mult)
                dve.tensor_tensor(m.rot[2][:], x2, cos, ALU.mult)
                dve.tensor_tensor(m.rot[3][:], x1, sin, ALU.mult)
                dve.drain()
                dve.tensor_tensor(x1, m.rot[0][:], m.rot[1][:], ALU.subtract)
                dve.tensor_tensor(x2, m.rot[2][:], m.rot[3][:], ALU.add)
                dve.drain()
            dve.sem_inc(normed, 1)

        def odd_heads(j):
            dve.wait_ge(turned, j + 1)
            dst, src = heads(j, 1)
            dve.tensor_scalar(dst, src, scales[j], None, ALU.mult).then_inc(odd_copied, 1)

        w.split_lo(dve, g0 + 1)
        if not dilated:
            dve.wait_ge(fa_done, 1)
            dve.tensor_tensor(m.fa_y[:], PS[:, 4, 0:NT * NH], m.fa_bias[:].unsqueeze(1).to_broadcast([P, NT, NH]),
                              ALU.add).then_inc(fa_z, 1)
            dve.wait_ge(fa_z, 1)
            dve.wait_ge(fa_ln, 1)
            dve.scalar_tensor_tensor(m.lf[:], m.fa_y[:], 0.0, m.fa_e[:], ALU.min, ALU.subtract).then_inc(lf_ready, 1)
        w.split_lo(dve, g0 + 2)
        w.split_lo(dve, g0 + 3)
        means(0)
        norm(0)
        w.split_lo(dve, g0 + 4)
        w.split_lo(dve, g0 + 5)
        means(1)
        odd_heads(0)
        norm(1)
        w.split_lo(dve, g0 + 6)
        w.split_lo(dve, g0 + 7)
        odd_heads(1)
        w.split_lo(dve, g0 + 8)

    @block.tensor
    def _(pe):
        def turn(j):
            pe.wait_ge(normed, j + 1)
            for pair in range(NH // 2):
                for t in range(NT):
                    a = t * NH * HEAD + pair * P
                    i = pe.transpose(PS[:, pair, t * P:(t + 1) * P], zn[j][:, a:a + P], m.ident)
            i.then_inc(turned, 1)

        def project(part, bank, before=None):
            for half in range(2):
                g = g0 + 2 * part + half
                w.ready(pe, g)
                block_to_tokens(pe, w, g, u, lambda t, h: PS[:, bank + t, half * 256:half * 256 + 256],
                                before=before if half == 0 else None, made=made if part == half == 0 else None)
                if part == half == 0 and not dilated:
                    pe.wait_ge(*at_free)
                    for t in range(NT):
                        for k in range(KD):
                            i = split_products(pe, PS[:, 4, t * NH:(t + 1) * NH], [x[:, k, t * P:(t + 1) * P] for x in u],
                                               [x[:, k * NH:(k + 1) * NH] for x in (m.fa_hi, m.fa_lo)], k == 0, k == KD - 1)
                    i.then_inc(fa_done, 1)

        project(0, 0)
        if not dilated:
            pe.wait_ge(lf_ready, 1)
            for j in range(NT):
                i = pe.matmul(PS[0:NH, 7, j * P:SEQ], m.lf[:, j * NH:(j + 1) * NH], m.upto[:, 0:SEQ - j * P],
                              start=j == 0, stop=j == NT - 1)
            i.then_inc(cum_done, 1)
            project(1, 4, lambda t: pe.wait_ge(cum_copied, 2) if t == 3 else None)
        else:
            pe.wait_ge(*mixed)
            project(1, 4)
        turn(0)
        pe.wait_ge(z_out, 2)
        project(2, 4)
        pe.wait_ge(even_copied, 1)
        pe.wait_ge(odd_copied, 1)
        turn(1)
        pe.wait_ge(v_out, 1)
        project(3, 4)

    qk_ready = [(even_copied, 2), (odd_copied, 2)] + ([] if dilated else [(cum_moved, 32)])
    return qk_ready, (g_out, 1)


def attention_phase_1(block, sem, name, PS, m, rows, mask, column, qk_ready, g_ready):
    scored, shifted, exped = (sem(f"{name}_{n}") for n in ("scored", "shifted", "exped"))
    turned, pt_act, pt_dve, out_done, mixed = (sem(f"{name}_{n}") for n in ("turned", "ptact", "ptdve", "out", "mixed"))
    score_at = [PS[:, 1, 384:512], PS[:, 2, 0:256], PS[:, 1, 0:384], PS[:, 0, 0:512]]

    @block.scalar
    def _(act):
        def exps(h):
            act.wait_ge(shifted, h + 1)
            for t in range(NT):
                part = m.S[h % 2][:, SOFF[t]:SOFF[t] + (t + 1) * P]
                act.activation(part, part, ACT.Exp, bias=m.nmax[h % 2][:, t:t + 1],
                               accum_out=m.psum[h % 4][:, t:t + 1]).then_inc(exped, 1)

        exps(0)
        for h in range(NH):
            act.wait_ge(turned, h + 1)
            if h >= 2:
                act.wait_ge(out_done, h - 1)
            act.activation(m.PT[h % 2][:, 0:512], PS[:, 3, :], ACT.Copy).then_inc(pt_act, 1)
            if h + 1 < NH:
                exps(h + 1)

    @block.vector
    def _(dve):
        def add_mask(h):
            dve.wait_ge(scored, h + 1)
            if h >= 2:
                dve.wait_ge(turned, h - 1)
            for t in range(NT):
                n = (t + 1) * P
                dve.tensor_tensor_reduce(out=m.S[h % 2][:, SOFF[t]:SOFF[t] + n], in0=score_at[t],
                                         in1=mask[:, SEQ - n:SEQ], scale=1.0, scalar=LOWEST, op0=ALU.add,
                                         op1=ALU.max, accum_out=m.nmax[h % 2][:, t:t + 1])
            dve.drain()
            dve.tensor_scalar(m.nmax[h % 2][:], m.nmax[h % 2][:], -1.0, None, ALU.mult).then_inc(shifted, 1)

        def finish(h):
            dve.wait_ge(out_done, h + 1)
            dve.reciprocal(m.rinv[:], m.psum[h % 4][:])
            dve.drain()
            full = [P, NT, HEAD]
            dve.tensor_tensor(m.o[:].rearrange("p (t d) -> p t d", d=HEAD),
                              PS[:, 6 + h % 2, 0:NT * HEAD].rearrange("p (t d) -> p t d", d=HEAD),
                              m.rinv[:].unsqueeze(2).to_broadcast(full), ALU.mult)
            dve.drain()
            dve.tensor_tensor(m.mix[:, :, column + h * HEAD:column + (h + 1) * HEAD],
                              m.o[:].rearrange("p (t d) -> p t d", d=HEAD),
                              m.G[:, :, h * HEAD:(h + 1) * HEAD], ALU.mult).then_inc(mixed, 1)

        for ready in qk_ready:
            dve.wait_ge(*ready)
        add_mask(0)
        dve.wait_ge(*g_ready)
        for h in range(NH):
            if h + 1 < NH:
                add_mask(h + 1)
            dve.wait_ge(turned, h + 1)
            if h >= 2:
                dve.wait_ge(out_done, h - 1)
            dve.tensor_copy(m.PT[h % 2][:, 512:1280], PS[:, 4:6, :].rearrange("p a n -> p (a n)")[:, 0:768]).then_inc(pt_dve, 1)
            if h >= 1:
                finish(h - 1)
        finish(NH - 1)

    @block.tensor
    def _(pe):
        def scores(h):
            if h >= 1:
                pe.wait_ge(shifted, h)
            for t in range(NT):
                i = pe.matmul(score_at[t], m.QT[0:rows, h, t * P:(t + 1) * P], m.KT[0:rows, h, 0:(t + 1) * P],
                              start=True, stop=True)
            i.then_inc(scored, 1)

        def turn(h):
            pe.wait_ge(exped, NT * (h + 1))
            if h >= 1:
                pe.wait_ge(pt_act, h)
                pe.wait_ge(pt_dve, h)
            flat = PS[:, 3:6, :].rearrange("p a n -> p (a n)")
            for j in range(NT):
                for t in range(j, NT):
                    a = PTOFF[j] + (t - j) * P
                    i = pe.transpose(flat[:, a:a + P], m.S[h % 2][:, SOFF[t] + j * P:SOFF[t] + (j + 1) * P], m.ident)
            i.then_inc(turned, 1)

        def outputs(h):
            pe.wait_ge(pt_act, h + 1)
            pe.wait_ge(pt_dve, h + 1)
            if h >= 2:
                pe.wait_ge(mixed, h - 1)
            for t in range(NT):
                for j in range(t + 1):
                    a = PTOFF[j] + (t - j) * P
                    i = pe.matmul(PS[:, 6 + h % 2, t * HEAD:(t + 1) * HEAD], m.PT[h % 2][:, a:a + P],
                                  m.V[:, j, h * HEAD:(h + 1) * HEAD], start=j == 0, stop=j == t)
            i.then_inc(out_done, 1)

        for ready in qk_ready:
            pe.wait_ge(*ready)
        scores(0)
        for h in range(NH):
            if h + 1 < NH:
                scores(h + 1)
            if h == 0:
                pe.wait_ge(*g_ready)
            turn(h)
            if h >= 1:
                outputs(h - 1)
        outputs(NH - 1)

    return mixed, NH


def gate_phase(block, sem, PS, w, g0, u, X, m, made):
    squared = sem("gate_squared")
    sig_done, banks_free, sig_free = sem("gate_sig"), sem("gate_banks"), sem("gate_sig_free")

    @block.sync
    def _(sp):
        w.load(sp, g0 + 2)
        w.load(sp, g0 + 3)

    @block.scalar
    def _(act):
        for b in range(4):
            w.split_hi(act, g0 + b + 1)
            w.wait_used(act, g0 + b)
            if b >= 2:
                act.wait_ge(sig_free, b - 1)
            act.activation(m.sig[b % 2][:], PS[:, 4 * (b % 2):4 * (b % 2) + 4, 0:256], ACT.Sigmoid).then_inc(sig_done, 1)
            act.wait_ge(sig_done, b + 1)
            act.sem_inc(banks_free, 1)
            if b == 3:
                for part, (cols, n) in enumerate(((slice(0, 768), 3), (slice(768, D), 4))):
                    act.wait_ge(sig_free, n)
                    for t in range(NT):
                        act.activation(m.mix[:, t, cols], X[:, t, cols], ACT.Square,
                                       accum_out=m.part_sums[:, part * NT + t:part * NT + t + 1]).then_inc(squared, 1)

    @block.vector
    def _(dve):
        for b in range(4):
            w.split_lo(dve, g0 + b + 1)
            dve.wait_ge(sig_done, b + 1)
            cols = slice(b * 256, (b + 1) * 256)
            dve.tensor_tensor(m.sig[b % 2][:], m.sig[b % 2][:], m.ple[:, :, cols], ALU.mult)
            dve.drain()
            dve.tensor_tensor(X[:, :, cols], X[:, :, cols], m.sig[b % 2][:], ALU.add).then_inc(sig_free, 1)
        dve.wait_ge(squared, 2 * NT)
        dve.tensor_tensor(m.sums[:, 0:NT], m.part_sums[:, 0:NT], m.part_sums[:, NT:2 * NT], ALU.add)

    @block.tensor
    def _(pe):
        pe.sem_inc(banks_free, 2)
        with pe.Fori(0, 2) as i:
            for j in range(2):
                w.ready(pe, g0 + j, i, 2)
                pe.wait_ge(banks_free, plus(i, 2, 1 + j))
                block_to_tokens(pe, w, g0 + j, u, lambda t, h: PS[:, 4 * j + t, 0:256], made=made if j == 0 else None)


class Box:
    pass


def first_model(nc, PS, X, x, stream_mem, uh, ul, free, ins, layer_count=DEPTH):
    (w1, consts, positions, norm_gains, qk_gains, fa_w, fa_b, pT) = ins
    mem = Memory(nc)
    mem.top = free
    m = Box()
    xn = mem.put("xn1", [P, NT, D])
    m.mix = xn
    table = mem.put("table1", [P, P + 3 * SEQ + HALF])
    m.ident = table[:, 0:P]
    mask_fox, mask_dil = table[:, P:P + SEQ], table[:, P + SEQ:P + 2 * SEQ]
    m.upto = table[:, P + 2 * SEQ:P + 3 * SEQ]
    inv_freq = table[:, P + 3 * SEQ:]
    gains = mem.put("norm_gains1", [P, 2 * KD])
    m.qk_gain = mem.put("qk_gain", [P, 4 * HEAD])
    m.cos, m.sin = mem.put("cos", [P, NT, HALF]), mem.put("sin", [P, NT, HALF])
    m.fa_raw, m.fa_hi, m.fa_lo = mem.put("fa_raw", [P, KD * NH]), mem.put("fa_hi", [P, KD * NH], F32R), mem.put("fa_lo", [P, KD * NH], F32R)
    m.fa_bias = mem.put("fa_bias", [P, NH])
    m.fa_y, m.fa_e, m.lf = (mem.put(n, [P, NT * NH]) for n in ("fa_y", "fa_e", "lf"))
    m.sums, m.rstd, m.scratch = (mem.put(n, [P, NT * NH]) for n in ("sums", "rstd", "scratch"))
    m.nmax = [mem.put(f"nmax{i}", [P, NT]) for i in range(2)]
    m.psum = [mem.put(f"psum{i}", [P, NT]) for i in range(4)]
    m.rinv = mem.put("rinv", [P, NT])
    m.part_sums = mem.put("part_sums", [P, 2 * NT])
    m.o = mem.put("o1", [P, NT * HEAD])
    p_hi, p_lo = mem.put("p_hi", [P, 2, SEQ], F32R), mem.put("p_lo", [P, 2, SEQ], F32R)
    at = mem.top
    m.QT = mem.put("QT", [HEAD + 2, NH, SEQ])
    m.KT = mem.put("KT", [HEAD + 2, NH, SEQ])
    m.V, m.G = mem.put("V1", [P, NT, NH * HEAD]), mem.put("G1", [P, NT, NH * HEAD])
    at2 = mem.top
    m.S = [mem.put(f"S{i}", [P, 1280]) for i in range(2)]
    m.PT = [mem.put(f"PT{i}", [P, 1280]) for i in range(2)]
    end = mem.top
    mem.top = at2
    m.zn = [mem.put(f"zn{i}", [P, NT * NH * HEAD]) for i in range(2)]
    m.cum, m.ncum = mem.put("cum", [NH, SEQ]), mem.put("ncum", [NH, SEQ])
    end = max(end, mem.top)
    m.rot = []
    for i in range(4):
        m.rot.append(mem.put(f"rot{i}", [P, NT, NH, HALF]))
    end = max(end, mem.top)
    assert end <= nc.sbuf_usable_end, end
    mem.top = at
    m.ple = mem.put("ple", [P, NT, D])
    m.sig = [mem.put(f"sig{i}", [P, NT, 256]) for i in range(2)]
    p_raw = mem.put("p_raw", [P, 2, SEQ])
    mem.top = at
    pos, posf, ang, turns, red, over = (mem.put(n, [P, NT], I32) if n == "pos" else mem.put(n, [P, NT] if n == "posf" else [P, NT, HALF])
                                        for n in ("pos", "posf", "ang", "turns", "red", "over"))

    with ExitStack() as ctx:
        sem = Semaphores(nc, ctx)
        arrived, angles, x_arrived = sem("tables_arrived"), sem("angles_ready"), sem("x_arrived")
        with nc.Block(no_gpsimd_drain=True) as block:
            @block.sync
            def _(sp):
                sp.dma_start(table[:], consts).then_inc(arrived, 16)
                sp.dma_start(pos[:], positions.rearrange("b (t p) -> p (b t)", p=P), allow_slow_non_contiguous=True).then_inc(arrived, 16)
                sp.dma_start(X[:], x.rearrange("b (t p) n -> p (b t) n", p=P)).then_inc(x_arrived, 16)

            @block.vector
            def _(dve):
                C1, C2 = 6.28125, 0.0019350051879882812
                C3 = 2 * np.pi - C1 - C2
                dve.wait_ge(arrived, 32)
                dve.tensor_copy(posf[:], pos[:])
                dve.drain()
                dve.tensor_tensor(ang[:], posf[:].unsqueeze(2).to_broadcast([P, NT, HALF]),
                                  inv_freq.unsqueeze(1).to_broadcast([P, NT, HALF]), ALU.mult)
                dve.drain()
                dve.tensor_scalar(turns[:], ang[:], float(1 / (2 * np.pi)), 12582912.0, ALU.mult, ALU.add)
                dve.drain()
                dve.tensor_scalar(turns[:], turns[:], 12582912.0, None, ALU.subtract)
                dve.drain()
                for c in (C1, C2, C3):
                    dve.scalar_tensor_tensor(ang[:], turns[:], -float(c), ang[:], ALU.mult, ALU.add)
                    dve.drain()
                dve.tensor_scalar(red[:], ang[:], float(np.pi / 2), None, ALU.add)
                dve.drain()
                dve.tensor_scalar(over[:], red[:], float(np.pi), -2 * float(np.pi), ALU.is_gt, ALU.mult)
                dve.drain()
                dve.tensor_tensor(red[:], red[:], over[:], ALU.add)
                dve.drain()
                for a in (red, ang):
                    dve.tensor_scalar(a[:], a[:], 3.1415925, -3.1415925, ALU.min, ALU.max).then_inc(angles, 1)

            @block.scalar
            def _(act):
                act.wait_ge(angles, 2)
                act.activation(m.cos[:], red[:], ACT.Sin)
                act.activation(m.sin[:], ang[:], ACT.Sin)
                act.wait_ge(x_arrived, 16)
                for t in range(NT):
                    act.activation(m.mix[:, t, :], X[:, t, :], ACT.Square, accum_out=m.sums[:, t:t + 1])
        nc.all_engine_barrier(sems_to_clear=sem.span())

    with ExitStack() as ctx:
        sem = Semaphores(nc, ctx)
        stream_sems = sem
        with nc.Fori(0, layer_count) as layer:
            w = WeightStream(stream_sems, *stream_mem, w1, NB1, layer)
            small = sem("small_arrived")
            p_split, p_done = sem("p_split"), sem("p_done")

            def start(kind, eng):
                one = bass.ds(layer, 1)
                if kind == "sync":
                    w.load(eng, 0)
                    eng.dma_start(gains[:], norm_gains[one].rearrange("o p n -> p (o n)")).then_inc(small, 16)
                    w.load(eng, 1)
                    eng.dma_start(m.qk_gain[:], qk_gains[one].rearrange("o p n -> p (o n)")).then_inc(small, 16)
                    eng.dma_start(m.fa_raw[:], fa_w[one].rearrange("o p n -> p (o n)")).then_inc(small, 16)
                    eng.dma_start(m.fa_bias[:], fa_b[one].rearrange("o p n -> p (o n)")).then_inc(small, 16)
                    eng.dma_start(p_raw[:].rearrange("p k n -> p (k n)"), pT[one].rearrange("o p n -> p (o n)")).then_inc(small, 16)
                if kind == "scalar":
                    w.split_hi(eng, 0)
                    eng.wait_ge(small, 80)
                if kind == "vector":
                    w.split_lo(eng, 0)

            def start_late(kind, eng):
                if kind == "scalar":
                    eng.activation(p_hi[:], p_raw[:], ACT.Copy).then_inc(p_split, 1)
                    eng.activation(m.fa_hi[:], m.fa_raw[:], ACT.Copy).then_inc(p_split, 1)
                if kind == "vector":
                    eng.wait_ge(p_split, 2)
                    eng.tensor_tensor(p_lo[:], p_raw[:], p_hi[:], ALU.subtract).then_inc(p_done, 1)
                    eng.tensor_tensor(m.fa_lo[:], m.fa_raw[:], m.fa_hi[:], ALU.subtract).then_inc(p_done, 1)

            u = (uh, ul)
            ple_copied = sem("ple_copied")

            def ple(kind, eng):
                g = 20
                if kind == "scalar":
                    w.split_hi(eng, g + 1)
                    w.wait_used(eng, g)
                    for t in range(NT):
                        eng.activation(m.ple[:, t, :].rearrange("p (a n) -> p a n", n=512), PS[:, 2 * t:2 * t + 2, :],
                                       ACT.Copy).then_inc(ple_copied, 1)
                if kind == "vector":
                    w.split_lo(eng, g + 1)
                if kind == "tensor":
                    w.ready(eng, g)
                    block_to_tokens(eng, w, g, (p_hi, p_lo), lambda t, h: PS[:, 2 * t + h, :], kd=2, halves=2)
                    eng.wait_ge(ple_copied, NT)

            with nc.Block(no_gpsimd_drain=True) as block:
                made = to_features_phase(block, sem, "norm1", PS, m.ident, xn, NT, uh, ul, gain=lambda k: gains[:, k:k + 1],
                                         norm=(X, m.sums, m.rstd, m.scratch), extra=start, late=start_late, squares="made")
                ready = projection_phase_1(block, sem, "fox", PS, w, 0, u, m, False, made, (p_done, 2))
                mixed = attention_phase_1(block, sem, "foxatt", PS, m, HEAD + 2, mask_fox, 0, *ready)
                ready = projection_phase_1(block, sem, "dil", PS, w, 8, u, m, True, mixed=mixed)
                mixed = attention_phase_1(block, sem, "dilatt", PS, m, HEAD, mask_dil, NH * HEAD, *ready)
                made = to_features_phase(block, sem, "mix1", PS, m.ident, m.mix, NT, uh, ul, src_done=mixed)
                sums = residual_phase(block, sem, "out1", PS, w, 16, u, X, m, 1, made)
                made = to_features_phase(block, sem, "norm1g", PS, m.ident, xn, NT, uh, ul, squares=sums, extra=ple,
                                         gain=lambda k: gains[:, KD + k:KD + k + 1], norm=(X, m.sums, m.rstd, m.scratch))
                gate_phase(block, sem, PS, w, 21, u, X, m, made)
            nc.all_engine_barrier(sems_to_clear=sem.span())


def ffn_phase(block, sem, name, PS, w, g0, u, X, f, m, made):
    silu_done, gated, h_hi, h_lo = (sem(f"{name}_{n}") for n in ("silu", "gated", "hhi", "hlo"))
    summed, free, squared = sem(f"{name}_summed"), sem(f"{name}_free"), sem(f"{name}_squared")
    LOOPS = (NCHUNK - 1) // 2
    END = g0 + 3 * NCHUNK

    def at(i, c, per=1, base=0):
        return plus(i, 2 * per, per * (1 + c) + base)

    @block.sync
    def _(sp):
        w.load(sp, g0 + 2)
        w.load(sp, g0 + 3)
        with sp.Fori(0, LOOPS - 1) as i:
            for j in range(6):
                w.load(sp, g0 + 4 + j, i, 6)
        for g in range(g0 + 4 + 6 * (LOOPS - 1), END + 2):
            w.load(sp, g)

    @block.scalar
    def _(act):
        w.split_hi(act, g0 + 1)
        w.wait_used(act, g0)
        act.activation(f.silu[:], PS[:, 0:2, :], ACT.Silu).then_inc(silu_done, 1)
        w.split_hi(act, g0 + 2)
        act.wait_ge(gated, 1)
        act.activation(f.h_hi[:], f.h[:], ACT.Copy).then_inc(h_hi, 1)
        with act.Fori(0, LOOPS) as i:
            for c in range(2):
                g = g0 + 2 + 3 * c
                w.split_hi(act, g + 1, i, 6)
                w.wait_used(act, g, i, 6)
                act.activation(f.silu[:], PS[:, 0:2, :], ACT.Silu).then_inc(silu_done, 1)
                w.split_hi(act, g + 2, i, 6)
                w.split_hi(act, g + 3, i, 6)
                act.wait_ge(gated, at(i, c, 1, 1))
                act.activation(f.h_hi[:], f.h[:], ACT.Copy).then_inc(h_hi, 1)
        w.split_hi(act, END)
        for t in range(NT):
            act.wait_ge(free, 2 + NT * (NCHUNK - 1) + t + 1)
            act.activation(m.mix[:, t, :], X[:, t, :], ACT.Square, accum_out=m.sums[:, t:t + 1]).then_inc(squared, 1)

    @block.vector
    def _(dve):
        def gate(g, i, step, n):
            dve.wait_ge(silu_done, n)
            w.wait_used(dve, g, i, step)
            dve.tensor_tensor(f.h[:], PS[:, 2:4, :], f.silu[:], ALU.mult).then_inc(gated, 1)
            dve.wait_ge(h_hi, n)
            dve.tensor_tensor(f.h_lo[:], f.h[:], f.h_hi[:], ALU.subtract).then_inc(h_lo, 1)

        def add(g, i, c, step, tiles):
            for t in tiles:
                if t < NT - 1:
                    dve.wait_ge(summed, at(i, c, NT - 1, t + 2 - NT))
                else:
                    w.wait_used(dve, g, i, step)
                b = 4 + 2 * (t % 2)
                x = X[:, t, :].rearrange("p (a n) -> p a n", n=512)
                dve.scalar_tensor_tensor(x, PS[:, b:b + 2, :], 0.5, x, ALU.mult, ALU.add).then_inc(free, 1)

        dve.sem_inc(free, 2)
        w.split_lo(dve, g0 + 1)
        w.split_lo(dve, g0 + 2)
        gate(g0 + 1, None, 0, 1)
        with dve.Fori(0, LOOPS) as i:
            for c in range(2):
                g = g0 + 2 + 3 * c
                w.split_lo(dve, g + 1, i, 6)
                add(g + 1, i, c, 6, (0, 1))
                w.split_lo(dve, g + 2, i, 6)
                add(g + 1, i, c, 6, (2, 3))
                w.split_lo(dve, g + 3, i, 6)
                gate(g + 2, i, 6, at(i, c, 1, 1))
        w.split_lo(dve, END)
        add(END - 1, None, NCHUNK - 1, 0, range(NT))

    @block.tensor
    def _(pe):
        def up(g, bank, i, step, made=None):
            w.ready(pe, g, i, step)
            block_to_features(pe, w, g, u, lambda t: PS[:, bank + t, :], made)

        def down(g, i, c, step):
            w.ready(pe, g, i, step)
            pe.wait_ge(h_lo, at(i, c))
            for t in range(NT):
                pe.wait_ge(free, at(i, c, NT, t + 1 - NT))
                for half in range(2):
                    for k in range(2):
                        a = k * D + half * 512
                        last = split_products(
                            pe, PS[:, 4 + 2 * (t % 2) + half, :], [x[:, k, t * P:(t + 1) * P] for x in (f.h_hi, f.h_lo)],
                            (w.hi[g % 2][:, a:a + 512], w.lo[g % 2][:, a:a + 512]), k == 0, k == 1)
                last.then_inc(summed if t < NT - 1 else w.used, 1)

        up(g0, 0, None, 0, made)
        up(g0 + 1, 2, None, 0)
        with pe.Fori(0, LOOPS) as i:
            for c in range(2):
                g = g0 + 2 + 3 * c
                pe.wait_ge(silu_done, at(i, c))
                up(g, 0, i, 6)
                down(g + 1, i, c, 6)
                pe.wait_ge(gated, at(i, c))
                up(g + 2, 2, i, 6)
        down(END - 1, None, NCHUNK - 1, 0)

    return squared, NT


def projection_phase_2(block, sem, PS, w, g0, u, m, one, pool_in, row_in, flag, made):
    s = Box()
    s.small, s.rmax, s.rexp, s.rsum, s.rln = (sem(f"mix2_{n}") for n in ("small", "rmax", "rexp", "rsum", "rln"))
    s.zread, s.zmin, s.ln1, s.ln2, s.diff = (sem(f"mix2_{n}") for n in ("zread", "zmin", "ln1", "ln2", "diff"))
    s.vread, s.uread, s.silu = (sem(f"mix2_{n}") for n in ("vread", "uread", "silu"))

    @block.sync
    def _(sp):
        w.load(sp, g0 + 2)
        made(sp, KD - 1, 0)
        sp.dma_start(m.lb[:], row_in[2]).then_inc(s.small, 16)
        sp.dma_start(m.flag[:], flag[one].rearrange("o p n -> p (o n)")).then_inc(s.small, 16)
        sp.dma_start(m.hnorm[:], row_in[0][one].rearrange("o p n -> p (o n)")).then_inc(s.small, 16)
        sp.dma_start(m.pscale[:], row_in[1][one].rearrange("o p n -> p (o n)")).then_inc(s.small, 16)
        sp.dma_start(m.bands[:], pool_in[0]).then_inc(s.small, 16)
        sp.dma_start(m.pool_w[:], pool_in[1][one].rearrange("o p n -> p (o n)")).then_inc(s.small, 16)
        for j in range(9):
            w.load(sp, g0 + 3 + j)

    zf = PS[:, 0:4, :]

    @block.scalar
    def _(act):
        w.split_hi(act, g0 + 1)
        act.wait_ge(s.rmax, 1)
        act.activation(m.e[:], m.lb[:], ACT.Exp).then_inc(s.rexp, 1)
        act.wait_ge(s.rsum, 1)
        act.activation(m.lnsum[:], m.esum[:], ACT.Ln).then_inc(s.rln, 1)
        w.split_hi(act, g0 + 2)
        w.wait_used(act, g0 + 1)
        act.activation(m.t1[:], zf, ACT.Abs).then_inc(s.zread, 1)
        act.activation(m.K[:], zf, ACT.Sigmoid, scale=-1.0).then_inc(s.zread, 1)
        w.split_hi(act, g0 + 3)
        act.wait_ge(s.zread, 2)
        act.activation(m.t1[:], m.t1[:], ACT.Exp, scale=-1.0)
        act.drain()
        act.activation(m.t1[:], m.t1[:], ACT.Ln, bias=1.0).then_inc(s.ln1, 1)
        w.split_hi(act, g0 + 4)
        w.wait_used(act, g0 + 3)
        act.activation(m.V[:], PS[:, 4:8, :], ACT.Copy).then_inc(s.vread, 1)
        act.wait_ge(s.diff, 1)
        act.activation(m.t2[:], m.t2[:], ACT.Abs)
        act.drain()
        act.activation(m.t2[:], m.t2[:], ACT.Exp, scale=-1.0)
        act.drain()
        act.activation(m.t2[:], m.t2[:], ACT.Ln, bias=1.0).then_inc(s.ln2, 1)
        w.split_hi(act, g0 + 5)
        w.split_hi(act, g0 + 6)
        w.wait_used(act, g0 + 5)
        act.activation(m.U[:], PS[:, 0:4, :], ACT.Copy).then_inc(s.uread, 1)
        w.split_hi(act, g0 + 7)
        w.split_hi(act, g0 + 8)
        w.wait_used(act, g0 + 7)
        act.activation(m.Q[:], PS[:, 4:8, :], ACT.Copy)
        w.split_hi(act, g0 + 9)
        w.split_hi(act, g0 + 10)
        w.wait_used(act, g0 + 9)
        act.activation(m.G[:], PS[:, 0:4, :], ACT.Silu).then_inc(s.silu, 1)

    @block.vector
    def _(dve):
        l0, l1 = m.lb[:, 0:DA], m.lb[:, DA:2 * DA]
        e0, e1 = m.e[:, 0:DA], m.e[:, DA:2 * DA]
        full = [P, NT, DA]
        w.split_lo(dve, g0 + 1)
        dve.wait_ge(s.small, 96)
        dve.tensor_tensor(m.esum[:], l0, l1, ALU.max)
        dve.drain()
        for part in (l0, l1):
            dve.tensor_tensor(part, part, m.esum[:], ALU.subtract)
        dve.drain()
        dve.sem_inc(s.rmax, 1)
        dve.wait_ge(s.rexp, 1)
        dve.tensor_tensor(m.esum[:], e0, e1, ALU.add).then_inc(s.rsum, 1)
        dve.wait_ge(s.rsum, 1)
        w.split_lo(dve, g0 + 2)
        dve.wait_ge(s.rln, 1)
        for part in (l0, l1):
            dve.tensor_tensor(part, part, m.lnsum[:], ALU.subtract)
        dve.reciprocal(m.esum[:], m.esum[:])
        dve.drain()
        for part in (e0, e1):
            dve.tensor_tensor(part, part, m.esum[:], ALU.mult)
        dve.drain()
        dve.tensor_tensor(m.esum[:], e0, e1, ALU.add)
        dve.drain()
        dve.tensor_tensor(m.esum[:], m.esum[:], e0, ALU.subtract)
        on, floor = m.flag[:, 0:1], m.flag[:, 1:2]
        dve.tensor_scalar(m.ln1m[:], l0, on, None, ALU.mult)
        dve.tensor_scalar(m.lnlb[:], l1, on, floor, ALU.mult, ALU.add)
        dve.drain()
        dve.tensor_scalar(m.one_less[:], m.esum[:], on, -1.0, ALU.mult, ALU.mult)
        dve.drain()
        dve.tensor_scalar(m.one_less[:], m.one_less[:], 1.0, None, ALU.add)
        dve.wait_ge(s.zread, 2)
        dve.tensor_scalar(m.t2[:], zf, 0.0, None, ALU.min).then_inc(s.zmin, 1)
        w.split_lo(dve, g0 + 3)
        dve.drain()
        dve.wait_ge(s.ln1, 1)
        dve.tensor_tensor(m.t2[:], m.t2[:], m.t1[:], ALU.subtract)
        dve.drain()
        rows = [a[:].unsqueeze(1).to_broadcast(full) for a in (m.ln1m, m.lnlb, m.one_less)]
        dve.tensor_tensor(m.t2[:], m.t2[:], rows[0], ALU.add)
        dve.drain()
        dve.tensor_tensor(m.LF[:], m.t2[:], rows[1], ALU.max)
        dve.drain()
        dve.tensor_tensor(m.t2[:], m.t2[:], rows[1], ALU.subtract).then_inc(s.diff, 1)
        w.split_lo(dve, g0 + 4)
        dve.tensor_tensor(m.K[:], m.K[:], rows[2], ALU.mult)
        w.split_lo(dve, g0 + 5)
        dve.wait_ge(s.ln2, 1)
        dve.drain()
        dve.tensor_tensor(m.LF[:], m.LF[:], m.t2[:], ALU.add)
        for j in (6, 7, 8, 9, 10):
            w.split_lo(dve, g0 + j)
        dve.wait_ge(s.silu, 1)
        dve.drain()
        dve.tensor_tensor(m.G[:], m.G[:], m.hnorm[:].unsqueeze(1).to_broadcast(full), ALU.mult)

    @block.tensor
    def _(pe):
        def project(part):
            for half in range(2):
                g = g0 + 2 * part + half
                w.ready(pe, g)
                block_to_tokens(pe, w, g, u, lambda t, h: PS[:, 4 * (part % 2) + t, half * 256:half * 256 + 256],
                                made=made if part == half == 0 else None)

        project(0)
        project(1)
        pe.wait_ge(s.zread, 2)
        pe.wait_ge(s.zmin, 1)
        project(2)
        pe.wait_ge(s.vread, 1)
        for half in range(2):
            g = g0 + 6 + half
            w.ready(pe, g)
            block_to_features(pe, w, g, u, lambda t: PS[:, 4 + 2 * half + t, :])
        pe.wait_ge(s.uread, 1)
        project(4)


def pool_and_states_phase(block, sem, PS, m):
    pooled, pool_copied, mapped, mapped_read = (sem(f"pool_{n}") for n in ("pooled", "copied", "mapped", "read"))
    suffix, suffix_exp, kp, dec, dec_exp, outer = (sem(f"state_{n}") for n in ("suffix", "sexp", "kp", "dec", "dexp", "outer"))

    @block.scalar
    def _(act):
        for g in range(4):
            act.wait_ge(pooled, g + 1)
            act.activation(m.pT[:, g, :], PS[:, g, :], ACT.Copy).then_inc(pool_copied, 1)
        for c in range(NT):
            act.wait_ge(suffix, c + 1)
            act.activation(m.Kp[:, c, :], PS[:, 4 + c, :], ACT.Exp).then_inc(suffix_exp, 1)
        act.wait_ge(dec, 1)
        act.activation(m.dec[:], PS[:, 7, 0:HH * 2], ACT.Exp).then_inc(dec_exp, 1)

    @block.vector
    def _(dve):
        for c in range(NT - 1):
            dve.wait_ge(suffix_exp, c + 1)
            dve.tensor_tensor(m.Kp[:, c, :], m.Kp[:, c, :], m.K[:, c, :], ALU.mult).then_inc(kp, 1)
        for g in range(4):
            dve.wait_ge(mapped, g + 1)
            dve.tensor_tensor(m.mix[:, :, DA + g * P:DA + (g + 1) * P], PS[:, g, :].rearrange("p (t n) -> p t n", n=P),
                              m.pscale[:, g * P:(g + 1) * P].unsqueeze(1).to_broadcast([P, NT, P]), ALU.mult)
        dve.wait_ge(outer, 1)
        dve.wait_ge(dec_exp, 1)
        dve.tensor_copy(m.St[:, 0, :], PS[:, 4, :])
        for c in (1, 2):
            dve.drain()
            for h in range(HH):
                cols = slice(h * P, (h + 1) * P)
                d = (c - 1) * HH + h
                dve.scalar_tensor_tensor(m.St[:, c, cols], m.St[:, c - 1, cols], m.dec[:, d:d + 1],
                                         PS[:, 4 + c, cols], ALU.mult, ALU.add)

    @block.tensor
    def _(pe):
        for g in range(4):
            for t in range(NT):
                out = PS[:, g, t * P:(t + 1) * P]
                i = pe.matmul(out, m.U[:, t, g * P:(g + 1) * P], m.band(g, 1 if t else 0), start=True, stop=t == 0)
                if t:
                    i = pe.matmul(out, m.U[:, t - 1, g * P:(g + 1) * P], m.band(g, 2), start=False, stop=True)
            i.then_inc(pooled, 1)
        for c in range(NT):
            pe.matmul(PS[:, 4 + c, :], m.after, m.LF[:, c, :], start=True, stop=True).then_inc(suffix, 1)
        for g in range(4):
            pe.wait_ge(pool_copied, g + 1)
            for t in range(NT):
                i = pe.matmul(PS[:, g, t * P:(t + 1) * P], m.pT[:, g, t * P:(t + 1) * P], m.pool_w[:, g * P:(g + 1) * P],
                              start=True, stop=True)
            i.then_inc(mapped, 1)
        pe.wait_ge(suffix_exp, 4)
        for c in (1, 2):
            for h in range(HH):
                d = (c - 1) * HH + h
                i = pe.matmul(PS[:, 7, d:d + 1], m.LF[:, c, h * P:(h + 1) * P], m.level[:, LEVELS * P + P - 1:LEVELS * P + P],
                              start=True, stop=True)
        i.then_inc(dec, 1)
        pe.wait_ge(kp, 3)
        for c in range(NT - 1):
            for h in range(HH):
                cols = slice(h * P, (h + 1) * P)
                i = pe.matmul(PS[:, 4 + c, cols], m.Kp[:, c, cols], m.V[:, c, cols], start=True, stop=True)
        i.then_inc(outer, 1)


def recurrence_phase(block, sem, PS, m):
    k_turned, k_copied, summed, exped, weighed, scored, kept, out_done, out_sq, out_read = (
        sem(f"rec_{n}") for n in ("kturned", "kcopied", "summed", "exped", "weighed", "scored", "kept", "out", "outsq", "outread"))
    zeroed, mean_ready, rstd_ready = sem("rec_zeroed"), sem("rec_mean"), sem("rec_rstd")
    UNITS = 5

    def right(ap, n, side=1):
        mm = P >> (n + 1)
        return ap.rearrange("p (b two m) -> p b two m", two=2, m=mm)[:, :, side, :]

    @block.gpsimd
    def _(pool):
        for i in range(2):
            pool.memset(m.AT[i][:], 0.0).then_inc(zeroed, 1)

    @block.scalar
    def _(act):
        def exps(h):
            act.wait_ge(k_turned, h + 1)
            if h >= 2:
                act.wait_ge(out_done, h - 1)
            act.activation(m.Kf[h % 2][:], PS[:, 4, :], ACT.Copy).then_inc(k_copied, 1)
            for c in range(NT):
                act.wait_ge(summed, NT * h + c + 1)
                b = 2 * (c % 2)
                act.activation(m.E[h % 2][:, :, c * P:(c + 1) * P],
                               PS[:, b:b + 2, :].rearrange("p a (l t) -> p (a l) t", t=P), ACT.Exp).then_inc(exped, 1)

        exps(0)
        exps(1)
        for h in range(HH):
            act.wait_ge(out_done, h + 1)
            act.activation(m.mix[:, :, h * P:(h + 1) * P], PS[:, 7, :].rearrange("p (c v) -> p c v", v=P), ACT.Square)\
               .then_inc(out_sq, 1)
            if h + 2 < HH:
                exps(h + 2)
        act.wait_ge(mean_ready, 1)
        act.activation(m.orstd[:], m.orstd[:], ACT.Sqrt).then_inc(rstd_ready, 1)

    @block.vector
    def _(dve):
        def weigh(h):
            dve.wait_ge(k_copied, h + 1)
            dve.wait_ge(exped, NT * (h + 1))
            E = m.E[h % 2]
            for n in range(LEVELS):
                for side, src in ((1, m.Q[:, h, :]), (0, m.Kf[h % 2][:])):
                    e = right(E[:, n, :], n, side)
                    dve.tensor_tensor(e, e, right(src, n, side), ALU.mult)
            dve.tensor_tensor(E[:, LEVELS, :], E[:, LEVELS, :], m.Q[:, h, :], ALU.mult)
            dve.drain()
            dve.sem_inc(weighed, 1)

        def keep(h):
            if h >= 2:
                dve.wait_ge(out_done, h - 1)
            AT = m.AT[h % 2]
            for unit in range(UNITS):
                dve.wait_ge(scored, UNITS * h + unit + 1)
                b = 5 + unit % 2
                for n in (2 * unit, 2 * unit + 1):
                    if n < LEVELS:
                        mm = P >> (n + 1)
                        a = (n % 2) * 256
                        dve.copy_predicated(right(AT[:].rearrange("p c t -> p (c t)"), n),
                                            m.masks[:, n * 256:(n + 1) * 256].rearrange("p (b m) -> p b m", m=mm),
                                            PS[:, b, a:a + 256].rearrange("p (b m) -> p b m", m=mm))
                        dve.drain()
                if unit == UNITS - 1:
                    dve.copy_predicated(AT[:].rearrange("p c t -> p (c t)"), m.masks[:, LEVELS * 256:], PS[:, b, :])
                dve.drain()
                dve.sem_inc(kept, 1)

        def finish(h):
            dve.wait_ge(out_sq, h + 1)
            dve.tensor_reduce(m.osum[:, h * NT:(h + 1) * NT], m.mix[:, :, h * P:(h + 1) * P], AX.X, ALU.add)
            dve.drain()
            dve.tensor_copy(m.mix[:, :, h * P:(h + 1) * P], PS[:, 7, :].rearrange("p (c v) -> p c v", v=P))
            dve.drain()
            dve.sem_inc(out_read, 1)

        dve.wait_ge(zeroed, 2)
        weigh(0)
        for h in range(HH):
            keep(h)
            if h + 1 < HH:
                weigh(h + 1)
            finish(h)
        dve.tensor_scalar(m.osum[:], m.osum[:], 1.0 / P, EPS, ALU.mult, ALU.add)
        dve.drain()
        dve.reciprocal(m.orstd[:], m.osum[:]).then_inc(mean_ready, 1)
        dve.tensor_tensor(m.mix[:, :, 0:DA], m.mix[:, :, 0:DA], m.G[:], ALU.mult)
        dve.wait_ge(rstd_ready, 1)
        refine(dve, m.osum[:], m.orstd[:], m.scratch[:])
        for c in range(NT):
            part = m.mix[:, c, 0:DA].rearrange("p (h v) -> p h v", v=P)
            rs = m.orstd[:].rearrange("p (h c) -> p h c", c=NT)[:, :, c:c + 1]
            dve.tensor_tensor(part, part, rs.to_broadcast([P, HH, P]), ALU.mult)

    @block.tensor
    def _(pe):
        def sums(h):
            if h:
                pe.wait_ge(k_copied, h)
            for c in range(NT):
                i = pe.transpose(PS[:, 4, c * P:(c + 1) * P], m.K[:, c, h * P:(h + 1) * P], m.ident)
            i.then_inc(k_turned, 1)
            for c in range(NT):
                if NT * h + c >= 2:
                    pe.wait_ge(exped, NT * h + c - 1)
                for half in range(2):
                    i = pe.matmul(PS[:, 2 * (c % 2) + half, :], m.LF[:, c, h * P:(h + 1) * P],
                                  m.level[:, half * 512:half * 512 + 512], start=True, stop=True)
                i.then_inc(summed, 1)

        def scores(h):
            pe.wait_ge(weighed, h + 1)
            W = m.E[h % 2]
            for unit in range(UNITS):
                if UNITS * h + unit >= 2:
                    pe.wait_ge(kept, UNITS * h + unit - 1)
                b = 5 + unit % 2
                if unit < UNITS - 1:
                    for n in (2 * unit, 2 * unit + 1):
                        if n < LEVELS:
                            for c in range(NT):
                                tile = W[:, n, c * P:(c + 1) * P]
                                a = (n % 2) * 256 + c * 64
                                i = pe.matmul(PS[:, b, a:a + 64], tile, right(tile, n), start=True, stop=True)
                else:
                    for c in range(NT):
                        i = pe.matmul(PS[:, b, c * P:(c + 1) * P], m.Kf[h % 2][:, c * P:(c + 1) * P],
                                      m.Q[:, h, c * P:(c + 1) * P], start=True, stop=True)
                i.then_inc(scored, 1)

        def outputs(h):
            pe.wait_ge(kept, UNITS * (h + 1))
            if h:
                pe.wait_ge(out_read, h)
            cols = slice(h * P, (h + 1) * P)
            for c in range(NT):
                out = PS[:, 7, c * P:(c + 1) * P]
                i = pe.matmul(out, m.AT[h % 2][:, c, :], m.V[:, c, cols], start=True, stop=c == 0)
                if c:
                    i = pe.matmul(out, m.E[h % 2][:, LEVELS, c * P:(c + 1) * P], m.St[:, c - 1, cols], start=False, stop=True)
            i.then_inc(out_done, 1)

        sums(0)
        sums(1)
        for h in range(HH):
            scores(h)
            outputs(h)
            if h + 2 < HH:
                sums(h + 2)


def cross_projection_phase(block, sem, PS, w, g0, u, um, m):
    free = sem("cross_free")
    scale = XD ** -0.5

    @block.sync
    def _(sp):
        with sp.Fori(0, 6) as i:
            for j in range(2):
                w.load(sp, g0 + 2 + j, i, 2)

    @block.scalar
    def _(act):
        act.sem_inc(free, 2)
        for part in range(3):
            with act.Fori(0, 2) as i:
                for j in range(2):
                    g = g0 + 4 * part + j
                    w.split_hi(act, g + 1, i, 2)
                    w.wait_used(act, g, i, 2)
                    if part == 0:
                        out, src = m.qT[:, bass.ds(i * 4 + 2 * j, 2), :], PS[:, 2 * j:2 * j + 2, :]
                    elif part == 1:
                        out, src = m.kT[:, bass.ds(i * 4 + 2 * j, 2), :], PS[:, 2 * j:2 * j + 2, 0:NMEM]
                    else:
                        out, src = m.Vm[:, :, bass.ds(i * 512 + j * 256, 256)], PS[:, 2 * j:2 * j + 2, 0:256]
                    act.activation(out, src, ACT.Copy, scale=scale if part == 0 else 1.0).then_inc(free, 1)

    @block.vector
    def _(dve):
        with dve.Fori(0, 6) as i:
            for j in range(2):
                w.split_lo(dve, g0 + 1 + j, i, 2)

    @block.tensor
    def _(pe):
        for part in range(3):
            with pe.Fori(0, 2) as i:
                for j in range(2):
                    g = g0 + 4 * part + j
                    w.ready(pe, g, i, 2)
                    pe.wait_ge(free, plus(i, 2, 4 * part + j + 1))
                    if part < 2:
                        n = (SEQ, NMEM)[part]
                        block_to_features(pe, w, g, (u, um)[part], lambda t: PS[:, 2 * j + t, 0:n])
                    else:
                        block_to_tokens(pe, w, g, um, lambda t, h: PS[:, 2 * j + t, 0:256], nt=MT)


def cross_attention_phase(block, sem, PS, m, uh, ul):
    scored, max_ready, exped, p_ready, turned, pt_act, pt_dve, out_done, hi_done, lo_done = (
        sem(f"cross_{n}") for n in ("scored", "max", "exped", "p", "turned", "ptact", "ptdve", "out", "hi", "lo"))

    @block.scalar
    def _(act):
        def exps(h):
            act.wait_ge(max_ready, h + 1)
            for t in range(NT):
                act.activation(m.Pm[h % 2][:, t, :], PS[:, 2 * (h % 2) + t // 2, (t % 2) * 256:(t % 2) * 256 + 256], ACT.Exp,
                               bias=m.xmax[h % 2][:, t:t + 1], accum_out=m.xsum[h % 2][:, t:t + 1]).then_inc(exped, 1)

        exps(0)
        exps(1)
        for h in range(XH):
            act.wait_ge(turned, h + 1)
            act.activation(m.PTm[h % 2][:, 0, :], PS[:, 4, :], ACT.Copy).then_inc(pt_act, 1)
            if h + 2 < XH:
                exps(h + 2)
            for f in range(2):
                act.wait_ge(out_done, 2 * h + f + 1)
                act.activation(uh[:, 2 * h + f, :], PS[:, 6 + f, :], ACT.Copy).then_inc(hi_done, 1)

    @block.vector
    def _(dve):
        def maxes(h):
            dve.wait_ge(scored, h + 1)
            dve.tensor_reduce(m.xmax[h % 2][:], PS[:, 2 * (h % 2):2 * (h % 2) + 2, :].rearrange("p a (t n) -> p (a t) n", n=NMEM),
                              AX.X, ALU.max)
            dve.drain()
            dve.tensor_scalar(m.xmax[h % 2][:], m.xmax[h % 2][:], -1.0, None, ALU.mult).then_inc(max_ready, 1)

        def divide(h):
            dve.wait_ge(exped, NT * (h + 1))
            dve.reciprocal(m.xsum[h % 2][:], m.xsum[h % 2][:])
            dve.drain()
            dve.tensor_tensor(m.Pm[h % 2][:], m.Pm[h % 2][:], m.xsum[h % 2][:].unsqueeze(2).to_broadcast([P, NT, NMEM]),
                              ALU.mult).then_inc(p_ready, 1)

        maxes(0)
        divide(0)
        maxes(1)
        for h in range(XH):
            if h + 1 < XH:
                divide(h + 1)
            dve.wait_ge(turned, h + 1)
            dve.tensor_copy(m.PTm[h % 2][:, 1, :], PS[:, 5, :]).then_inc(pt_dve, 1)
            if h + 2 < XH:
                maxes(h + 2)
            for f in range(2):
                dve.wait_ge(hi_done, 2 * h + f + 1)
                dve.tensor_tensor(ul[:, 2 * h + f, :], PS[:, 6 + f, :], uh[:, 2 * h + f, :], ALU.subtract).then_inc(lo_done, 1)

    @block.tensor
    def _(pe):
        def scores(h):
            if h >= 2:
                pe.wait_ge(exped, NT * (h - 1))
            for t in range(NT):
                out = PS[:, 2 * (h % 2) + t // 2, (t % 2) * 256:(t % 2) * 256 + 256]
                for f in range(2):
                    i = pe.matmul(out, m.qT[:, 2 * h + f, t * P:(t + 1) * P], m.kT[:, 2 * h + f, :], start=f == 0, stop=f == 1)
            i.then_inc(scored, 1)

        scores(0)
        scores(1)
        for h in range(XH):
            pe.wait_ge(p_ready, h + 1)
            if h:
                pe.wait_ge(pt_act, h)
                pe.wait_ge(pt_dve, h)
            for t in range(NT):
                for k in range(MT):
                    i = pe.transpose(PS[:, 4 + k, t * P:(t + 1) * P], m.Pm[h % 2][:, t, k * P:(k + 1) * P], m.ident)
            i.then_inc(turned, 1)
            if h + 2 < XH:
                scores(h + 2)
            pe.wait_ge(pt_act, h + 1)
            pe.wait_ge(pt_dve, h + 1)
            for f in range(2):
                if h:
                    pe.wait_ge(lo_done, 2 * h - 1 + f)
                for k in range(MT):
                    a = h * XD + f * P
                    i = pe.matmul(PS[:, 6 + f, :], m.Vm[:, k, a:a + P], m.PTm[h % 2][:, k, :], start=k == 0, stop=k == 1)
                i.then_inc(out_done, 1)


def second_model(nc, PS, X, stream_mem, uh, ul, free, ins, out):
    (w2, consts, mask_in, bands_in, flag_in, mem_in, norm_gains, row_in, pool_w, final_gain) = ins
    mem = Memory(nc)
    mem.top = free
    m, f = Box(), Box()
    start_xn = mem.top
    xn = mem.put("xn2", [P, NT, D])
    m.mix = xn
    after_xn = mem.top
    mem.top = start_xn
    m.lb, m.e = mem.put("lb", [P, 2 * DA]), mem.put("lb_exp", [P, 2 * DA])
    m.esum, m.lnsum = mem.put("lb_sum", [P, DA]), mem.put("lb_lnsum", [P, DA])
    m.ln1m, m.lnlb = mem.put("ln_one_less", [P, DA]), mem.put("ln_lb", [P, DA])
    assert mem.top <= after_xn
    mem.top = after_xn
    table = mem.put("table2", [P, P + (LEVELS + 1) * P + P])
    m.ident = table[:, 0:P]
    m.level = table[:, P:P + (LEVELS + 1) * P]
    m.after = table[:, P + (LEVELS + 1) * P:]
    masks = mem.put("masks", [P, (LEVELS + 2) * 256], U8)
    m.masks = masks[:, :]
    gains = mem.put("norm_gains2", [P, 5 * KD])
    m.flag = mem.put("flag", [P, 2])
    m.sums, m.rstd, m.scratch = mem.put("sums2", [P, NT]), mem.put("rstd2", [P, NT]), mem.put("scratch2", [P, HH * NT])
    m.osum, m.orstd, m.dec = mem.put("osum", [P, HH * NT]), mem.put("orstd", [P, HH * NT]), mem.put("dec", [P, HH * 2])
    m.part_sums = mem.put("part_sums2", [P, 2 * NT])
    m.xmax = [mem.put(f"xmax{i}", [P, NT]) for i in range(2)]
    m.xsum = [mem.put(f"xsum{i}", [P, NT]) for i in range(2)]
    shared = mem.top
    m.LF, m.K, m.V, m.G = (mem.put(n, [P, NT, DA]) for n in ("LF", "K2", "V2", "G2"))
    m.Q = mem.put("Q2", [P, HH, SEQ])
    e_at = mem.top
    m.E = [mem.put(f"E{i}", [P, LEVELS + 1, SEQ]) for i in range(2)]
    after_e = mem.top
    m.Kf = [mem.put(f"Kf{i}", [P, SEQ]) for i in range(2)]
    m.AT = [mem.put(f"AT{i}", [P, NT, P]) for i in range(2)]
    m.St = mem.put("St", [P, NT - 1, DA])
    end = mem.top
    mem.top = after_e
    bands = mem.put("bands", [P, 12 * P])
    m.bands = bands
    m.band = lambda g, kind: bands[:, (g * 3 + kind) * P:(g * 3 + kind + 1) * P]
    m.pool_w = mem.put("pool_w", [P, 4 * P])
    end = max(end, mem.top)
    assert mem.top <= after_e + 10 * 1024
    mem.top = e_at
    m.t1, m.t2, m.U = (mem.put(n, [P, NT, DA]) for n in ("t1", "t2", "U2"))
    m.one_less, m.pscale, m.hnorm = (mem.put(n, [P, DA]) for n in ("one_less", "pscale", "hnorm"))
    assert mem.top <= after_e
    mem.top = e_at
    m.pT, m.Kp = mem.put("pT", [P, 4, SEQ]), mem.put("Kp", [P, NT, DA])
    mem.top = shared
    f.silu, f.h = mem.put("silu", [P, 2, SEQ]), mem.put("h", [P, 2, SEQ])
    f.h_hi, f.h_lo = mem.put("h_hi", [P, 2, SEQ], F32R), mem.put("h_lo", [P, 2, SEQ], F32R)
    mem.top = shared
    mh, ml = mem.put("mem_hi", [P, KD, NMEM], F32R), mem.put("mem_lo", [P, KD, NMEM], F32R)
    m.qT, m.kT = mem.put("qT", [P, KD, SEQ]), mem.put("kT", [P, KD, NMEM])
    m.Vm = mem.put("Vm", [P, MT, D])
    m.Pm = [mem.put(f"Pm{i}", [P, NT, NMEM]) for i in range(2)]
    m.PTm = [mem.put(f"PTm{i}", [P, MT, SEQ]) for i in range(2)]
    m.memory = mem.put("memory", [P, MT, D])
    end = max(end, mem.top)
    assert end <= nc.sbuf_usable_end, (end, nc.sbuf_usable_end)
    mem.top = shared
    final_row = mem.put("final_row", [P, D])
    mask_numbers = mem.put("mask_numbers", [P, (LEVELS + 2) * 256])

    u = (uh, ul)
    with ExitStack() as ctx:
        sem = Semaphores(nc, ctx)
        arrived = sem("tables2_arrived")
        with nc.Block(no_gpsimd_drain=True) as block:
            @block.sync
            def _(sp):
                sp.dma_start(table[:], consts).then_inc(arrived, 16)
                sp.dma_start(mask_numbers[:], mask_in).then_inc(arrived, 16)

            @block.vector
            def _(dve):
                dve.wait_ge(arrived, 32)
                dve.tensor_copy(masks[:], mask_numbers[:])

            @block.scalar
            def _(act):
                for t in range(NT):
                    act.activation(xn[:, t, :], X[:, t, :], ACT.Square, accum_out=m.sums[:, t:t + 1])
        nc.all_engine_barrier(sems_to_clear=sem.span())

    with ExitStack() as ctx:
        sem = Semaphores(nc, ctx)
        with nc.Fori(0, DEPTH) as layer:
            w = WeightStream(sem, *stream_mem, w2, NB2, layer)
            small = sem("small2")
            one = bass.ds(layer, 1)

            def start(kind, eng):
                if kind == "sync":
                    w.load(eng, 0)
                    eng.dma_start(gains[:], norm_gains[one].rearrange("o p n -> p (o n)")).then_inc(small, 16)
                    w.load(eng, 1)
                if kind == "scalar":
                    w.split_hi(eng, 0)
                    eng.wait_ge(small, 16)
                if kind == "vector":
                    w.split_lo(eng, 0)

            def load_memory(kind, eng):
                if kind == "sync":
                    eng.dma_start(m.memory[:], mem_in.rearrange("b (t p) n -> p (b t) n", p=P)).then_inc(m.memory_arrived, 16)
                    eng.wait_ge(m.memory_arrived, 16)

            def norm(block, name, n, squares=None, extra=None):
                return to_features_phase(block, sem, name, PS, m.ident, xn, NT, uh, ul, extra=extra, squares=squares,
                                         norm=(X, m.sums, m.rstd, m.scratch),
                                         gain=lambda k: gains[:, n * KD + k:n * KD + k + 1])

            with nc.Block(no_gpsimd_drain=True) as block:
                made = norm(block, "normf1", 0, "made", start)
                sums = ffn_phase(block, sem, "ffn1", PS, w, 0, u, X, f, m, made)
                made = norm(block, "normmix", 1, sums)
                projection_phase_2(block, sem, PS, w, 33, u, m, one, (bands_in, pool_w), row_in, flag_in, made)
            with nc.Block(no_gpsimd_drain=True) as block:
                pool_and_states_phase(block, sem, PS, m)
            with nc.Block(no_gpsimd_drain=True) as block:
                recurrence_phase(block, sem, PS, m)
            m.memory_arrived = sem("memory_arrived")
            with nc.Block(no_gpsimd_drain=True) as block:
                made = to_features_phase(block, sem, "mix2", PS, m.ident, m.mix, NT, uh, ul)
                sums = residual_phase(block, sem, "out2", PS, w, 43, u, X, m, made=made)
                norm(block, "normxa", 2, sums, load_memory)
            with nc.Block(no_gpsimd_drain=True) as block:
                to_features_phase(block, sem, "normmem", PS, m.ident, xn, MT, mh, ml, norm=(m.memory, m.sums, m.rstd, m.scratch),
                                  gain=lambda k: gains[:, 3 * KD + k:3 * KD + k + 1])
            with nc.Block(no_gpsimd_drain=True) as block:
                cross_projection_phase(block, sem, PS, w, 47, u, (mh, ml), m)
            with nc.Block(no_gpsimd_drain=True) as block:
                cross_attention_phase(block, sem, PS, m, uh, ul)
            with nc.Block(no_gpsimd_drain=True) as block:
                sums = residual_phase(block, sem, "xout", PS, w, 59, u, X, m)
                made = norm(block, "normf2", 4, sums)
                ffn_phase(block, sem, "ffn2", PS, w, 63, u, X, f, m, made)
            nc.all_engine_barrier(sems_to_clear=sem.span())

    with ExitStack() as ctx:
        sem = Semaphores(nc, ctx)
        arrived, mean_ready, rstd_ready, done, stored = (
            sem(f"final_{n}") for n in ("arrived", "mean", "rstd", "done", "stored"))
        with nc.Block(no_gpsimd_drain=True) as block:
            @block.sync
            def _(sp):
                sp.dma_start(final_row[:], final_gain).then_inc(arrived, 16)
                for t in range(NT):
                    sp.wait_ge(done, t + 1)
                    sp.dma_start(out[0, t * P:(t + 1) * P, :], X[:, t, :]).then_inc(stored, 16)
                sp.wait_ge(stored, 16 * NT)

            @block.scalar
            def _(act):
                act.wait_ge(mean_ready, 1)
                act.activation(m.rstd[:], m.rstd[:], ACT.Sqrt).then_inc(rstd_ready, 1)

            @block.vector
            def _(dve):
                dve.tensor_scalar(m.sums[:], m.sums[:], 1.0 / D, EPS, ALU.mult, ALU.add)
                dve.drain()
                dve.reciprocal(m.rstd[:], m.sums[:]).then_inc(mean_ready, 1)
                dve.wait_ge(rstd_ready, 1)
                refine(dve, m.sums[:], m.rstd[:], m.scratch[:, 0:NT])
                dve.wait_ge(arrived, 16)
                for t in range(NT):
                    dve.scalar_tensor_tensor(X[:, t, :], X[:, t, :], m.rstd[:, t:t + 1], final_row[:], ALU.mult, ALU.mult)\
                       .then_inc(done, 1)


def two_models(nc, x, first_ins, second_ins, out):
    mem = Memory(nc)
    PS = nc.alloc_psum_tensor("PS", [P, 8, 512], F32)
    X = mem.put("X", [P, NT, D])
    uh, ul = mem.put("uh", [P, KD, SEQ], F32R), mem.put("ul", [P, KD, SEQ], F32R)
    stream_mem = ([mem.put(f"w_raw{i}", [P, BLK]) for i in range(2)], [mem.put(f"w_hi{i}", [P, BLK], F32R) for i in range(2)],
                  [mem.put(f"w_lo{i}", [P, BLK], F32R) for i in range(2)])
    first_model(nc, PS, X, x, stream_mem, uh, ul, mem.top, first_ins)
    second_model(nc, PS, X, stream_mem, uh, ul, mem.top, second_ins, out)


def wide_blocks(a):
    n = a.shape[2] // 256
    return a.reshape(DEPTH, KD, P, n, 256).transpose(0, 3, 2, 1, 4).reshape(DEPTH, n, P, BLK)


def deep_blocks(a):
    n = a.shape[1] // 256
    return a.reshape(DEPTH, n, 2, P, D).transpose(0, 1, 3, 2, 4).reshape(DEPTH, n, P, BLK)


def columns(a):
    return a.reshape(DEPTH, KD, P).transpose(0, 2, 1)


def replicated(a):
    return np.repeat(a[:, None, :], P, axis=1)


def kernel(**inputs):
    import concourse.bacc as _bacc
    from concourse.bass_utils import run_bass_kernel_spmd as _run

    a = {n: np.asarray(v) for n, v in inputs.items()}
    w_in = a["w_in"]
    q4 = 4 * 512
    fox, dil = w_in[:, :, 0:q4], w_in[:, :, q4 + NH:]
    w1 = np.concatenate([wide_blocks(fox), wide_blocks(dil), wide_blocks(a["w_out"]), deep_blocks(a["w_ple"]),
                         wide_blocks(a["w_ple_gate"])], 1)
    fa_w = w_in[:, :, q4:q4 + NH].reshape(DEPTH, KD, P, NH).transpose(0, 2, 1, 3).reshape(DEPTH, P, KD * NH)

    def ffn(n):
        up, gate, down = wide_blocks(a[n + "_w1_2"]), wide_blocks(a[n + "_w3_2"]), deep_blocks(a[n + "_w2_2"])
        order = [up[:, 0], gate[:, 0]]
        for c in range(1, NCHUNK):
            order += [up[:, c], down[:, c - 1], gate[:, c]]
        return np.stack(order + [down[:, NCHUNK - 1]], 1)

    qfigu = wide_blocks(a["w_in_2"])
    mixer = np.concatenate([qfigu[:, 2:4], qfigu[:, 4:6], qfigu[:, 8:10], qfigu[:, 0:2], qfigu[:, 6:8]], 1)
    w2 = np.concatenate([ffn("ffn1"), mixer, wide_blocks(a["w_out_2"]), wide_blocks(a["xa_wq_2"]),
                         wide_blocks(a["xa_wkv_2"]), wide_blocks(a["xa_wo_2"]), ffn("ffn2")], 1)
    first_table, second_table, masks, bands, flag = constants()
    arrays = {
        "x": a["x"], "w1": w1, "first_table": first_table, "positions": a["positions"],
        "gains1": np.concatenate([columns(a["norm_g"]), columns(a["ple_norm_g"])], 2),
        "qk_gains": replicated(a["qk_norm_g"].reshape(DEPTH, 4 * HEAD)), "fa_w": fa_w, "fa_b": replicated(a["b_f"]),
        "pT": a["p"][:, 0].transpose(0, 2, 1).reshape(DEPTH, 2, P, SEQ).transpose(0, 2, 1, 3).reshape(DEPTH, P, 2 * SEQ),
        "w2": w2, "second_table": second_table, "masks": masks, "bands": bands, "flag": flag, "mem": a["mem_2"],
        "gains2": np.concatenate([columns(a[n]) for n in ("ffn1_norm_2", "mix_norm_2", "xa_norm_2", "mem_norm_2", "ffn2_norm_2")], 2),
        "hgrn_norm": replicated(a["hgrn_norm_2"]), "pool_scale": replicated(a["pool_scale_2"]),
        "lb_logits": np.concatenate(list(replicated(a["lb_logits_2"])), 1),
        "pool_w": a["pool_w_2"].transpose(0, 2, 1, 3).reshape(DEPTH, P, 4 * P),
        "final": np.repeat(a["final_norm_2"][None, :], P, axis=0),
    }
    nc = _bacc.Bacc("TRN2", target_bir_lowering=False, num_devices=1)
    fed, ap = {}, {}
    for name, v in arrays.items():
        v = np.ascontiguousarray(v)
        fed[f"in_{name}"] = v
        ap[name] = nc.dram_tensor(f"in_{name}", v.shape, mybir.dt.from_np(v.dtype), kind="ExternalInput").ap()
    out = nc.dram_tensor("out_0", (1, SEQ, D), F32, kind="ExternalOutput").ap()
    two_models(nc, ap["x"],
               [ap[n] for n in ("w1", "first_table", "positions", "gains1", "qk_gains", "fa_w", "fa_b", "pT")],
               [ap["w2"], ap["second_table"], ap["masks"], ap["bands"], ap["flag"], ap["mem"], ap["gains2"],
                (ap["hgrn_norm"], ap["pool_scale"], ap["lb_logits"]), ap["pool_w"], ap["final"]], out)
    return _run(nc, [fed], core_ids=[0]).results[0]["out_0"]
```

```python
from contextlib import ExitStack

import numpy as np

import concourse.bass as bass
from concourse import mybir

F32 = mybir.dt.float32
F32R = mybir.dt.float32r
I32 = mybir.dt.int32
U8 = mybir.dt.uint8
ALU = mybir.AluOpType
ACT = mybir.ActivationFunctionType
AX = mybir.AxisListType

P = 128
DEPTH = 2
SEQ = 512
NT = SEQ // P
D = 1024
KD = D // P
EPS = 1e-6
NEG = -1e30
LOWEST = -3.0e38

HEAD = 64
NH = 8
ROPE = 16
HALF = ROPE // 2
PLE = 256

NMEM = 256
MT = NMEM // P
DFF = 2816
DA = 512
HH = 4
LEVELS = 7
XH = 4
XD = 256

BLK = 2048
NB1 = 25
NB2 = 96
NCHUNK = DFF // 256

S0, S1, S2, S3 = 0, 128, 384, 768
SOFF = (S0, S1, S2, S3)
PTOFF = (0, 512, 1024, 896)


def constants():
    q = np.arange(P)[:, None]
    k = np.arange(P)[None, :]
    fox = np.zeros((P, NT, P), np.float32)
    fox[:, NT - 1] = np.where(k <= q, 0.0, NEG)
    dil = np.zeros((P, NT, P), np.float32)
    for j in range(NT):
        dist = (NT - 1 - j) * P + q - k
        count = ((dist >= 0) & (dist <= 128)).astype(int) + ((dist >= 0) & (dist % 4 == 0)) + ((dist >= 0) & (dist % 16 == 0))
        dil[:, j] = np.where(count > 0, np.log(np.maximum(count, 1).astype(np.float32)), NEG)
    upto = np.ones((P, NT, P), np.float32)
    upto[:, 0] = (q <= k)
    ident = np.eye(P, dtype=np.float32)
    inv = (np.float32(500000.0) ** (-np.arange(HALF, dtype=np.float32) / np.float32(HALF))).astype(np.float32)
    inv = np.broadcast_to(inv, (P, HALF))
    first = np.concatenate([ident, fox.reshape(P, -1), dil.reshape(P, -1), upto.reshape(P, -1), inv], 1)

    s, t = q, k
    level = np.zeros((P, LEVELS + 1, P), np.float32)
    masks = []
    for n in range(LEVELS):
        m = P >> (n + 1)
        ref = (t // (2 * m)) * 2 * m + m - 1
        right = (t // m) % 2 == 1
        level[:, n] = np.where(right, (s > ref) & (s <= t), (s > t) & (s <= ref))
        keep = ((s // (2 * m)) == (t // (2 * m))) & ((s // m) % 2 == 0)
        masks.append(keep[:, right[0]])
    level[:, LEVELS] = s <= t
    after = (s > t).astype(np.float32)
    second = np.concatenate([ident, level.reshape(P, -1), after], 1)
    masks = np.concatenate([np.tile(a, (1, NT)) for a in masks + [s == t]], 1).astype(np.float32)
    bands = np.zeros((P, 4, 3, P), np.float32)
    for g, w in enumerate((2, 4, 8, 16)):
        bands[:, g, 0] = ((s <= t) & (s > t - w)) / np.minimum(t + 1, w) - (s == t)
        bands[:, g, 1] = ((s <= t) & (s > t - w)) / w - (s == t)
        bands[:, g, 2] = (s - P > t - w) / w
    flag = np.zeros((DEPTH, P, 2), np.float32)
    flag[1:, :, 0] = 1.0
    flag[:1, :, 1] = NEG
    return [np.ascontiguousarray(a, np.float32) for a in (first, second, masks, bands.reshape(P, -1), flag)]


class Semaphores:

    def __init__(self, nc, ctx):
        self.nc, self.ctx, self.numbers = nc, ctx, []

    def __call__(self, name):
        s = self.ctx.enter_context(self.nc.semaphore(name))
        self.numbers.append(s.num)
        return s

    def span(self):
        return range(min(self.numbers), max(self.numbers) + 1)


class Memory:

    def __init__(self, nc):
        self.nc, self.top = nc, (nc.sbuf_base + 63) // 64 * 64

    def put(self, name, shape, dtype=F32):
        size = 4
        for n in shape[1:]:
            size *= n
        if dtype == U8:
            size //= 4
        h = self.nc.alloc_sbuf_tensor_at(name, shape, dtype, offset=self.top)
        self.top += (size + 63) // 64 * 64
        return h


def plus(i, step, base):
    return base if i is None else i * step + base


def refine(dve, mean, root, scratch):
    dve.scalar_tensor_tensor(scratch, root, -0.5, root, ALU.mult, ALU.mult)
    dve.drain()
    dve.tensor_tensor(scratch, scratch, mean, ALU.mult)
    dve.drain()
    dve.scalar_tensor_tensor(root, scratch, 1.5, root, ALU.add, ALU.mult)
    dve.drain()


class WeightStream:

    def __init__(self, sem, raw, hi, lo, dram, per_layer, layer):
        self.raw, self.hi, self.lo = raw, hi, lo
        self.dram = dram.rearrange("l b p n -> (l b) p n")
        self.per_layer, self.layer = per_layer, layer
        self.loaded = [sem("w_loaded0"), sem("w_loaded1")]
        self.hi_done, self.lo_done, self.used = sem("w_hi_done"), sem("w_lo_done"), sem("w_used")

    def load(self, sp, g, i=None, step=0):
        if i is None and g >= self.per_layer:
            return
        if i is not None or g >= 2:
            sp.wait_ge(self.lo_done, plus(i, step, g - 1))
        sp.dma_start(self.raw[g % 2][:], self.dram[bass.ds(self.layer * self.per_layer + plus(i, step, g), 1)]
                     .rearrange("o p n -> p (o n)")).then_inc(self.loaded[g % 2], 16)

    def split_hi(self, act, g, i=None, step=0):
        if i is None and g >= self.per_layer:
            return
        act.wait_ge(self.loaded[g % 2], plus(i, step * 8, 16 * (g // 2 + 1)))
        if i is not None or g >= 2:
            act.wait_ge(self.used, plus(i, step, g - 1))
        act.activation(self.hi[g % 2][:], self.raw[g % 2][:], ACT.Copy).then_inc(self.hi_done, 1)

    def split_lo(self, dve, g, i=None, step=0):
        if i is None and g >= self.per_layer:
            return
        dve.wait_ge(self.hi_done, plus(i, step, g + 1))
        dve.tensor_tensor(self.lo[g % 2][:], self.raw[g % 2][:], self.hi[g % 2][:], ALU.subtract).then_inc(self.lo_done, 1)

    def ready(self, pe, g, i=None, step=0):
        pe.wait_ge(self.lo_done, plus(i, step, g + 1))

    def wait_used(self, eng, g, i=None, step=0):
        eng.wait_ge(self.used, plus(i, step, g + 1))


def split_products(pe, out, still, moving, first, last):
    (sh, sl), (mh, ml) = still, moving
    pe.matmul(out, sh, mh, start=first, stop=False)
    pe.matmul(out, sh, ml, start=False, stop=False)
    return pe.matmul(out, sl, mh, start=False, stop=last)


def block_to_tokens(pe, w, g, u, outs, nt=NT, kd=KD, halves=1, before=None, made=None,
                    tile_done=None):
    if made:
        n = BLK // KD
        for k in range(KD):
            for t in range(nt):
                if t == 0 or k == 0:
                    made(pe, k, t + 1)
                last = split_products(
                    pe, outs(t, 0), [x[:, k, t * P:(t + 1) * P] for x in u],
                    (w.hi[g % 2][:, k * n:(k + 1) * n], w.lo[g % 2][:, k * n:(k + 1) * n]), k == 0, k == KD - 1)
        last.then_inc(w.used, 1)
        return
    n = BLK // kd // halves
    for t in range(nt):
        if before:
            before(t)
        for h in range(halves):
            for k in range(kd):
                a = k * n * halves + h * n
                last = split_products(
                    pe, outs(t, h), [x[:, k, t * P:(t + 1) * P] for x in u],
                    (w.hi[g % 2][:, a:a + n], w.lo[g % 2][:, a:a + n]), k == 0, k == kd - 1)
        if tile_done and t < nt - 1:
            last.then_inc(tile_done, 1)
    last.then_inc(w.used, 1)


class RowNorm:

    GROUPS = ((0, NT - 1), (NT - 1, NT))

    def __init__(self, sem, name, x, src, m):
        self.x, self.src, self.m = x, src, m
        self.squared, self.mean_ready, self.rstd_ready, self.src_ready = (
            sem(f"{name}_{n}") for n in ("squared", "mean", "rstd", "src"))

    def square(self, act, t, cols=slice(0, D), part=None):
        to = self.m.sums[:, t:t + 1] if part is None else self.m.part_sums[:, part * NT + t:part * NT + t + 1]
        act.activation(self.src[:, t, cols], self.x[:, t, cols], ACT.Square, accum_out=to).then_inc(self.squared, 1)

    def mean(self, dve, group, squares, parts=False):
        a, b = self.GROUPS[group]
        m = self.m
        if squares:
            dve.wait_ge(self.squared, squares)
        if parts:
            dve.tensor_tensor(m.sums[:, a:b], m.part_sums[:, a:b], m.part_sums[:, NT + a:NT + b], ALU.add)
            dve.drain()
        dve.tensor_scalar(m.sums[:, a:b], m.sums[:, a:b], 1.0 / D, EPS, ALU.mult, ALU.add)
        dve.drain()
        dve.reciprocal(m.rstd[:, a:b], m.sums[:, a:b]).then_inc(self.mean_ready, 1)

    def root(self, act, group):
        a, b = self.GROUPS[group]
        act.wait_ge(self.mean_ready, group + 1)
        act.activation(self.m.rstd[:, a:b], self.m.rstd[:, a:b], ACT.Sqrt).then_inc(self.rstd_ready, 1)

    def refine(self, dve, group):
        a, b = self.GROUPS[group]
        dve.wait_ge(self.rstd_ready, group + 1)
        refine(dve, self.m.sums[:, a:b], self.m.rstd[:, a:b], self.m.scratch[:, a:b])

    def scale(self, dve, t):
        dve.tensor_scalar(self.src[:, t, :], self.x[:, t, :], self.m.rstd[:, t:t + 1], None, ALU.mult).then_inc(self.src_ready, 1)

    def finish(self, dve, squares, parts=False):
        self.refine(dve, 0)
        self.scale(dve, 0)
        self.mean(dve, 1, squares, parts)
        for t in range(1, NT - 1):
            self.scale(dve, t)
        self.refine(dve, 1)
        self.scale(dve, NT - 1)


def block_to_features(pe, w, g, u, outs, made=None, first_done=None):
    for f, k in [(f, k) for k in range(KD) for f in range(2)] if made else [(f, k) for f in range(2) for k in range(KD)]:
        if made and (f == 0 or k == 0):
            made(pe, k, f + 1)
        a = k * 256 + f * P
        last = split_products(
            pe, outs(f), (w.hi[g % 2][:, a:a + P], w.lo[g % 2][:, a:a + P]),
            [x[:, k, :] for x in u], k == 0, k == KD - 1)
        if first_done and f == 0 and k == KD - 1:
            last.then_inc(first_done, 1)
    last.then_inc(w.used, 1)


def to_features_phase(block, sem, name, PS, ident, src, nt, uh, ul, gain=None, norm=None, alone=False, extra=None,
                      late=None, src_done=None, early=None):
    turned, hi_ready, lo_ready = sem(f"{name}_turned"), sem(f"{name}_hi"), sem(f"{name}_lo")
    n = nt * P

    @block.sync
    def _(sp):
        if extra:
            extra("sync", sp)

    @block.scalar
    def _(act):
        if alone:
            norm.root(act, 0)
            norm.root(act, 1)
        if extra:
            extra("scalar", act)
        for k in range(KD):
            act.wait_ge(turned, min(k + 5, KD) if early else k + 1)
            act.activation(uh[:, k, 0:n], PS[:, k, 0:n], ACT.Copy, scale=gain(k) if gain else 1.0).then_inc(hi_ready, 1)
        if late:
            late("scalar", act)

    @block.vector
    def _(dve):
        if alone:
            norm.mean(dve, 0, 0)
            norm.finish(dve, 0)
        if extra:
            extra("vector", dve)
        for k in range(KD):
            dve.wait_ge(hi_ready, k + 1)
            if gain:
                i = dve.scalar_tensor_tensor(ul[:, k, 0:n], PS[:, k, 0:n], gain(k), uh[:, k, 0:n], ALU.mult, ALU.subtract)
            else:
                i = dve.tensor_tensor(ul[:, k, 0:n], PS[:, k, 0:n], uh[:, k, 0:n], ALU.subtract)
            i.then_inc(lo_ready, 1)
        if late:
            late("vector", dve)

    @block.tensor
    def _(pe):
        if extra:
            extra("tensor", pe)

        def turn(t, ks):
            for k in ks:
                i = pe.transpose(PS[:, k, t * P:(t + 1) * P], src[:, t, k * P:(k + 1) * P], ident)
                if t == nt - 1:
                    i.then_inc(turned, 1)

        if early:
            pe.wait_ge(*early)
            for t in range(nt):
                turn(t, range(4, KD))
        for t in range(nt):
            if norm:
                pe.wait_ge(norm.src_ready, t + 1)
            if src_done:
                pe.wait_ge(src_done[0], src_done[1][t])
            turn(t, range(4 if early else KD))

    return lambda pe, k, banks: pe.wait_ge(lo_ready, max(k + 1, banks))


def residual_phase(block, sem, name, PS, w, g0, u, X, norm, extra_blocks=0, made=None):
    free = sem(f"{name}_free")
    tile_done, tile_added = sem(f"{name}_tile"), sem(f"{name}_added")
    most, rest = slice(0, 768), slice(768, D)

    @block.sync
    def _(sp):
        if g0 + 6 <= w.per_layer:
            with sp.Fori(0, 2) as i:
                for j in range(2):
                    w.load(sp, g0 + 2 + j, i, 2)
        else:
            w.load(sp, g0 + 2)
            w.load(sp, g0 + 3)
        for j in range(extra_blocks):
            w.load(sp, g0 + 6 + j)

    @block.scalar
    def _(act):
        with act.Fori(0, 2) as i:
            for j in range(2):
                w.split_hi(act, g0 + 1 + j, i, 2)
        act.wait_ge(free, 2 + 3)
        for t in range(NT):
            norm.square(act, t, most, 0)
        for t in range(NT):
            if t == NT - 1:
                norm.root(act, 0)
            act.wait_ge(tile_added, t + 1)
            norm.square(act, t, rest, 1)
        norm.root(act, 1)

    @block.vector
    def _(dve):
        for b in range(3):
            w.split_lo(dve, g0 + 1 + b)
            w.wait_used(dve, g0 + b)
            part = X[:, :, b * 256:(b + 1) * 256]
            dve.tensor_tensor(part, PS[:, 4 * (b % 2):4 * (b % 2) + 4, 0:256], part, ALU.add).then_inc(free, 1)
        w.split_lo(dve, g0 + 4)
        for t in range(NT):
            if t < NT - 1:
                dve.wait_ge(tile_done, NT - 1 + t + 1)
            else:
                norm.mean(dve, 0, 2 * NT - 1, True)
                w.wait_used(dve, g0 + 3)
            dve.tensor_tensor(X[:, t, rest], PS[:, 4 + t, 0:256], X[:, t, rest], ALU.add).then_inc(tile_added, 1)
        norm.finish(dve, 2 * NT, True)

    @block.tensor
    def _(pe):
        pe.sem_inc(free, 2)
        with pe.Fori(0, 2) as i:
            for j in range(2):
                w.ready(pe, g0 + j, i, 2)
                pe.wait_ge(free, plus(i, 2, 1 + j))
                block_to_tokens(pe, w, g0 + j, u, lambda t, h: PS[:, 4 * j + t, 0:256], made=made if j == 0 else None,
                                tile_done=tile_done if j == 1 else None)
        pe.wait_ge(tile_added, NT)


class HeadScores:

    def __init__(self, sem, name, PS, m, rows, mask):
        self.PS, self.m, self.rows, self.mask = PS, m, rows, mask
        self.scored, self.shifted, self.exped, self.turned = (sem(f"{name}_{n}") for n in ("scored", "shifted", "exped", "turned"))
        self.at = [PS[:, 1, 384:512], PS[:, 2, 0:256], PS[:, 1, 0:384], PS[:, 0, 0:512]]

    def products(self, pe, h):
        if h >= 1:
            pe.wait_ge(self.shifted, h)
        for t in range(NT):
            i = pe.matmul(self.at[t], self.m.QT[0:self.rows, h, t * P:(t + 1) * P], self.m.KT[0:self.rows, h, 0:(t + 1) * P],
                          start=True, stop=True)
        i.then_inc(self.scored, 1)

    def add_mask(self, dve, h):
        m = self.m
        dve.wait_ge(self.scored, h + 1)
        if h >= 2:
            dve.wait_ge(self.turned, h - 1)
        for t in range(NT):
            n = (t + 1) * P
            dve.tensor_tensor_reduce(out=m.S[h % 2][:, SOFF[t]:SOFF[t] + n], in0=self.at[t],
                                     in1=self.mask[:, SEQ - n:SEQ], scale=1.0, scalar=LOWEST, op0=ALU.add,
                                     op1=ALU.max, accum_out=m.nmax[h % 2][:, t:t + 1])
        dve.drain()
        dve.tensor_scalar(m.nmax[h % 2][:], m.nmax[h % 2][:], -1.0, None, ALU.mult).then_inc(self.shifted, 1)

    def exps(self, act, h):
        m = self.m
        act.wait_ge(self.shifted, h + 1)
        for t in range(NT):
            part = m.S[h % 2][:, SOFF[t]:SOFF[t] + (t + 1) * P]
            act.activation(part, part, ACT.Exp, bias=m.nmax[h % 2][:, t:t + 1],
                           accum_out=m.psum[h % 4][:, t:t + 1]).then_inc(self.exped, 1)


def projection_phase_1(block, sem, name, PS, w, g0, u, m, dilated, scores, made=None, at_free=None, mixed=None):
    g_out = sem(f"{name}_gout")
    z_out, sq_done, mean_ready, rstd_ready = (sem(f"{name}_{n}") for n in ("zout", "sq", "mean", "rstd"))
    normed, turned, even_copied, odd_copied, v_out = (sem(f"{name}_{n}") for n in ("normed", "turned", "even", "odd", "vout"))
    if not dilated:
        fa_done, fa_z, fa_exp, fa_ln = (sem(f"{name}_{n}") for n in ("fa", "faz", "faexp", "faln"))
        lf_ready, cum_done, ones_set, cum_copied, cum_moved = (
            sem(f"{name}_{n}") for n in ("lf", "cum", "ones", "cumcopied", "cummoved"))
    zn = m.zn
    gains = (2, 3) if dilated else (0, 1)
    qk_ready = [(even_copied, 2), (odd_copied, 2)] + ([] if dilated else [(cum_moved, 32)])

    @block.sync
    def _(sp):
        for j in range(8):
            w.load(sp, g0 + 2 + j)
        if not dilated:
            sp.wait_ge(ones_set, 2)
            sp.wait_ge(cum_copied, 2)
            sp.dma_start(m.QT[HEAD + 1:HEAD + 2, :, :], m.cum[:]).then_inc(cum_moved, 16)
            sp.dma_start(m.KT[HEAD:HEAD + 1, :, :], m.ncum[:]).then_inc(cum_moved, 16)
            sp.wait_ge(cum_moved, 32)

    @block.gpsimd
    def _(pool):
        if not dilated:
            pool.wait_ge(*at_free)
            pool.memset(m.QT[HEAD:HEAD + 2, :, :], 1.0).then_inc(ones_set, 1)
            pool.memset(m.KT[HEAD:HEAD + 2, :, :], 1.0).then_inc(ones_set, 1)

    def heads(j, odd):
        dst = (m.QT, m.KT)[j][0:HEAD, :, :].rearrange("p (a two) n -> p a two n", two=2)[:, :, odd, :]
        return dst, PS[HEAD * odd:HEAD * odd + HEAD, 0:4, :]

    scales = (HEAD ** -0.5, 1.0)

    @block.scalar
    def _(act):
        def take(j):
            w.wait_used(act, g0 + 2 * j + 1)
            act.activation(zn[j][:], PS[:, 4 * j:4 * j + 4, :].rearrange("p a n -> p (a n)"), ACT.Copy).then_inc(z_out, 1)

        def squares(j):
            act.wait_ge(z_out, j + 1)
            if mixed and j == 0:
                act.wait_ge(*mixed)
            act.activation(m.G[:].rearrange("p a n -> p (a n)"), zn[j][:], ACT.Square).then_inc(sq_done, 1)

        def root(j):
            act.wait_ge(mean_ready, j + 1)
            act.activation(m.rstd[:], m.rstd[:], ACT.Sqrt).then_inc(rstd_ready, 1)

        def even_heads(j):
            act.wait_ge(turned, j + 1)
            dst, src = heads(j, 0)
            act.activation(dst, src, ACT.Copy, scale=scales[j]).then_inc(even_copied, 1)

        w.split_hi(act, g0 + 1)
        if not dilated:
            act.wait_ge(fa_z, 1)
            act.activation(m.fa_e[:], m.fa_y[:], ACT.Abs).then_inc(fa_exp, 1)
            act.wait_ge(fa_exp, 1)
            act.activation(m.fa_e[:], m.fa_e[:], ACT.Exp, scale=-1.0).then_inc(fa_exp, 1)
            act.wait_ge(fa_exp, 2)
            act.activation(m.fa_e[:], m.fa_e[:], ACT.Ln, bias=1.0).then_inc(fa_ln, 1)
        w.split_hi(act, g0 + 2)
        take(0)
        w.split_hi(act, g0 + 3)
        squares(0)
        if not dilated:
            act.wait_ge(cum_done, 1)
            act.activation(m.cum[:], PS[0:NH, 7, :], ACT.Copy).then_inc(cum_copied, 1)
            act.activation(m.ncum[:], PS[0:NH, 7, :], ACT.Copy, scale=-1.0).then_inc(cum_copied, 1)
        root(0)
        w.split_hi(act, g0 + 4)
        take(1)
        w.split_hi(act, g0 + 5)
        squares(1)
        even_heads(0)
        root(1)
        w.split_hi(act, g0 + 6)
        w.wait_used(act, g0 + 5)
        act.activation(m.V[:], PS[:, 4:8, :], ACT.Copy).then_inc(v_out, 1)
        w.split_hi(act, g0 + 7)
        even_heads(1)
        w.split_hi(act, g0 + 8)
        scores.exps(act, 0)
        w.wait_used(act, g0 + 7)
        act.activation(m.G[:], PS[:, 4:8, :], ACT.Silu).then_inc(g_out, 1)

    @block.vector
    def _(dve):
        shape = [P, NT * NH, HEAD]

        def means(j):
            dve.wait_ge(sq_done, j + 1)
            dve.tensor_reduce(m.sums[:], m.G[:].rearrange("p a (h d) -> p (a h) d", d=HEAD), AX.X, ALU.add)
            dve.drain()
            dve.tensor_scalar(m.sums[:], m.sums[:], 1.0 / HEAD, EPS, ALU.mult, ALU.add)
            dve.drain()
            dve.reciprocal(m.rstd[:], m.sums[:]).then_inc(mean_ready, 1)

        def norm(j):
            n3 = zn[j][:].rearrange("p (a d) -> p a d", d=HEAD)
            dve.wait_ge(rstd_ready, j + 1)
            refine(dve, m.sums[:], m.rstd[:], m.scratch[:])
            dve.tensor_tensor(n3, n3, m.rstd[:].unsqueeze(2).to_broadcast(shape), ALU.mult)
            dve.drain()
            gi = gains[j]
            dve.tensor_tensor(n3, n3, m.qk_gain[:, gi * HEAD:(gi + 1) * HEAD].unsqueeze(1).to_broadcast(shape), ALU.mult)
            dve.drain()
            if dilated:
                z4 = zn[j][:].rearrange("p (t h d) -> p t h d", t=NT, h=NH)
                x1, x2 = z4[:, :, :, 0:HALF], z4[:, :, :, HALF:ROPE]
                full = [P, NT, NH, HALF]
                cos, sin = (a[:].unsqueeze(2).to_broadcast(full) for a in (m.cos, m.sin))
                dve.tensor_tensor(m.rot[0][:], x1, cos, ALU.mult)
                dve.tensor_tensor(m.rot[1][:], x2, sin, ALU.mult)
                dve.tensor_tensor(m.rot[2][:], x2, cos, ALU.mult)
                dve.tensor_tensor(m.rot[3][:], x1, sin, ALU.mult)
                dve.drain()
                dve.tensor_tensor(x1, m.rot[0][:], m.rot[1][:], ALU.subtract)
                dve.tensor_tensor(x2, m.rot[2][:], m.rot[3][:], ALU.add)
                dve.drain()
            dve.sem_inc(normed, 1)

        def odd_heads(j):
            dve.wait_ge(turned, j + 1)
            dst, src = heads(j, 1)
            dve.tensor_scalar(dst, src, scales[j], None, ALU.mult).then_inc(odd_copied, 1)

        w.split_lo(dve, g0 + 1)
        if not dilated:
            dve.wait_ge(fa_done, 1)
            dve.tensor_tensor(m.fa_y[:], PS[:, 4, 0:NT * NH], m.fa_bias[:].unsqueeze(1).to_broadcast([P, NT, NH]),
                              ALU.add).then_inc(fa_z, 1)
            dve.wait_ge(fa_z, 1)
            dve.wait_ge(fa_ln, 1)
            dve.scalar_tensor_tensor(m.lf[:], m.fa_y[:], 0.0, m.fa_e[:], ALU.min, ALU.subtract).then_inc(lf_ready, 1)
        w.split_lo(dve, g0 + 2)
        w.split_lo(dve, g0 + 3)
        means(0)
        norm(0)
        w.split_lo(dve, g0 + 4)
        w.split_lo(dve, g0 + 5)
        means(1)
        odd_heads(0)
        norm(1)
        w.split_lo(dve, g0 + 6)
        w.split_lo(dve, g0 + 7)
        odd_heads(1)
        w.split_lo(dve, g0 + 8)
        for ready in qk_ready:
            dve.wait_ge(*ready)
        scores.add_mask(dve, 0)

    @block.tensor
    def _(pe):
        def turn(j):
            pe.wait_ge(normed, j + 1)
            for pair in range(NH // 2):
                for t in range(NT):
                    a = t * NH * HEAD + pair * P
                    i = pe.transpose(PS[:, pair, t * P:(t + 1) * P], zn[j][:, a:a + P], m.ident)
            i.then_inc(turned, 1)

        def project(part, bank, before=None):
            for half in range(2):
                g = g0 + 2 * part + half
                if part == 3 and half == 1:
                    for ready in qk_ready:
                        pe.wait_ge(*ready)
                    scores.products(pe, 0)
                w.ready(pe, g)
                block_to_tokens(pe, w, g, u, lambda t, h: PS[:, bank + t, half * 256:half * 256 + 256],
                                before=before if half == 0 else None, made=made if part == half == 0 else None)
                if part == half == 0 and not dilated:
                    pe.wait_ge(*at_free)
                    for t in range(NT):
                        for k in range(KD):
                            i = split_products(pe, PS[:, 4, t * NH:(t + 1) * NH], [x[:, k, t * P:(t + 1) * P] for x in u],
                                               [x[:, k * NH:(k + 1) * NH] for x in (m.fa_hi, m.fa_lo)], k == 0, k == KD - 1)
                    i.then_inc(fa_done, 1)

        project(0, 0)
        if not dilated:
            pe.wait_ge(lf_ready, 1)
            for j in range(NT):
                i = pe.matmul(PS[0:NH, 7, j * P:SEQ], m.lf[:, j * NH:(j + 1) * NH], m.upto[:, 0:SEQ - j * P],
                              start=j == 0, stop=j == NT - 1)
            i.then_inc(cum_done, 1)
            project(1, 4, lambda t: pe.wait_ge(cum_copied, 2) if t == 3 else None)
        else:
            pe.wait_ge(*mixed)
            project(1, 4)
        turn(0)
        pe.wait_ge(z_out, 2)
        project(2, 4)
        pe.wait_ge(even_copied, 1)
        pe.wait_ge(odd_copied, 1)
        turn(1)
        pe.wait_ge(v_out, 1)
        project(3, 4)

    return g_out, 1


def attention_phase_1(block, sem, name, PS, m, scores, column, g_ready):
    pt_act, pt_dve, out_done, mixed = (sem(f"{name}_{n}") for n in ("ptact", "ptdve", "out", "mixed"))
    turned, exped = scores.turned, scores.exped

    @block.scalar
    def _(act):
        for h in range(NH):
            act.wait_ge(turned, h + 1)
            if h >= 2:
                act.wait_ge(out_done, h - 1)
            act.activation(m.PT[h % 2][:, 0:512], PS[:, 3, :], ACT.Copy).then_inc(pt_act, 1)
            if h + 1 < NH:
                scores.exps(act, h + 1)

    @block.vector
    def _(dve):
        def finish(h):
            dve.wait_ge(out_done, h + 1)
            dve.reciprocal(m.rinv[:], m.psum[h % 4][:])
            dve.drain()
            full = [P, NT, HEAD]
            dve.tensor_tensor(m.o[:].rearrange("p (t d) -> p t d", d=HEAD),
                              PS[:, 6 + h % 2, 0:NT * HEAD].rearrange("p (t d) -> p t d", d=HEAD),
                              m.rinv[:].unsqueeze(2).to_broadcast(full), ALU.mult)
            dve.drain()
            dve.tensor_tensor(m.mix[:, :, column + h * HEAD:column + (h + 1) * HEAD],
                              m.o[:].rearrange("p (t d) -> p t d", d=HEAD),
                              m.G[:, :, h * HEAD:(h + 1) * HEAD], ALU.mult).then_inc(mixed, 1)

        dve.wait_ge(*g_ready)
        for h in range(NH):
            if h + 1 < NH:
                scores.add_mask(dve, h + 1)
            dve.wait_ge(turned, h + 1)
            if h >= 2:
                dve.wait_ge(out_done, h - 1)
            dve.tensor_copy(m.PT[h % 2][:, 512:1280], PS[:, 4:6, :].rearrange("p a n -> p (a n)")[:, 0:768]).then_inc(pt_dve, 1)
            if h >= 1:
                finish(h - 1)
        finish(NH - 1)

    @block.tensor
    def _(pe):
        def turn(h):
            pe.wait_ge(exped, NT * (h + 1))
            if h >= 1:
                pe.wait_ge(pt_act, h)
                pe.wait_ge(pt_dve, h)
            flat = PS[:, 3:6, :].rearrange("p a n -> p (a n)")
            for j in range(NT):
                for t in range(j, NT):
                    a = PTOFF[j] + (t - j) * P
                    i = pe.transpose(flat[:, a:a + P], m.S[h % 2][:, SOFF[t] + j * P:SOFF[t] + (j + 1) * P], m.ident)
            i.then_inc(turned, 1)

        def outputs(h):
            pe.wait_ge(pt_act, h + 1)
            pe.wait_ge(pt_dve, h + 1)
            if h >= 2:
                pe.wait_ge(mixed, h - 1)
            for t in range(NT):
                for j in range(t + 1):
                    a = PTOFF[j] + (t - j) * P
                    i = pe.matmul(PS[:, 6 + h % 2, t * HEAD:(t + 1) * HEAD], m.PT[h % 2][:, a:a + P],
                                  m.V[:, j, h * HEAD:(h + 1) * HEAD], start=j == 0, stop=j == t)
            i.then_inc(out_done, 1)

        for h in range(NH):
            if h + 1 < NH:
                scores.products(pe, h + 1)
            if h == 0:
                pe.wait_ge(*g_ready)
            turn(h)
            if h >= 1:
                outputs(h - 1)
        outputs(NH - 1)

    return mixed, NH


def gate_phase(block, sem, PS, w, g0, u, X, m, made):
    squared = sem("gate_squared")
    sig_done, banks_free, sig_free = sem("gate_sig"), sem("gate_banks"), sem("gate_sig_free")

    @block.sync
    def _(sp):
        w.load(sp, g0 + 2)
        w.load(sp, g0 + 3)

    @block.scalar
    def _(act):
        def squares(part, cols, n):
            act.wait_ge(sig_free, n)
            for t in range(NT):
                act.activation(m.mix[:, t, cols], X[:, t, cols], ACT.Square,
                               accum_out=m.part_sums[:, part * NT + t:part * NT + t + 1]).then_inc(squared, 1)

        for b in range(4):
            w.split_hi(act, g0 + b + 1)
            if b == 3:
                squares(0, slice(0, 768), 3)
            w.wait_used(act, g0 + b)
            if b >= 2:
                act.wait_ge(sig_free, b - 1)
            act.activation(m.sig[b % 2][:], PS[:, 4 * (b % 2):4 * (b % 2) + 4, 0:256], ACT.Sigmoid).then_inc(sig_done, 1)
            act.wait_ge(sig_done, b + 1)
            act.sem_inc(banks_free, 1)
        squares(1, slice(768, D), 4)

    @block.vector
    def _(dve):
        for b in range(4):
            w.split_lo(dve, g0 + b + 1)
            dve.wait_ge(sig_done, b + 1)
            cols = slice(b * 256, (b + 1) * 256)
            dve.tensor_tensor(m.sig[b % 2][:], m.sig[b % 2][:], m.ple[:, :, cols], ALU.mult)
            dve.drain()
            dve.tensor_tensor(X[:, :, cols], X[:, :, cols], m.sig[b % 2][:], ALU.add).then_inc(sig_free, 1)
        dve.wait_ge(squared, 2 * NT)
        dve.tensor_tensor(m.sums[:, 0:NT], m.part_sums[:, 0:NT], m.part_sums[:, NT:2 * NT], ALU.add)

    @block.tensor
    def _(pe):
        pe.sem_inc(banks_free, 2)
        with pe.Fori(0, 2) as i:
            for j in range(2):
                w.ready(pe, g0 + j, i, 2)
                pe.wait_ge(banks_free, plus(i, 2, 1 + j))
                block_to_tokens(pe, w, g0 + j, u, lambda t, h: PS[:, 4 * j + t, 0:256], made=made if j == 0 else None)


class Box:
    pass


def first_model(nc, PS, X, x, stream_mem, uh, ul, free, ins):
    (w1, consts, positions, norm_gains, qk_gains, fa_w, fa_b, pT) = ins
    mem = Memory(nc)
    mem.top = free
    m = Box()
    xn = mem.put("xn1", [P, NT, D])
    m.mix = xn
    table = mem.put("table1", [P, P + 3 * SEQ + HALF])
    m.ident = table[:, 0:P]
    mask_fox, mask_dil = table[:, P:P + SEQ], table[:, P + SEQ:P + 2 * SEQ]
    m.upto = table[:, P + 2 * SEQ:P + 3 * SEQ]
    inv_freq = table[:, P + 3 * SEQ:]
    gains = mem.put("norm_gains1", [P, 2 * KD])
    m.qk_gain = mem.put("qk_gain", [P, 4 * HEAD])
    m.cos, m.sin = mem.put("cos", [P, NT, HALF]), mem.put("sin", [P, NT, HALF])
    m.fa_raw, m.fa_hi, m.fa_lo = mem.put("fa_raw", [P, KD * NH]), mem.put("fa_hi", [P, KD * NH], F32R), mem.put("fa_lo", [P, KD * NH], F32R)
    m.fa_bias = mem.put("fa_bias", [P, NH])
    m.fa_y, m.fa_e, m.lf = (mem.put(n, [P, NT * NH]) for n in ("fa_y", "fa_e", "lf"))
    m.sums, m.rstd, m.scratch = (mem.put(n, [P, NT * NH]) for n in ("sums", "rstd", "scratch"))
    m.nmax = [mem.put(f"nmax{i}", [P, NT]) for i in range(2)]
    m.psum = [mem.put(f"psum{i}", [P, NT]) for i in range(4)]
    m.rinv = mem.put("rinv", [P, NT])
    m.part_sums = mem.put("part_sums", [P, 2 * NT])
    m.o = mem.put("o1", [P, NT * HEAD])
    p_hi, p_lo = mem.put("p_hi", [P, 2, SEQ], F32R), mem.put("p_lo", [P, 2, SEQ], F32R)
    at = mem.top
    m.QT = mem.put("QT", [HEAD + 2, NH, SEQ])
    m.KT = mem.put("KT", [HEAD + 2, NH, SEQ])
    m.V, m.G = mem.put("V1", [P, NT, NH * HEAD]), mem.put("G1", [P, NT, NH * HEAD])
    at2 = mem.top
    m.S = [mem.put(f"S{i}", [P, 1280]) for i in range(2)]
    m.PT = [mem.put(f"PT{i}", [P, 1280]) for i in range(2)]
    end = mem.top
    mem.top = at2
    m.zn = [mem.put(f"zn{i}", [P, NT * NH * HEAD]) for i in range(2)]
    m.cum, m.ncum = mem.put("cum", [NH, SEQ]), mem.put("ncum", [NH, SEQ])
    end = max(end, mem.top)
    m.rot = []
    for i in range(4):
        m.rot.append(mem.put(f"rot{i}", [P, NT, NH, HALF]))
    end = max(end, mem.top)
    assert end <= nc.sbuf_usable_end, end
    mem.top = at
    m.ple = mem.put("ple", [P, NT, D])
    m.sig = [mem.put(f"sig{i}", [P, NT, 256]) for i in range(2)]
    p_raw = mem.put("p_raw", [P, 2, SEQ])
    mem.top = at
    pos, posf, ang, turns, red, over = (mem.put(n, [P, NT], I32) if n == "pos" else mem.put(n, [P, NT] if n == "posf" else [P, NT, HALF])
                                        for n in ("pos", "posf", "ang", "turns", "red", "over"))

    with ExitStack() as ctx:
        sem = Semaphores(nc, ctx)
        arrived, angles, x_arrived = sem("tables_arrived"), sem("angles_ready"), sem("x_arrived")
        with nc.Block(no_gpsimd_drain=True) as block:
            @block.sync
            def _(sp):
                sp.dma_start(table[:], consts).then_inc(arrived, 16)
                sp.dma_start(pos[:], positions.rearrange("b (t p) -> p (b t)", p=P), allow_slow_non_contiguous=True).then_inc(arrived, 16)
                sp.dma_start(X[:], x.rearrange("b (t p) n -> p (b t) n", p=P)).then_inc(x_arrived, 16)

            @block.vector
            def _(dve):
                C1, C2 = 6.28125, 0.0019350051879882812
                C3 = 2 * np.pi - C1 - C2
                dve.wait_ge(arrived, 32)
                dve.tensor_copy(posf[:], pos[:])
                dve.drain()
                dve.tensor_tensor(ang[:], posf[:].unsqueeze(2).to_broadcast([P, NT, HALF]),
                                  inv_freq.unsqueeze(1).to_broadcast([P, NT, HALF]), ALU.mult)
                dve.drain()
                dve.tensor_scalar(turns[:], ang[:], float(1 / (2 * np.pi)), 12582912.0, ALU.mult, ALU.add)
                dve.drain()
                dve.tensor_scalar(turns[:], turns[:], 12582912.0, None, ALU.subtract)
                dve.drain()
                for c in (C1, C2, C3):
                    dve.scalar_tensor_tensor(ang[:], turns[:], -float(c), ang[:], ALU.mult, ALU.add)
                    dve.drain()
                dve.tensor_scalar(red[:], ang[:], float(np.pi / 2), None, ALU.add)
                dve.drain()
                dve.tensor_scalar(over[:], red[:], float(np.pi), -2 * float(np.pi), ALU.is_gt, ALU.mult)
                dve.drain()
                dve.tensor_tensor(red[:], red[:], over[:], ALU.add)
                dve.drain()
                for a in (red, ang):
                    dve.tensor_scalar(a[:], a[:], 3.1415925, -3.1415925, ALU.min, ALU.max).then_inc(angles, 1)

            @block.scalar
            def _(act):
                act.wait_ge(angles, 2)
                act.activation(m.cos[:], red[:], ACT.Sin)
                act.activation(m.sin[:], ang[:], ACT.Sin)
                act.wait_ge(x_arrived, 16)
                for t in range(NT):
                    act.activation(m.mix[:, t, :], X[:, t, :], ACT.Square, accum_out=m.sums[:, t:t + 1])
        nc.all_engine_barrier(sems_to_clear=sem.span())

    with ExitStack() as ctx:
        sem = Semaphores(nc, ctx)
        with nc.Fori(0, DEPTH) as layer:
            w = WeightStream(sem, *stream_mem, w1, NB1, layer)
            small = sem("small_arrived")
            p_split, p_done = sem("p_split"), sem("p_done")

            def start(kind, eng):
                one = bass.ds(layer, 1)
                if kind == "sync":
                    w.load(eng, 0)
                    eng.dma_start(gains[:], norm_gains[one].rearrange("o p n -> p (o n)")).then_inc(small, 16)
                    w.load(eng, 1)
                    eng.dma_start(m.qk_gain[:], qk_gains[one].rearrange("o p n -> p (o n)")).then_inc(small, 16)
                    eng.dma_start(m.fa_raw[:], fa_w[one].rearrange("o p n -> p (o n)")).then_inc(small, 16)
                    eng.dma_start(m.fa_bias[:], fa_b[one].rearrange("o p n -> p (o n)")).then_inc(small, 16)
                    eng.dma_start(p_raw[:].rearrange("p k n -> p (k n)"), pT[one].rearrange("o p n -> p (o n)")).then_inc(small, 16)
                if kind == "scalar":
                    w.split_hi(eng, 0)
                    eng.wait_ge(small, 80)
                if kind == "vector":
                    w.split_lo(eng, 0)

            def start_late(kind, eng):
                if kind == "scalar":
                    eng.activation(p_hi[:], p_raw[:], ACT.Copy).then_inc(p_split, 1)
                    eng.activation(m.fa_hi[:], m.fa_raw[:], ACT.Copy).then_inc(p_split, 1)
                if kind == "vector":
                    eng.wait_ge(p_split, 2)
                    eng.tensor_tensor(p_lo[:], p_raw[:], p_hi[:], ALU.subtract).then_inc(p_done, 1)
                    eng.tensor_tensor(m.fa_lo[:], m.fa_raw[:], m.fa_hi[:], ALU.subtract).then_inc(p_done, 1)

            u = (uh, ul)
            ple_tile, ple_copied = sem("ple_tile"), sem("ple_copied")

            def ple(kind, eng):
                g = 20
                if kind == "scalar":
                    w.split_hi(eng, g + 1)
                    for t in range(NT):
                        if t < NT - 1:
                            eng.wait_ge(ple_tile, t + 1)
                        else:
                            w.wait_used(eng, g)
                        eng.activation(m.ple[:, t, :].rearrange("p (a n) -> p a n", n=512), PS[:, 2 * t:2 * t + 2, :],
                                       ACT.Copy).then_inc(ple_copied, 1)
                if kind == "vector":
                    w.split_lo(eng, g + 1)
                if kind == "tensor":
                    w.ready(eng, g)
                    block_to_tokens(eng, w, g, (p_hi, p_lo), lambda t, h: PS[:, 2 * t + h, :], kd=2, halves=2,
                                    tile_done=ple_tile)
                    eng.wait_ge(ple_copied, NT)

            with nc.Block(no_gpsimd_drain=True) as block:
                made = to_features_phase(block, sem, "norm1", PS, m.ident, xn, NT, uh, ul, gain=lambda k: gains[:, k:k + 1],
                                         norm=RowNorm(sem, "norm1", X, xn, m), alone=True, extra=start, late=start_late)
                scores = HeadScores(sem, "foxatt", PS, m, HEAD + 2, mask_fox)
                g_ready = projection_phase_1(block, sem, "fox", PS, w, 0, u, m, False, scores, made, (p_done, 2))
                mixed = attention_phase_1(block, sem, "foxatt", PS, m, scores, 0, g_ready)
                scores = HeadScores(sem, "dilatt", PS, m, HEAD, mask_dil)
                g_ready = projection_phase_1(block, sem, "dil", PS, w, 8, u, m, True, scores, mixed=mixed)
                mixed = attention_phase_1(block, sem, "dilatt", PS, m, scores, NH * HEAD, g_ready)
                made = to_features_phase(block, sem, "mix1", PS, m.ident, m.mix, NT, uh, ul, src_done=(mixed[0], [NH] * NT))
                norm = RowNorm(sem, "norm1g", X, xn, m)
                residual_phase(block, sem, "out1", PS, w, 16, u, X, norm, 1, made)
                made = to_features_phase(block, sem, "norm1g", PS, m.ident, xn, NT, uh, ul, norm=norm, extra=ple,
                                         gain=lambda k: gains[:, KD + k:KD + k + 1])
                gate_phase(block, sem, PS, w, 21, u, X, m, made)
            nc.all_engine_barrier(sems_to_clear=sem.span())


def ffn_phase(block, sem, name, PS, w, g0, u, X, f, m, made, norm=None):
    silu_done, gated, h_hi, h_lo = (sem(f"{name}_{n}") for n in ("silu", "gated", "hhi", "hlo"))
    summed, free, half_up = sem(f"{name}_summed"), sem(f"{name}_free"), sem(f"{name}_halfup")
    LOOPS = (NCHUNK - 1) // 2
    END = g0 + 3 * NCHUNK

    def at(i, c, per=1, base=0):
        return plus(i, 2 * per, per * (1 + c) + base)

    @block.sync
    def _(sp):
        w.load(sp, g0 + 2)
        w.load(sp, g0 + 3)
        with sp.Fori(0, LOOPS - 1) as i:
            for j in range(6):
                w.load(sp, g0 + 4 + j, i, 6)
        for g in range(g0 + 4 + 6 * (LOOPS - 1), END + 2):
            w.load(sp, g)

    @block.scalar
    def _(act):
        w.split_hi(act, g0 + 1)
        w.wait_used(act, g0)
        act.activation(f.silu[:], PS[:, 0:2, :], ACT.Silu).then_inc(silu_done, 1)
        w.split_hi(act, g0 + 2)
        act.wait_ge(gated, 1)
        act.activation(f.h_hi[:], f.h[:], ACT.Copy).then_inc(h_hi, 1)

        def chunk(i, c):
            g = g0 + 2 + 3 * c
            w.split_hi(act, g + 1, i, 6)
            w.wait_used(act, g, i, 6)
            act.activation(f.silu[:], PS[:, 0:2, :], ACT.Silu).then_inc(silu_done, 1)
            w.split_hi(act, g + 2, i, 6)
            w.split_hi(act, g + 3, i, 6)

        def high(i, c):
            act.wait_ge(gated, at(i, c, 1, 1))
            act.activation(f.h_hi[:], f.h[:], ACT.Copy).then_inc(h_hi, 1)

        with act.Fori(0, LOOPS - 1) as i:
            for c in range(2):
                chunk(i, c)
                high(i, c)
        chunk(LOOPS - 1, 0)
        high(LOOPS - 1, 0)
        chunk(LOOPS - 1, 1)
        for half in range(2):
            act.wait_ge(gated, NCHUNK + half)
            act.activation(f.h_hi[:, half, :], f.h[:, half, :], ACT.Copy).then_inc(h_hi, 1)
        w.split_hi(act, END)
        for t in range(NT):
            if norm and t == NT - 1:
                norm.root(act, 0)
            act.wait_ge(free, 2 + NT * (NCHUNK - 1) + t + 1)
            if norm:
                norm.square(act, t)
            else:
                act.activation(m.mix[:, t, :], X[:, t, :], ACT.Square, accum_out=m.sums[:, t:t + 1])
        if norm:
            norm.root(act, 1)

    @block.vector
    def _(dve):
        def gate(g, i, step, n):
            dve.wait_ge(silu_done, n)
            w.wait_used(dve, g, i, step)
            dve.tensor_tensor(f.h[:], PS[:, 2:4, :], f.silu[:], ALU.mult).then_inc(gated, 1)
            dve.wait_ge(h_hi, n)
            dve.tensor_tensor(f.h_lo[:], f.h[:], f.h_hi[:], ALU.subtract).then_inc(h_lo, 1)

        def add(g, i, c, step, tiles):
            for t in tiles:
                if t < NT - 1:
                    dve.wait_ge(summed, at(i, c, NT - 1, t + 2 - NT))
                else:
                    w.wait_used(dve, g, i, step)
                b = 4 + 2 * (t % 2)
                x = X[:, t, :].rearrange("p (a n) -> p a n", n=512)
                dve.scalar_tensor_tensor(x, PS[:, b:b + 2, :], 0.5, x, ALU.mult, ALU.add).then_inc(free, 1)

        w.split_lo(dve, g0 + 1)
        w.split_lo(dve, g0 + 2)
        gate(g0 + 1, None, 0, 1)

        def chunk(i, c):
            g = g0 + 2 + 3 * c
            w.split_lo(dve, g + 1, i, 6)
            add(g + 1, i, c, 6, (0, 1))
            w.split_lo(dve, g + 2, i, 6)
            add(g + 1, i, c, 6, (2, 3))
            w.split_lo(dve, g + 3, i, 6)

        with dve.Fori(0, LOOPS - 1) as i:
            for c in range(2):
                chunk(i, c)
                gate(g0 + 4 + 3 * c, i, 6, at(i, c, 1, 1))
        chunk(LOOPS - 1, 0)
        gate(g0 + 4, LOOPS - 1, 6, at(LOOPS - 1, 0, 1, 1))
        chunk(LOOPS - 1, 1)
        dve.wait_ge(silu_done, NCHUNK)
        for half in range(2):
            if half == 0:
                dve.wait_ge(half_up, LOOPS)
            else:
                w.wait_used(dve, END - 2)
            dve.tensor_tensor(f.h[:, half, :], PS[:, 2 + half, :], f.silu[:, half, :], ALU.mult).then_inc(gated, 1)
            dve.wait_ge(h_hi, NCHUNK + half)
            dve.tensor_tensor(f.h_lo[:, half, :], f.h[:, half, :], f.h_hi[:, half, :], ALU.subtract).then_inc(h_lo, 1)
        add(END - 1, None, NCHUNK - 1, 0, (0, 1))
        w.split_lo(dve, END)
        add(END - 1, None, NCHUNK - 1, 0, (2,))
        if norm:
            norm.mean(dve, 0, NT - 1)
        add(END - 1, None, NCHUNK - 1, 0, (NT - 1,))
        if norm:
            norm.finish(dve, NT)

    @block.tensor
    def _(pe):
        def up(g, bank, i, step, made=None, first_done=None):
            w.ready(pe, g, i, step)
            block_to_features(pe, w, g, u, lambda t: PS[:, bank + t, :], made, first_done)

        def down_part(g, t, k):
            for half in range(2):
                a = k * D + half * 512
                last = split_products(
                    pe, PS[:, 4 + 2 * (t % 2) + half, :], [x[:, k, t * P:(t + 1) * P] for x in (f.h_hi, f.h_lo)],
                    (w.hi[g % 2][:, a:a + 512], w.lo[g % 2][:, a:a + 512]), k == 0, k == 1)
            return last

        def down(g, i, c, step):
            w.ready(pe, g, i, step)
            pe.wait_ge(h_lo, at(i, c))
            for t in range(NT):
                pe.wait_ge(free, at(i, c, NT, t + 1 - NT))
                down_part(g, t, 0)
                down_part(g, t, 1).then_inc(summed if t < NT - 1 else w.used, 1)

        pe.sem_inc(free, 2)
        up(g0, 0, None, 0, made)
        up(g0 + 1, 2, None, 0)
        with pe.Fori(0, LOOPS) as i:
            for c in range(2):
                g = g0 + 2 + 3 * c
                pe.wait_ge(silu_done, at(i, c))
                up(g, 0, i, 6)
                down(g + 1, i, c, 6)
                pe.wait_ge(gated, at(i, c))
                up(g + 2, 2, i, 6, first_done=half_up if c == 1 else None)
        w.ready(pe, END - 1)
        for t, k in ((0, 0), (1, 0), (0, 1), (1, 1), (2, 0), (2, 1), (3, 0), (3, 1)):
            pe.wait_ge(h_lo, NCHUNK + k)
            if k == 0:
                pe.wait_ge(free, 2 + NT * (NCHUNK - 1) + t - 1)
            last = down_part(END - 1, t, k)
            if k == 1:
                last.then_inc(summed if t < NT - 1 else w.used, 1)


def projection_phase_2(block, sem, PS, w, g0, u, m, one, pool_in, row_in, flag, made):
    s = Box()
    s.small, s.rmax, s.rexp, s.rsum, s.rln = (sem(f"mix2_{n}") for n in ("small", "rmax", "rexp", "rsum", "rln"))
    s.zread, s.zmin, s.ln1, s.ln2, s.diff = (sem(f"mix2_{n}") for n in ("zread", "zmin", "ln1", "ln2", "diff"))
    s.vread, s.uread, s.silu, s.lf = (sem(f"mix2_{n}") for n in ("vread", "uread", "silu", "lf"))

    @block.sync
    def _(sp):
        w.load(sp, g0 + 2)
        made(sp, KD - 1, 0)
        sp.dma_start(m.lb[:], row_in[2]).then_inc(s.small, 16)
        sp.dma_start(m.flag[:], flag[one].rearrange("o p n -> p (o n)")).then_inc(s.small, 16)
        sp.dma_start(m.hnorm[:], row_in[0][one].rearrange("o p n -> p (o n)")).then_inc(s.small, 16)
        sp.dma_start(m.pscale[:], row_in[1][one].rearrange("o p n -> p (o n)")).then_inc(s.small, 16)
        sp.dma_start(m.bands[:], pool_in[0]).then_inc(s.small, 16)
        sp.dma_start(m.pool_w[:], pool_in[1][one].rearrange("o p n -> p (o n)")).then_inc(s.small, 16)
        for j in range(9):
            w.load(sp, g0 + 3 + j)

    zf = PS[:, 0:4, :]

    @block.scalar
    def _(act):
        w.split_hi(act, g0 + 1)
        act.wait_ge(s.rmax, 1)
        act.activation(m.e[:], m.lb[:], ACT.Exp).then_inc(s.rexp, 1)
        act.wait_ge(s.rsum, 1)
        act.activation(m.lnsum[:], m.esum[:], ACT.Ln).then_inc(s.rln, 1)
        w.split_hi(act, g0 + 2)
        w.split_hi(act, g0 + 3)
        act.activation(m.t1[:], zf, ACT.Abs).then_inc(s.zread, 1)
        act.activation(m.K[:], zf, ACT.Sigmoid, scale=-1.0).then_inc(s.zread, 1)
        w.split_hi(act, g0 + 4)
        act.wait_ge(s.zread, 2)
        act.activation(m.t1[:], m.t1[:], ACT.Exp, scale=-1.0)
        act.drain()
        act.activation(m.t1[:], m.t1[:], ACT.Ln, bias=1.0).then_inc(s.ln1, 1)
        w.split_hi(act, g0 + 5)
        act.activation(m.V[:], PS[:, 4:8, :], ACT.Copy).then_inc(s.vread, 1)
        act.wait_ge(s.diff, 1)
        act.activation(m.t2[:], m.t2[:], ACT.Abs)
        act.drain()
        act.activation(m.t2[:], m.t2[:], ACT.Exp, scale=-1.0)
        act.drain()
        act.activation(m.t2[:], m.t2[:], ACT.Ln, bias=1.0).then_inc(s.ln2, 1)
        w.split_hi(act, g0 + 6)
        w.wait_used(act, g0 + 5)
        act.activation(m.U[:], PS[:, 0:4, :], ACT.Copy).then_inc(s.uread, 1)
        w.split_hi(act, g0 + 7)
        w.split_hi(act, g0 + 8)
        w.wait_used(act, g0 + 7)
        act.activation(m.Q[:], PS[:, 4:8, :], ACT.Copy)
        w.split_hi(act, g0 + 9)
        w.split_hi(act, g0 + 10)
        w.wait_used(act, g0 + 9)
        act.activation(m.G[:], PS[:, 0:4, :], ACT.Silu).then_inc(s.silu, 1)

    @block.vector
    def _(dve):
        l0, l1 = m.lb[:, 0:DA], m.lb[:, DA:2 * DA]
        e0, e1 = m.e[:, 0:DA], m.e[:, DA:2 * DA]
        full = [P, NT, DA]
        w.split_lo(dve, g0 + 1)
        dve.wait_ge(s.small, 96)
        dve.tensor_tensor(m.esum[:], l0, l1, ALU.max)
        dve.drain()
        for part in (l0, l1):
            dve.tensor_tensor(part, part, m.esum[:], ALU.subtract)
        dve.drain()
        dve.sem_inc(s.rmax, 1)
        dve.wait_ge(s.rexp, 1)
        dve.tensor_tensor(m.esum[:], e0, e1, ALU.add).then_inc(s.rsum, 1)
        dve.wait_ge(s.rsum, 1)
        w.split_lo(dve, g0 + 2)
        dve.wait_ge(s.rln, 1)
        for part in (l0, l1):
            dve.tensor_tensor(part, part, m.lnsum[:], ALU.subtract)
        dve.reciprocal(m.esum[:], m.esum[:])
        dve.drain()
        for part in (e0, e1):
            dve.tensor_tensor(part, part, m.esum[:], ALU.mult)
        dve.drain()
        dve.tensor_tensor(m.esum[:], e0, e1, ALU.add)
        dve.drain()
        dve.tensor_tensor(m.esum[:], m.esum[:], e0, ALU.subtract)
        on, floor = m.flag[:, 0:1], m.flag[:, 1:2]
        dve.tensor_scalar(m.ln1m[:], l0, on, None, ALU.mult)
        dve.tensor_scalar(m.lnlb[:], l1, on, floor, ALU.mult, ALU.add)
        dve.drain()
        dve.tensor_scalar(m.one_less[:], m.esum[:], on, -1.0, ALU.mult, ALU.mult)
        dve.drain()
        dve.tensor_scalar(m.one_less[:], m.one_less[:], 1.0, None, ALU.add)
        w.split_lo(dve, g0 + 3)
        dve.wait_ge(s.zread, 2)
        dve.tensor_scalar(m.t2[:], zf, 0.0, None, ALU.min).then_inc(s.zmin, 1)
        w.split_lo(dve, g0 + 4)
        dve.drain()
        dve.wait_ge(s.ln1, 1)
        dve.tensor_tensor(m.t2[:], m.t2[:], m.t1[:], ALU.subtract)
        dve.drain()
        rows = [a[:].unsqueeze(1).to_broadcast(full) for a in (m.ln1m, m.lnlb, m.one_less)]
        dve.tensor_tensor(m.t2[:], m.t2[:], rows[0], ALU.add)
        dve.drain()
        dve.tensor_tensor(m.LF[:], m.t2[:], rows[1], ALU.max)
        dve.drain()
        dve.tensor_tensor(m.t2[:], m.t2[:], rows[1], ALU.subtract).then_inc(s.diff, 1)
        w.split_lo(dve, g0 + 5)
        dve.tensor_tensor(m.K[:], m.K[:], rows[2], ALU.mult)
        dve.wait_ge(s.ln2, 1)
        dve.drain()
        dve.tensor_tensor(m.LF[:], m.LF[:], m.t2[:], ALU.add).then_inc(s.lf, 1)
        for j in (6, 7, 8, 9, 10):
            w.split_lo(dve, g0 + j)
        dve.wait_ge(s.silu, 1)
        dve.drain()
        dve.tensor_tensor(m.G[:], m.G[:], m.hnorm[:].unsqueeze(1).to_broadcast(full), ALU.mult)

    @block.tensor
    def _(pe):
        def project(part):
            for half in range(2):
                g = g0 + 2 * part + half
                w.ready(pe, g)
                block_to_tokens(pe, w, g, u, lambda t, h: PS[:, 4 * (part % 2) + t, half * 256:half * 256 + 256],
                                made=made if part == half == 0 else None)

        project(0)
        project(1)
        pe.wait_ge(s.zread, 2)
        pe.wait_ge(s.zmin, 1)
        project(2)
        pe.wait_ge(s.vread, 1)
        for half in range(2):
            g = g0 + 6 + half
            w.ready(pe, g)
            block_to_features(pe, w, g, u, lambda t: PS[:, 4 + 2 * half + t, :])
        pe.wait_ge(s.uread, 1)
        project(4)

    return (s.lf, 1), (s.silu, 1)


def pool_and_states_phase(block, sem, PS, m, uh, ul, lf_ready, banks_free):
    lf_hi, lf_lo, state_read = sem("lf_hi"), sem("lf_lo"), sem("state_read")
    pooled, pool_copied, mapped, mapped_read = (sem(f"pool_{n}") for n in ("pooled", "copied", "mapped", "read"))
    suffix, suffix_exp, kp, dec, dec_exp, outer = (sem(f"state_{n}") for n in ("suffix", "sexp", "kp", "dec", "dexp", "outer"))

    @block.scalar
    def _(act):
        act.wait_ge(*lf_ready)
        act.activation(uh[:, 6, 0:P], m.after, ACT.Copy)
        act.activation(uh[:, 0:NT, :], m.LF[:], ACT.Copy).then_inc(lf_hi, 1)
        act.activation(uh[:, 4:6, :].rearrange("p a n -> p (a n)"), m.level, ACT.Copy).then_inc(lf_hi, 1)
        for g in range(4):
            act.wait_ge(pooled, g + 1)
            act.activation(m.pT[:, g, :], PS[:, g, :], ACT.Copy).then_inc(pool_copied, 1)
        for c in range(NT):
            act.wait_ge(suffix, c + 1)
            act.activation(m.Kp[:, c, :], PS[:, 4 + c, :], ACT.Exp).then_inc(suffix_exp, 1)
        act.wait_ge(dec, 1)
        act.activation(m.dec[:], PS[:, 7, 0:HH * 2], ACT.Exp).then_inc(dec_exp, 1)

    @block.vector
    def _(dve):
        dve.wait_ge(lf_hi, 1)
        dve.tensor_tensor(ul[:, 0:NT, :], m.LF[:], uh[:, 0:NT, :], ALU.subtract).then_inc(lf_lo, 1)
        for c in range(NT - 1):
            dve.wait_ge(suffix_exp, c + 1)
            dve.tensor_tensor(m.Kp[:, c, :], m.Kp[:, c, :], m.K[:, c, :], ALU.mult).then_inc(kp, 1)
        for g in range(4):
            dve.wait_ge(mapped, g + 1)
            dve.tensor_tensor(m.mix[:, :, DA + g * P:DA + (g + 1) * P], PS[:, g, :].rearrange("p (t n) -> p t n", n=P),
                              m.pscale[:, g * P:(g + 1) * P].unsqueeze(1).to_broadcast([P, NT, P]), ALU.mult)\
               .then_inc(mapped_read, 1)
        dve.wait_ge(outer, 1)
        dve.wait_ge(dec_exp, 1)
        dve.tensor_copy(m.St[:, 0, :], PS[:, 4, :]).then_inc(state_read, 1)
        for c in (1, 2):
            dve.drain()
            for h in range(HH):
                cols = slice(h * P, (h + 1) * P)
                d = (c - 1) * HH + h
                dve.scalar_tensor_tensor(m.St[:, c, cols], m.St[:, c - 1, cols], m.dec[:, d:d + 1],
                                         PS[:, 4 + c, cols], ALU.mult, ALU.add)

    @block.tensor
    def _(pe):
        pe.wait_ge(*lf_ready)
        pe.wait_ge(*banks_free)
        for g in range(4):
            for t in range(NT):
                out = PS[:, g, t * P:(t + 1) * P]
                i = pe.matmul(out, m.U[:, t, g * P:(g + 1) * P], m.band(g, 1 if t else 0), start=True, stop=t == 0)
                if t:
                    i = pe.matmul(out, m.U[:, t - 1, g * P:(g + 1) * P], m.band(g, 2), start=False, stop=True)
            i.then_inc(pooled, 1)
        for c in range(NT):
            pe.wait_ge(lf_lo, 1)
            pe.matmul(PS[:, 4 + c, :], uh[:, 6, 0:P], uh[:, c, :], start=True, stop=False)
            pe.matmul(PS[:, 4 + c, :], uh[:, 6, 0:P], ul[:, c, :], start=False, stop=True).then_inc(suffix, 1)
        for g in range(4):
            pe.wait_ge(pool_copied, g + 1)
            for t in range(NT):
                i = pe.matmul(PS[:, g, t * P:(t + 1) * P], m.pT[:, g, t * P:(t + 1) * P], m.pool_w[:, g * P:(g + 1) * P],
                              start=True, stop=True)
            i.then_inc(mapped, 1)
        pe.wait_ge(suffix_exp, 4)
        for c in (1, 2):
            for h in range(HH):
                d = (c - 1) * HH + h
                i = pe.matmul(PS[:, 7, d:d + 1], m.LF[:, c, h * P:(h + 1) * P], m.level[:, LEVELS * P + P - 1:LEVELS * P + P],
                              start=True, stop=True)
        i.then_inc(dec, 1)
        pe.wait_ge(kp, 3)
        for c in range(NT - 1):
            for h in range(HH):
                cols = slice(h * P, (h + 1) * P)
                i = pe.matmul(PS[:, 4 + c, cols], m.Kp[:, c, cols], m.V[:, c, cols], start=True, stop=True)
        i.then_inc(outer, 1)

    return (mapped_read, 4), (state_read, 1)


def recurrence_phase(block, sem, PS, m, uh, ul, pooled, bank_free):
    mixed, keys_weighed = sem("rec_mixed"), sem("rec_keysweighed")
    k_turned, k_copied, summed, exped, weighed, scored, kept, out_done, out_sq, out_read = (
        sem(f"rec_{n}") for n in ("kturned", "kcopied", "summed", "exped", "weighed", "scored", "kept", "out", "outsq", "outread"))
    zeroed, mean_ready, rstd_ready = sem("rec_zeroed"), sem("rec_mean"), sem("rec_rstd")
    UNITS = 5

    def right(ap, n, side=1):
        mm = P >> (n + 1)
        return ap.rearrange("p (b two m) -> p b two m", two=2, m=mm)[:, :, side, :]

    @block.gpsimd
    def _(pool):
        pool.wait_ge(*pooled)
        for i in range(2):
            pool.memset(m.AT[i][:], 0.0).then_inc(zeroed, 1)
        for h in range(HH):
            pool.wait_ge(k_copied, h + 1)
            pool.wait_ge(exped, NT * (h + 1))
            for n in range(LEVELS):
                e = right(m.E[h % 2][:, n, :], n, 0)
                i = pool.tensor_tensor(e, e, right(m.Kf[h % 2][:], n, 0), ALU.mult)
            i.then_inc(keys_weighed, 1)

    @block.scalar
    def _(act):
        def exps(h):
            act.wait_ge(k_turned, h + 1)
            if h >= 2:
                act.wait_ge(out_done, h - 1)
            act.activation(m.Kf[h % 2][:], PS[:, 4, :], ACT.Copy).then_inc(k_copied, 1)
            for c in range(NT):
                act.wait_ge(summed, NT * h + c + 1)
                b = 2 * (c % 2)
                act.activation(m.E[h % 2][:, :, c * P:(c + 1) * P],
                               PS[:, b:b + 2, :].rearrange("p a (l t) -> p (a l) t", t=P), ACT.Exp).then_inc(exped, 1)

        act.wait_ge(*pooled)
        exps(0)
        exps(1)
        for h in range(HH):
            act.wait_ge(out_done, h + 1)
            act.activation(m.mix[:, :, h * P:(h + 1) * P], PS[:, 7, :].rearrange("p (c v) -> p c v", v=P), ACT.Square)\
               .then_inc(out_sq, 1)
            if h + 2 < HH:
                exps(h + 2)
        act.wait_ge(mean_ready, 1)
        act.activation(m.orstd[:], m.orstd[:], ACT.Sqrt).then_inc(rstd_ready, 1)

    @block.vector
    def _(dve):
        def weigh(h):
            dve.wait_ge(exped, NT * (h + 1))
            E = m.E[h % 2]
            for n in range(LEVELS):
                e = right(E[:, n, :], n)
                dve.tensor_tensor(e, e, right(m.Q[:, h, :], n), ALU.mult)
            dve.tensor_tensor(E[:, LEVELS, :], E[:, LEVELS, :], m.Q[:, h, :], ALU.mult)
            dve.drain()
            dve.sem_inc(weighed, 1)

        def keep(h):
            if h >= 2:
                dve.wait_ge(out_done, h - 1)
            AT = m.AT[h % 2]
            for unit in range(UNITS):
                dve.wait_ge(scored, UNITS * h + unit + 1)
                b = 5 + unit % 2
                for n in (2 * unit, 2 * unit + 1):
                    if n < LEVELS:
                        mm = P >> (n + 1)
                        a = (n % 2) * 256
                        dve.copy_predicated(right(AT[:].rearrange("p c t -> p (c t)"), n),
                                            m.masks[:, n * 256:(n + 1) * 256].rearrange("p (b m) -> p b m", m=mm),
                                            PS[:, b, a:a + 256].rearrange("p (b m) -> p b m", m=mm))
                        dve.drain()
                if unit == UNITS - 1:
                    dve.copy_predicated(AT[:].rearrange("p c t -> p (c t)"), m.masks[:, LEVELS * 256:], PS[:, b, :])
                dve.drain()
                dve.sem_inc(kept, 1)

        def finish(h):
            dve.wait_ge(out_sq, h + 1)
            dve.tensor_reduce(m.osum[:, h * NT:(h + 1) * NT], m.mix[:, :, h * P:(h + 1) * P], AX.X, ALU.add)
            dve.drain()
            dve.tensor_tensor(m.mix[:, :, h * P:(h + 1) * P], PS[:, 7, :].rearrange("p (c v) -> p c v", v=P),
                              m.G[:, :, h * P:(h + 1) * P], ALU.mult)
            dve.drain()
            dve.sem_inc(out_read, 1)

        dve.wait_ge(zeroed, 2)
        weigh(0)
        for h in range(HH):
            keep(h)
            if h + 1 < HH:
                weigh(h + 1)
            finish(h)
        dve.tensor_scalar(m.osum[:], m.osum[:], 1.0 / P, EPS, ALU.mult, ALU.add)
        dve.drain()
        dve.reciprocal(m.orstd[:], m.osum[:]).then_inc(mean_ready, 1)
        dve.wait_ge(rstd_ready, 1)
        refine(dve, m.osum[:], m.orstd[:], m.scratch[:])
        for c in range(NT):
            part = m.mix[:, c, 0:DA].rearrange("p (h v) -> p h v", v=P)
            rs = m.orstd[:].rearrange("p (h c) -> p h c", c=NT)[:, :, c:c + 1]
            dve.tensor_tensor(part, part, rs.to_broadcast([P, HH, P]), ALU.mult).then_inc(mixed, 1)

    @block.tensor
    def _(pe):
        def sums(h):
            pe.wait_ge(*((k_copied, h) if h else bank_free))
            for c in range(NT):
                i = pe.transpose(PS[:, 4, c * P:(c + 1) * P], m.K[:, c, h * P:(h + 1) * P], m.ident)
            i.then_inc(k_turned, 1)
            for c in range(NT):
                if NT * h + c >= 2:
                    pe.wait_ge(exped, NT * h + c - 1)
                for half in range(2):
                    for x in (uh, ul):
                        i = pe.matmul(PS[:, 2 * (c % 2) + half, :], x[:, c, h * P:(h + 1) * P],
                                      uh[:, 4 + half, :], start=x is uh, stop=x is ul)
                i.then_inc(summed, 1)

        def scores(h):
            pe.wait_ge(weighed, h + 1)
            pe.wait_ge(keys_weighed, h + 1)
            W = m.E[h % 2]
            for unit in range(UNITS):
                if UNITS * h + unit >= 2:
                    pe.wait_ge(kept, UNITS * h + unit - 1)
                b = 5 + unit % 2
                if unit < UNITS - 1:
                    for n in (2 * unit, 2 * unit + 1):
                        if n < LEVELS:
                            for c in range(NT):
                                tile = W[:, n, c * P:(c + 1) * P]
                                a = (n % 2) * 256 + c * 64
                                i = pe.matmul(PS[:, b, a:a + 64], tile, right(tile, n), start=True, stop=True)
                else:
                    for c in range(NT):
                        i = pe.matmul(PS[:, b, c * P:(c + 1) * P], m.Kf[h % 2][:, c * P:(c + 1) * P],
                                      m.Q[:, h, c * P:(c + 1) * P], start=True, stop=True)
                i.then_inc(scored, 1)

        def outputs(h):
            pe.wait_ge(kept, UNITS * (h + 1))
            if h:
                pe.wait_ge(out_read, h)
            cols = slice(h * P, (h + 1) * P)
            for c in range(NT):
                out = PS[:, 7, c * P:(c + 1) * P]
                i = pe.matmul(out, m.AT[h % 2][:, c, :], m.V[:, c, cols], start=True, stop=c == 0)
                if c:
                    i = pe.matmul(out, m.E[h % 2][:, LEVELS, c * P:(c + 1) * P], m.St[:, c - 1, cols], start=False, stop=True)
            i.then_inc(out_done, 1)

        pe.wait_ge(*pooled)
        sums(0)
        sums(1)
        for h in range(HH):
            scores(h)
            outputs(h)
            if h + 2 < HH:
                sums(h + 2)

    return (out_read, HH), (mixed, [c + 1 for c in range(NT)])


class MemoryNorm:

    def __init__(self, sem, PS, m, mh, ml, gain):
        self.PS, self.m, self.mh, self.ml, self.gain = PS, m, mh, ml, gain
        self.arrived, self.squared, self.mean_ready, self.rstd_ready, self.normed, self.turned, self.hi, self.lo = (
            sem(f"memory_{n}") for n in ("arrived", "squared", "mean", "rstd", "normed", "turned", "hi", "lo"))
        self.sums, self.rstd, self.scratch = m.xsum[0][:, 0:MT], m.xmax[0][:, 0:MT], m.xmax[1][:, 0:MT]

    def norm(self, block, mem_in, place_free):
        m = self.m

        @block.sync
        def _(sp):
            sp.wait_ge(*place_free)
            sp.dma_start(m.memory[:], mem_in.rearrange("b (t p) n -> p (b t) n", p=P)).then_inc(self.arrived, 16)

        @block.scalar
        def _(act):
            act.wait_ge(self.arrived, 16)
            for t in range(MT):
                act.activation(m.Pm[t][:].rearrange("p a n -> p (a n)"), m.memory[:, t, :], ACT.Square,
                               accum_out=self.sums[:, t:t + 1]).then_inc(self.squared, 1)
            act.wait_ge(self.mean_ready, 1)
            act.activation(self.rstd, self.rstd, ACT.Sqrt).then_inc(self.rstd_ready, 1)

        @block.vector
        def _(dve):
            dve.wait_ge(self.squared, MT)
            dve.tensor_scalar(self.sums, self.sums, 1.0 / D, EPS, ALU.mult, ALU.add)
            dve.drain()
            dve.reciprocal(self.rstd, self.sums).then_inc(self.mean_ready, 1)
            dve.wait_ge(self.rstd_ready, 1)
            refine(dve, self.sums, self.rstd, self.scratch)
            for t in range(MT):
                dve.tensor_scalar(m.memory[:, t, :], m.memory[:, t, :], self.rstd[:, t:t + 1], None, ALU.mult)\
                   .then_inc(self.normed, 1)

    def bank(self, k, a, b):
        return self.PS[:, 4 + k // 2, (k % 2) * NMEM + a:(k % 2) * NMEM + b]

    def turn(self, pe):
        pe.wait_ge(self.normed, MT)
        for k in range(KD):
            for t in range(MT):
                i = pe.transpose(self.bank(k, t * P, (t + 1) * P), self.m.memory[:, t, k * P:(k + 1) * P], self.m.ident)
        i.then_inc(self.turned, 1)

    def split_hi(self, act):
        act.wait_ge(self.turned, 1)
        for k in range(KD):
            act.activation(self.mh[:, k, :], self.bank(k, 0, NMEM), ACT.Copy, scale=self.gain(k)).then_inc(self.hi, 1)

    def split_lo(self, dve):
        for k in range(KD):
            dve.wait_ge(self.hi, k + 1)
            dve.scalar_tensor_tensor(self.ml[:, k, :], self.bank(k, 0, NMEM), self.gain(k), self.mh[:, k, :],
                                     ALU.mult, ALU.subtract).then_inc(self.lo, 1)


def cross_projection_phase(block, sem, PS, w, g0, u, memory, m, made):
    free = sem("cross_free")
    scale = XD ** -0.5
    um = (memory.mh, memory.ml)

    @block.sync
    def _(sp):
        with sp.Fori(0, 6) as i:
            for j in range(2):
                w.load(sp, g0 + 2 + j, i, 2)

    @block.scalar
    def _(act):
        for b in range(4):
            w.split_hi(act, g0 + b + 1)
            w.wait_used(act, g0 + b)
            j = b % 2
            act.activation(m.qT[:, 2 * b:2 * b + 2, :], PS[:, 2 * j:2 * j + 2, :], ACT.Copy, scale=scale).then_inc(free, 1)
            if b == 1:
                memory.split_hi(act)
        for part in (1, 2):
            with act.Fori(0, 2) as i:
                for j in range(2):
                    g = g0 + 4 * part + j
                    w.split_hi(act, g + 1, i, 2)
                    w.wait_used(act, g, i, 2)
                    if part == 1:
                        out, src = m.kT[:, bass.ds(i * 4 + 2 * j, 2), :], PS[:, 2 * j:2 * j + 2, 0:NMEM]
                    else:
                        out, src = m.Vm[:, :, bass.ds(i * 512 + j * 256, 256)], PS[:, 2 * j:2 * j + 2, 0:256]
                    act.activation(out, src, ACT.Copy).then_inc(free, 1)

    @block.vector
    def _(dve):
        for b in range(4):
            w.split_lo(dve, g0 + b + 1)
            if b == 2:
                memory.split_lo(dve)
        with dve.Fori(2, 6) as i:
            for j in range(2):
                w.split_lo(dve, g0 + 1 + j, i, 2)

    @block.tensor
    def _(pe):
        pe.sem_inc(free, 2)
        for b in range(4):
            w.ready(pe, g0 + b)
            pe.wait_ge(free, b + 1)
            block_to_features(pe, w, g0 + b, u, lambda t: PS[:, 2 * (b % 2) + t, :], made if b == 0 else None)
            if b == 0:
                memory.turn(pe)
        pe.wait_ge(memory.lo, KD)
        for part in (1, 2):
            with pe.Fori(0, 2) as i:
                for j in range(2):
                    g = g0 + 4 * part + j
                    w.ready(pe, g, i, 2)
                    pe.wait_ge(free, plus(i, 2, 4 * part + j + 1))
                    if part == 1:
                        block_to_features(pe, w, g, um, lambda t: PS[:, 2 * j + t, 0:NMEM])
                    else:
                        block_to_tokens(pe, w, g, um, lambda t, h: PS[:, 2 * j + t, 0:256], nt=MT)

    return free, 2 + 12


def cross_attention_phase(block, sem, PS, m, uh, ul, ready):
    scored, max_ready, exped, p_ready, turned, pt_act, pt_dve, out_done, hi_done, lo_done = (
        sem(f"cross_{n}") for n in ("scored", "max", "exped", "p", "turned", "ptact", "ptdve", "out", "hi", "lo"))

    @block.scalar
    def _(act):
        def exps(h):
            act.wait_ge(max_ready, h + 1)
            for t in range(NT):
                act.activation(m.Pm[h % 2][:, t, :], PS[:, 2 * (h % 2) + t // 2, (t % 2) * 256:(t % 2) * 256 + 256], ACT.Exp,
                               bias=m.xmax[h % 2][:, t:t + 1], accum_out=m.xsum[h % 2][:, t:t + 1]).then_inc(exped, 1)

        exps(0)
        exps(1)
        for h in range(XH):
            act.wait_ge(turned, h + 1)
            act.activation(m.PTm[h % 2][:, 0, :], PS[:, 4, :], ACT.Copy).then_inc(pt_act, 1)
            if h + 2 < XH:
                exps(h + 2)
            for f in range(2):
                act.wait_ge(out_done, 2 * h + f + 1)
                act.activation(uh[:, 2 * h + f, :], PS[:, 6 + f, :], ACT.Copy).then_inc(hi_done, 1)

    @block.vector
    def _(dve):
        def maxes(h):
            dve.wait_ge(scored, h + 1)
            dve.tensor_reduce(m.xmax[h % 2][:], PS[:, 2 * (h % 2):2 * (h % 2) + 2, :].rearrange("p a (t n) -> p (a t) n", n=NMEM),
                              AX.X, ALU.max)
            dve.drain()
            dve.tensor_scalar(m.xmax[h % 2][:], m.xmax[h % 2][:], -1.0, None, ALU.mult).then_inc(max_ready, 1)

        def divide(h):
            dve.wait_ge(exped, NT * (h + 1))
            dve.reciprocal(m.xsum[h % 2][:], m.xsum[h % 2][:])
            dve.drain()
            dve.tensor_tensor(m.Pm[h % 2][:], m.Pm[h % 2][:], m.xsum[h % 2][:].unsqueeze(2).to_broadcast([P, NT, NMEM]),
                              ALU.mult).then_inc(p_ready, 1)

        maxes(0)
        divide(0)
        maxes(1)
        for h in range(XH):
            dve.wait_ge(turned, h + 1)
            dve.tensor_copy(m.PTm[h % 2][:, 1, :], PS[:, 5, :]).then_inc(pt_dve, 1)
            if h + 1 < XH:
                divide(h + 1)
            if h + 2 < XH:
                maxes(h + 2)
            for f in range(2):
                dve.wait_ge(hi_done, 2 * h + f + 1)
                dve.tensor_tensor(ul[:, 2 * h + f, :], PS[:, 6 + f, :], uh[:, 2 * h + f, :], ALU.subtract).then_inc(lo_done, 1)

    @block.tensor
    def _(pe):
        def scores(h):
            if h >= 2:
                pe.wait_ge(exped, NT * (h - 1))
            for t in range(NT):
                out = PS[:, 2 * (h % 2) + t // 2, (t % 2) * 256:(t % 2) * 256 + 256]
                for f in range(2):
                    i = pe.matmul(out, m.qT[:, 2 * h + f, t * P:(t + 1) * P], m.kT[:, 2 * h + f, :], start=f == 0, stop=f == 1)
            i.then_inc(scored, 1)

        pe.wait_ge(*ready)
        scores(0)
        scores(1)
        for h in range(XH):
            pe.wait_ge(p_ready, h + 1)
            if h:
                pe.wait_ge(pt_act, h)
                pe.wait_ge(pt_dve, h)
            for t in range(NT):
                for k in range(MT):
                    i = pe.transpose(PS[:, 4 + k, t * P:(t + 1) * P], m.Pm[h % 2][:, t, k * P:(k + 1) * P], m.ident)
            i.then_inc(turned, 1)
            if h + 2 < XH:
                scores(h + 2)
            pe.wait_ge(pt_act, h + 1)
            pe.wait_ge(pt_dve, h + 1)
            for f in range(2):
                if h:
                    pe.wait_ge(lo_done, 2 * h - 1 + f)
                for k in range(MT):
                    a = h * XD + f * P
                    i = pe.matmul(PS[:, 6 + f, :], m.Vm[:, k, a:a + P], m.PTm[h % 2][:, k, :], start=k == 0, stop=k == 1)
                i.then_inc(out_done, 1)

    return lambda pe, k, banks: pe.wait_ge(lo_done, k + 1)


def second_model(nc, PS, X, stream_mem, uh, ul, free, ins, out):
    (w2, consts, mask_in, bands_in, flag_in, mem_in, norm_gains, row_in, pool_w, final_gain) = ins
    mem = Memory(nc)
    mem.top = free
    m, f = Box(), Box()
    start_xn = mem.top
    xn = mem.put("xn2", [P, NT, D])
    m.mix = xn
    after_xn = mem.top
    mem.top = start_xn
    m.lb, m.e = mem.put("lb", [P, 2 * DA]), mem.put("lb_exp", [P, 2 * DA])
    m.esum, m.lnsum = mem.put("lb_sum", [P, DA]), mem.put("lb_lnsum", [P, DA])
    m.ln1m, m.lnlb = mem.put("ln_one_less", [P, DA]), mem.put("ln_lb", [P, DA])
    assert mem.top <= after_xn
    mem.top = after_xn
    table = mem.put("table2", [P, P + (LEVELS + 1) * P + P])
    m.ident = table[:, 0:P]
    m.level = table[:, P:P + (LEVELS + 1) * P]
    m.after = table[:, P + (LEVELS + 1) * P:]
    masks = mem.put("masks", [P, (LEVELS + 2) * 256], U8)
    m.masks = masks[:, :]
    gains = mem.put("norm_gains2", [P, 5 * KD])
    m.flag = mem.put("flag", [P, 2])
    m.sums, m.rstd, m.scratch = mem.put("sums2", [P, NT]), mem.put("rstd2", [P, NT]), mem.put("scratch2", [P, HH * NT])
    m.osum, m.orstd, m.dec = mem.put("osum", [P, HH * NT]), mem.put("orstd", [P, HH * NT]), mem.put("dec", [P, HH * 2])
    m.part_sums = mem.put("part_sums2", [P, 2 * NT])
    m.xmax = [mem.put(f"xmax{i}", [P, NT]) for i in range(2)]
    m.xsum = [mem.put(f"xsum{i}", [P, NT]) for i in range(2)]
    shared = mem.top
    m.LF, m.K, m.V, m.G = (mem.put(n, [P, NT, DA]) for n in ("LF", "K2", "V2", "G2"))
    m.Q = mem.put("Q2", [P, HH, SEQ])
    e_at = mem.top
    m.E = [mem.put(f"E{i}", [P, LEVELS + 1, SEQ]) for i in range(2)]
    after_e = mem.top
    m.Kf = [mem.put(f"Kf{i}", [P, SEQ]) for i in range(2)]
    m.AT = [mem.put(f"AT{i}", [P, NT, P]) for i in range(2)]
    m.St = mem.put("St", [P, NT - 1, DA])
    end = mem.top
    mem.top = after_e
    bands = mem.put("bands", [P, 12 * P])
    m.bands = bands
    m.band = lambda g, kind: bands[:, (g * 3 + kind) * P:(g * 3 + kind + 1) * P]
    m.pool_w = mem.put("pool_w", [P, 4 * P])
    end = max(end, mem.top)
    assert mem.top <= after_e + 10 * 1024
    mem.top = e_at
    m.t1, m.t2, m.U = (mem.put(n, [P, NT, DA]) for n in ("t1", "t2", "U2"))
    m.one_less, m.pscale, m.hnorm = (mem.put(n, [P, DA]) for n in ("one_less", "pscale", "hnorm"))
    assert mem.top <= after_e
    mem.top = e_at
    m.pT, m.Kp = mem.put("pT", [P, 4, SEQ]), mem.put("Kp", [P, NT, DA])
    mem.top = shared
    f.silu, f.h = mem.put("silu", [P, 2, SEQ]), mem.put("h", [P, 2, SEQ])
    f.h_hi, f.h_lo = mem.put("h_hi", [P, 2, SEQ], F32R), mem.put("h_lo", [P, 2, SEQ], F32R)
    mem.top = shared
    mh, ml = mem.put("mem_hi", [P, KD, NMEM], F32R), mem.put("mem_lo", [P, KD, NMEM], F32R)
    m.qT, m.kT = mem.put("qT", [P, KD, SEQ]), mem.put("kT", [P, KD, NMEM])
    m.Vm = mem.put("Vm", [P, MT, D])
    m.Pm = [mem.put(f"Pm{i}", [P, NT, NMEM]) for i in range(2)]
    m.PTm = [mem.put(f"PTm{i}", [P, MT, SEQ]) for i in range(2)]
    m.memory = mem.put("memory", [P, MT, D])
    end = max(end, mem.top)
    assert end <= nc.sbuf_usable_end, (end, nc.sbuf_usable_end)
    mem.top = shared
    final_row = mem.put("final_row", [P, D])
    mask_numbers = mem.put("mask_numbers", [P, (LEVELS + 2) * 256])

    u = (uh, ul)
    with ExitStack() as ctx:
        sem = Semaphores(nc, ctx)
        arrived = sem("tables2_arrived")
        with nc.Block(no_gpsimd_drain=True) as block:
            @block.sync
            def _(sp):
                sp.dma_start(table[:], consts).then_inc(arrived, 16)
                sp.dma_start(mask_numbers[:], mask_in).then_inc(arrived, 16)

            @block.vector
            def _(dve):
                dve.wait_ge(arrived, 32)
                dve.tensor_copy(masks[:], mask_numbers[:])

            @block.scalar
            def _(act):
                for t in range(NT):
                    act.activation(xn[:, t, :], X[:, t, :], ACT.Square, accum_out=m.sums[:, t:t + 1])
        nc.all_engine_barrier(sems_to_clear=sem.span())

    with ExitStack() as ctx:
        sem = Semaphores(nc, ctx)
        with nc.Fori(0, DEPTH) as layer:
            w = WeightStream(sem, *stream_mem, w2, NB2, layer)
            small = sem("small2")
            one = bass.ds(layer, 1)

            def start(kind, eng):
                if kind == "sync":
                    w.load(eng, 0)
                    eng.dma_start(gains[:], norm_gains[one].rearrange("o p n -> p (o n)")).then_inc(small, 16)
                    w.load(eng, 1)
                if kind == "scalar":
                    w.split_hi(eng, 0)
                    eng.wait_ge(small, 16)
                if kind == "vector":
                    w.split_lo(eng, 0)

            def features(block, name, n, norm, **more):
                return to_features_phase(block, sem, name, PS, m.ident, xn, NT, uh, ul, norm=norm,
                                         gain=lambda k: gains[:, n * KD + k:n * KD + k + 1], **more)

            norms = [RowNorm(sem, name, X, xn, m) for name in ("normf1", "normmix", "normxa", "normf2")]
            with nc.Block(no_gpsimd_drain=True) as block:
                made = features(block, "normf1", 0, norms[0], alone=True, extra=start)
                ffn_phase(block, sem, "ffn1", PS, w, 0, u, X, f, m, made, norms[1])
                made = features(block, "normmix", 1, norms[1])
                lf_ready, banks_free = projection_phase_2(block, sem, PS, w, 33, u, m, one, (bands_in, pool_w), row_in,
                                                          flag_in, made)
                pooled, bank_free = pool_and_states_phase(block, sem, PS, m, uh, ul, lf_ready, banks_free)
                out_read, mixed = recurrence_phase(block, sem, PS, m, uh, ul, pooled, bank_free)
                made = to_features_phase(block, sem, "mix2", PS, m.ident, m.mix, NT, uh, ul, src_done=mixed, early=out_read)
                memory = MemoryNorm(sem, PS, m, mh, ml, lambda k: gains[:, 3 * KD + k:3 * KD + k + 1])
                memory.norm(block, mem_in, (mixed[0], NT))
                residual_phase(block, sem, "out2", PS, w, 43, u, X, norms[2], made=made)
                made = features(block, "normxa", 2, norms[2])
                ready = cross_projection_phase(block, sem, PS, w, 47, u, memory, m, made)
                made = cross_attention_phase(block, sem, PS, m, uh, ul, ready)
                residual_phase(block, sem, "xout", PS, w, 59, u, X, norms[3], made=made)
                made = features(block, "normf2", 4, norms[3])
                ffn_phase(block, sem, "ffn2", PS, w, 63, u, X, f, m, made)
            nc.all_engine_barrier(sems_to_clear=sem.span())

    with ExitStack() as ctx:
        sem = Semaphores(nc, ctx)
        arrived, mean_ready, rstd_ready, done, stored = (
            sem(f"final_{n}") for n in ("arrived", "mean", "rstd", "done", "stored"))
        with nc.Block(no_gpsimd_drain=True) as block:
            @block.sync
            def _(sp):
                sp.dma_start(final_row[:], final_gain).then_inc(arrived, 16)
                for t in range(NT):
                    sp.wait_ge(done, t + 1)
                    sp.dma_start(out[0, t * P:(t + 1) * P, :], X[:, t, :]).then_inc(stored, 16)
                sp.wait_ge(stored, 16 * NT)

            @block.scalar
            def _(act):
                act.wait_ge(mean_ready, 1)
                act.activation(m.rstd[:], m.rstd[:], ACT.Sqrt).then_inc(rstd_ready, 1)

            @block.vector
            def _(dve):
                dve.tensor_scalar(m.sums[:], m.sums[:], 1.0 / D, EPS, ALU.mult, ALU.add)
                dve.drain()
                dve.reciprocal(m.rstd[:], m.sums[:]).then_inc(mean_ready, 1)
                dve.wait_ge(rstd_ready, 1)
                refine(dve, m.sums[:], m.rstd[:], m.scratch[:, 0:NT])
                dve.wait_ge(arrived, 16)
                for t in range(NT):
                    dve.scalar_tensor_tensor(X[:, t, :], X[:, t, :], m.rstd[:, t:t + 1], final_row[:], ALU.mult, ALU.mult)\
                       .then_inc(done, 1)


def two_models(nc, x, first_ins, second_ins, out):
    mem = Memory(nc)
    PS = nc.alloc_psum_tensor("PS", [P, 8, 512], F32)
    X = mem.put("X", [P, NT, D])
    uh, ul = mem.put("uh", [P, KD, SEQ], F32R), mem.put("ul", [P, KD, SEQ], F32R)
    stream_mem = ([mem.put(f"w_raw{i}", [P, BLK]) for i in range(2)], [mem.put(f"w_hi{i}", [P, BLK], F32R) for i in range(2)],
                  [mem.put(f"w_lo{i}", [P, BLK], F32R) for i in range(2)])
    first_model(nc, PS, X, x, stream_mem, uh, ul, mem.top, first_ins)
    second_model(nc, PS, X, stream_mem, uh, ul, mem.top, second_ins, out)


def wide_blocks(a):
    n = a.shape[2] // 256
    return a.reshape(DEPTH, KD, P, n, 256).transpose(0, 3, 2, 1, 4).reshape(DEPTH, n, P, BLK)


def deep_blocks(a):
    n = a.shape[1] // 256
    return a.reshape(DEPTH, n, 2, P, D).transpose(0, 1, 3, 2, 4).reshape(DEPTH, n, P, BLK)


def columns(a):
    return a.reshape(DEPTH, KD, P).transpose(0, 2, 1)


def replicated(a):
    return np.repeat(a[:, None, :], P, axis=1)


def kernel(**inputs):
    import concourse.bacc as _bacc
    from concourse.bass_utils import run_bass_kernel_spmd as _run

    a = {n: np.asarray(v) for n, v in inputs.items()}
    w_in = a["w_in"]
    q4 = 4 * 512
    fox, dil = w_in[:, :, 0:q4], w_in[:, :, q4 + NH:]
    w1 = np.concatenate([wide_blocks(fox), wide_blocks(dil), wide_blocks(a["w_out"]), deep_blocks(a["w_ple"]),
                         wide_blocks(a["w_ple_gate"])], 1)
    fa_w = w_in[:, :, q4:q4 + NH].reshape(DEPTH, KD, P, NH).transpose(0, 2, 1, 3).reshape(DEPTH, P, KD * NH)

    def ffn(n):
        up, gate, down = wide_blocks(a[n + "_w1_2"]), wide_blocks(a[n + "_w3_2"]), deep_blocks(a[n + "_w2_2"])
        order = [up[:, 0], gate[:, 0]]
        for c in range(1, NCHUNK):
            order += [up[:, c], down[:, c - 1], gate[:, c]]
        return np.stack(order + [down[:, NCHUNK - 1]], 1)

    qfigu = wide_blocks(a["w_in_2"])
    mixer = np.concatenate([qfigu[:, 2:4], qfigu[:, 4:6], qfigu[:, 8:10], qfigu[:, 0:2], qfigu[:, 6:8]], 1)
    w2 = np.concatenate([ffn("ffn1"), mixer, wide_blocks(a["w_out_2"]), wide_blocks(a["xa_wq_2"]),
                         wide_blocks(a["xa_wkv_2"]), wide_blocks(a["xa_wo_2"]), ffn("ffn2")], 1)
    first_table, second_table, masks, bands, flag = constants()
    arrays = {
        "x": a["x"], "w1": w1, "first_table": first_table, "positions": a["positions"],
        "gains1": np.concatenate([columns(a["norm_g"]), columns(a["ple_norm_g"])], 2),
        "qk_gains": replicated(a["qk_norm_g"].reshape(DEPTH, 4 * HEAD)), "fa_w": fa_w, "fa_b": replicated(a["b_f"]),
        "pT": a["p"][:, 0].transpose(0, 2, 1).reshape(DEPTH, 2, P, SEQ).transpose(0, 2, 1, 3).reshape(DEPTH, P, 2 * SEQ),
        "w2": w2, "second_table": second_table, "masks": masks, "bands": bands, "flag": flag, "mem": a["mem_2"],
        "gains2": np.concatenate([columns(a[n]) for n in ("ffn1_norm_2", "mix_norm_2", "xa_norm_2", "mem_norm_2", "ffn2_norm_2")], 2),
        "hgrn_norm": replicated(a["hgrn_norm_2"]), "pool_scale": replicated(a["pool_scale_2"]),
        "lb_logits": np.concatenate(list(replicated(a["lb_logits_2"])), 1),
        "pool_w": a["pool_w_2"].transpose(0, 2, 1, 3).reshape(DEPTH, P, 4 * P),
        "final": np.repeat(a["final_norm_2"][None, :], P, axis=0),
    }
    nc = _bacc.Bacc("TRN2", target_bir_lowering=False, num_devices=1)
    fed, ap = {}, {}
    for name, v in arrays.items():
        v = np.ascontiguousarray(v)
        fed[f"in_{name}"] = v
        ap[name] = nc.dram_tensor(f"in_{name}", v.shape, mybir.dt.from_np(v.dtype), kind="ExternalInput").ap()
    out = nc.dram_tensor("out_0", (1, SEQ, D), F32, kind="ExternalOutput").ap()
    two_models(nc, ap["x"],
               [ap[n] for n in ("w1", "first_table", "positions", "gains1", "qk_gains", "fa_w", "fa_b", "pT")],
               [ap["w2"], ap["second_table"], ap["masks"], ap["bands"], ap["flag"], ap["mem"], ap["gains2"],
                (ap["hgrn_norm"], ap["pool_scale"], ap["lb_logits"]), ap["pool_w"], ap["final"]], out)
    return _run(nc, [fed], core_ids=[0]).results[0]["out_0"]
```
